# Optimizing a Trainium2 kernel written in Bass

```python
import jax
import jax.numpy as jnp
from jax import lax
import numpy as np

D_MODEL = 2048
BATCH = 1
SEQ = 128
DEPTH = 1
DEC_BATCH = 1
DEC_SEQ = 1024
PAST_LEN = 128

GRID_W = 64
D_MIX = D_MODEL
HEAD_A = 64
D_A = D_MIX // 4
H_A = D_A // HEAD_A
R_W = 64
R_A = 64
R_G = 128
DECAY_SCALE = 0.606531
GN_EPS_A = 64e-5
D_B = 3 * D_MIX // 8
LRU_BLOCK = 64
NB_B = D_B // LRU_BLOCK
LRU_C = 8.0
CONV_W = 4
CONV_LEFT = CONV_W // 2
D_C = D_MIX - D_A - D_B
P_C = 64
H_C = D_C // P_C
G_C = 2
N_C = 128
CHUNK = 128
N_EXPERTS = 16
CAP_FACTOR = 2
D_EXPERT = D_MODEL // 2
ALPHA = (2.0 * DEPTH) ** 0.25
BETA = (8.0 * DEPTH) ** -0.25
LN_EPS = 1e-5
RMS_EPS = 1e-5
RWKV_SIZES = [D_A, D_A, D_A, R_W, R_W, R_A, R_A, R_G]
RWKV_FEAT = sum(RWKV_SIZES)
SSD_CONV_CH = D_C + 2 * G_C * N_C
IN_SIZES = [RWKV_FEAT, D_B, D_B, D_C, SSD_CONV_CH, H_C, H_C]
N_IN = sum(IN_SIZES)
RWKV_SPLITS = [int(v) for v in np.cumsum(RWKV_SIZES)[:-1]]
IN_SPLITS = [int(v) for v in np.cumsum(IN_SIZES)[:-1]]
F32 = jnp.float32

kernel_name = 'hybrid_rwkv7_rglru_ssd_ec_diffusion_step'

def layer_norm(x, g, b):
    xf = x.astype(F32)
    mu = jnp.mean(xf, axis=-1, keepdims=True)
    var = jnp.mean(jnp.square(xf - mu), axis=-1, keepdims=True)
    return ((xf - mu) * lax.rsqrt(var + LN_EPS) * g + b).astype(x.dtype)

def grid_pos_embed(n_tokens, dtype):
    rows = n_tokens // GRID_W
    quarter = D_MODEL // 4
    omega = 1.0 / (10000.0 ** (jnp.arange(quarter, dtype=F32) / quarter))
    r_idx = jnp.broadcast_to(jnp.arange(rows, dtype=F32)[:, None], (rows, GRID_W)).reshape(-1)
    c_idx = jnp.broadcast_to(jnp.arange(GRID_W, dtype=F32)[None, :], (rows, GRID_W)).reshape(-1)
    ang_r = r_idx[:, None] * omega[None]
    ang_c = c_idx[:, None] * omega[None]
    pe = jnp.concatenate([jnp.sin(ang_r), jnp.cos(ang_r), jnp.sin(ang_c), jnp.cos(ang_c)], axis=-1)
    return pe.astype(dtype)

def centred_shift_mix(u, mu):
    up = jnp.pad(u, ((0, 0), (1, 1), (0, 0)))
    nb = 0.5 * (up[:, :-2] + up[:, 2:])
    return u + mu * (nb - u)

def depthwise_conv_centred(u, w, b):
    t = u.shape[1]
    up = jnp.pad(u, ((0, 0), (CONV_LEFT, CONV_W - 1 - CONV_LEFT), (0, 0)))
    return b + sum(w[j] * up[:, j:j + t] for j in range(CONV_W))

def wkv7_scan(r, w, k, v, kk, a, s0, reverse):
    def step(s, inp):
        r_t, w_t, k_t, v_t, kk_t, a_t = inp
        sa = jnp.einsum('bhvk,bhk->bhv', s, -kk_t)
        s = s * w_t[:, :, None, :] + sa[..., None] * (kk_t * a_t)[:, :, None, :] + v_t[..., None] * k_t[:, :, None, :]
        return s, jnp.einsum('bhvk,bhk->bhv', s, r_t)
    xs = tuple(jnp.moveaxis(t, 1, 0) for t in (r, w, k, v, kk, a))
    s_fin, y = lax.scan(step, s0, xs, reverse=reverse)
    return jnp.moveaxis(y, 0, 1), s_fin

def rwkv7_mixer(feats, s0, mu, w0, w_up, a0, a_up, g_up, k_k, k_a, r_k, gn_g, gn_b):
    f = centred_shift_mix(feats.astype(F32), mu)
    r, k, v, wd_f, wd_b, ad_f, ad_b, gd = jnp.split(f, RWKV_SPLITS, axis=-1)
    bsz, t, _ = r.shape
    heads = lambda z: z.reshape(bsz, t, H_A, HEAD_A)
    g = jax.nn.sigmoid(gd) @ g_up
    kk = heads(k * k_k)
    kk = kk / jnp.maximum(jnp.sqrt(jnp.sum(kk * kk, axis=-1, keepdims=True)), 1e-12)
    rh, vh = heads(r), heads(v)
    s0 = s0.astype(F32)
    y_sum = 0.0
    bonus = 0.0
    finals = []
    for d, (wd, ad) in enumerate(((wd_f, ad_f), (wd_b, ad_b))):
        w = jnp.exp(-DECAY_SCALE * jax.nn.sigmoid(w0[d] + jnp.tanh(wd) @ w_up[d]))
        a = jax.nn.sigmoid(a0[d] + ad @ a_up[d])
        kd = heads(k * (1.0 + (a - 1.0) * k_a))
        y, s_fin = wkv7_scan(rh, heads(w), kd, vh, kk, heads(a), s0[:, d], reverse=(d == 1))
        y_sum = y_sum + y
        bonus = bonus + jnp.sum(rh * kd * r_k, axis=-1, keepdims=True)
        finals.append(s_fin)
    m = jnp.mean(y_sum, axis=-1, keepdims=True)
    var = jnp.mean(jnp.square(y_sum - m), axis=-1, keepdims=True)
    yn = ((y_sum - m) * lax.rsqrt(var + GN_EPS_A)).reshape(bsz, t, D_A) * gn_g + gn_b
    out = (yn + (bonus * vh).reshape(bsz, t, D_A)) * g
    return out, jnp.stack(finals, axis=1)

def linear_recurrence(a, u, h0, reverse):
    def combine(left, right):
        a1, b1 = left
        a2, b2 = right
        return a1 * a2, a2 * b1 + b2
    a_cum, h = lax.associative_scan(combine, (a, u), reverse=reverse, axis=1)
    h = h + a_cum * h0[:, None]
    h_fin = h[:, 0] if reverse else h[:, -1]
    return h, h_fin

def rglru_mixer(xb, gb, h0, conv_w, conv_b, w_a, b_a, w_x, b_x, lam):
    xc = depthwise_conv_centred(xb.astype(F32), conv_w, conv_b)
    bsz, t, _ = xc.shape
    xh = xc.reshape(bsz, t, NB_B, LRU_BLOCK)
    h0 = h0.astype(F32)
    h_sum = 0.0
    finals = []
    for d in range(2):
        rg = jax.nn.sigmoid(jnp.einsum('btni,nij->btnj', xh, w_a[d]).reshape(bsz, t, D_B) + b_a[d])
        ig = jax.nn.sigmoid(jnp.einsum('btni,nij->btnj', xh, w_x[d]).reshape(bsz, t, D_B) + b_x[d])
        log_a = -LRU_C * rg * jax.nn.softplus(-lam[d])
        u = jnp.sqrt(-jnp.expm1(2.0 * log_a)) * (ig * xc)
        h, h_fin = linear_recurrence(jnp.exp(log_a), u, h0[:, d], reverse=(d == 1))
        h_sum = h_sum + h
        finals.append(h_fin)
    return h_sum * jax.nn.gelu(gb.astype(F32)), jnp.stack(finals, axis=1)

def ssd_chunked(x, dt, a, bh, ch, s0):
    bsz, t, h, p = x.shape
    nc = t // CHUNK
    xd = (x * dt[..., None]).reshape(bsz, nc, CHUNK, h, p)
    acs = jnp.cumsum(jnp.transpose((a * dt).reshape(bsz, nc, CHUNK, h), (0, 3, 1, 2)), axis=-1)
    bc = bh.reshape(bsz, nc, CHUNK, h, -1)
    cc = ch.reshape(bsz, nc, CHUNK, h, -1)
    causal = jnp.tril(jnp.ones((CHUNK, CHUNK), dtype=bool))
    lmat = jnp.exp(jnp.where(causal, acs[..., :, None] - acs[..., None, :], -jnp.inf))
    cb = jnp.einsum('bclhn,bcshn->bhcls', cc, bc)
    y_diag = jnp.einsum('bhcls,bcshp->bclhp', cb * lmat, xd)
    decay_states = jnp.exp(acs[..., -1:] - acs)
    chunk_states = jnp.einsum('bclhn,bhcl,bclhp->bchpn', bc, decay_states, xd)
    chunk_decay = jnp.exp(acs[..., -1])
    def step(s, inp):
        st, dec = inp
        return dec[..., None, None] * s + st, s
    s_fin, s_prev = lax.scan(step, s0, (jnp.moveaxis(chunk_states, 1, 0), jnp.moveaxis(chunk_decay, 2, 0)))
    s_prev = jnp.moveaxis(s_prev, 0, 1)
    y_off = jnp.einsum('bclhn,bchpn,bhcl->bclhp', cc, s_prev, jnp.exp(acs))
    return (y_diag + y_off).reshape(bsz, t, h, p), s_fin

def ssd_mixer(z, xbc, dt_f, dt_b, s0, conv_w, conv_b, dt_bias, a_log, d_skip, norm_g):
    xbc = jax.nn.silu(depthwise_conv_centred(xbc.astype(F32), conv_w, conv_b))
    xs, bm, cm = jnp.split(xbc, [D_C, D_C + G_C * N_C], axis=-1)
    bsz, t, _ = xs.shape
    xh = xs.reshape(bsz, t, H_C, P_C)
    bh = jnp.repeat(bm.reshape(bsz, t, G_C, N_C), H_C // G_C, axis=2)
    chh = jnp.repeat(cm.reshape(bsz, t, G_C, N_C), H_C // G_C, axis=2)
    s0 = s0.astype(F32)
    flip = lambda u: jnp.flip(u, axis=1)
    ident = lambda u: u
    y = d_skip[:, None] * xh
    finals = []
    for d, dt_raw in enumerate((dt_f, dt_b)):
        orient = ident if d == 0 else flip
        dt = jax.nn.softplus(dt_raw.astype(F32) + dt_bias[d])
        a = -jnp.exp(a_log[d].astype(F32))
        yd, s_fin = ssd_chunked(orient(xh), orient(dt), a, orient(bh), orient(chh), s0[:, d])
        y = y + orient(yd)
        finals.append(s_fin)
    yg = y.reshape(bsz, t, D_C) * jax.nn.silu(z.astype(F32))
    yn = yg * lax.rsqrt(jnp.mean(yg * yg, axis=-1, keepdims=True) + RMS_EPS) * norm_g
    return yn, jnp.stack(finals, axis=1)

def ec_moe(h, router_w, w_gate, w_up, w_down):
    bsz, t, d = h.shape
    cap = CAP_FACTOR * t // N_EXPERTS
    aff = jax.nn.softmax((h @ router_w).astype(F32), axis=-1)
    gates, idx = lax.top_k(jnp.swapaxes(aff, 1, 2), cap)
    xs = jax.vmap(lambda hb, ib: hb[ib])(h, idx)
    act = jax.nn.silu(jnp.einsum('becd,edf->becf', xs, w_gate)) * jnp.einsum('becd,edf->becf', xs, w_up)
    ye = jnp.einsum('becf,efd->becd', act, w_down) * gates[..., None].astype(h.dtype)
    return jax.vmap(lambda yb, ib: jnp.zeros((t, d), yb.dtype).at[ib.reshape(-1)].add(yb.reshape(-1, d)))(ye, idx)

def setup_inputs(seed: int = 0) -> dict:
    key = jax.random.key(seed)
    ks = iter(jax.random.split(key, 64))
    nrm = lambda shape, scale: scale * jax.random.normal(next(ks), shape, F32)
    unif = lambda shape, lo, hi: jax.random.uniform(next(ks), shape, F32, lo, hi)
    L = DEPTH
    a_pow = unif((L, 2, D_B), 0.9, 0.999)
    a_base = a_pow ** (1.0 / LRU_C)
    dt0 = jnp.exp(unif((L, 2, H_C), float(np.log(1e-3)), float(np.log(1e-1))))
    return {
        'x_prompt': nrm((BATCH, SEQ, D_MODEL), 1.0),
        'x_sample': nrm((DEC_BATCH, DEC_SEQ, D_MODEL), 1.0),
        'c': nrm((DEC_BATCH, D_MODEL), 1.0),
        'c_ctx': nrm((D_MODEL,), 1.0),
        'state_rwkv': nrm((DEC_BATCH, L, 2, H_A, HEAD_A, HEAD_A), 0.1),
        'state_rglru': nrm((DEC_BATCH, L, 2, D_B), 1.0),
        'state_ssd': nrm((DEC_BATCH, L, 2, H_C, P_C, N_C), 0.1),
        'w_mod': nrm((L, D_MODEL, 6 * D_MODEL), 0.5 * D_MODEL ** -0.5),
        'b_mod': nrm((L, 6 * D_MODEL), 0.02),
        'w_in': nrm((L, D_MODEL, N_IN), D_MODEL ** -0.5),
        'w_out': nrm((L, D_MIX, D_MODEL), BETA * D_MIX ** -0.5),
        'rwkv_mu': unif((L, RWKV_FEAT), 0.0, 1.0),
        'rwkv_w0': nrm((L, 2, D_A), 1.0),
        'rwkv_w_up': nrm((L, 2, R_W, D_A), R_W ** -0.5),
        'rwkv_a0': nrm((L, 2, D_A), 0.5),
        'rwkv_a_up': nrm((L, 2, R_A, D_A), R_A ** -0.5),
        'rwkv_g_up': nrm((L, R_G, D_A), R_G ** -0.5),
        'rwkv_k_k': 0.85 + nrm((L, D_A), 0.05),
        'rwkv_k_a': 1.0 + nrm((L, D_A), 0.05),
        'rwkv_r_k': nrm((L, H_A, HEAD_A), 0.1),
        'rwkv_gn_g': 1.0 + nrm((L, D_A), 0.05),
        'rwkv_gn_b': nrm((L, D_A), 0.02),
        'lru_conv_w': nrm((L, CONV_W, D_B), CONV_W ** -0.5),
        'lru_conv_b': nrm((L, D_B), 0.02),
        'lru_w_a': nrm((L, 2, NB_B, LRU_BLOCK, LRU_BLOCK), LRU_BLOCK ** -0.5),
        'lru_b_a': nrm((L, 2, D_B), 0.02),
        'lru_w_x': nrm((L, 2, NB_B, LRU_BLOCK, LRU_BLOCK), LRU_BLOCK ** -0.5),
        'lru_b_x': nrm((L, 2, D_B), 0.02),
        'lru_lambda': jnp.log(a_base) - jnp.log1p(-a_base),
        'ssd_conv_w': nrm((L, CONV_W, SSD_CONV_CH), CONV_W ** -0.5),
        'ssd_conv_b': nrm((L, SSD_CONV_CH), 0.02),
        'ssd_dt_bias': dt0 + jnp.log(-jnp.expm1(-dt0)),
        'ssd_a_log': jnp.log(unif((L, 2, H_C), 1.0, 16.0)),
        'ssd_d': 1.0 + nrm((L, H_C), 0.05),
        'ssd_norm_g': 1.0 + nrm((L, D_C), 0.05),
        'ln1_g': 1.0 + nrm((L, D_MODEL), 0.05),
        'ln1_b': nrm((L, D_MODEL), 0.02),
        'ln2_g': 1.0 + nrm((L, D_MODEL), 0.05),
        'ln2_b': nrm((L, D_MODEL), 0.02),
        'router_w': nrm((L, D_MODEL, N_EXPERTS), D_MODEL ** -0.5),
        'exp_w_gate': nrm((L, N_EXPERTS, D_MODEL, D_EXPERT), D_MODEL ** -0.5),
        'exp_w_up': nrm((L, N_EXPERTS, D_MODEL, D_EXPERT), D_MODEL ** -0.5),
        'exp_w_down': nrm((L, N_EXPERTS, D_EXPERT, D_MODEL), BETA * D_EXPERT ** -0.5),
    }

def reference(x_prompt, x_sample, c, c_ctx, state_rwkv, state_rglru, state_ssd,
              w_mod, b_mod, w_in, w_out,
              rwkv_mu, rwkv_w0, rwkv_w_up, rwkv_a0, rwkv_a_up, rwkv_g_up, rwkv_k_k, rwkv_k_a, rwkv_r_k,
              rwkv_gn_g, rwkv_gn_b,
              lru_conv_w, lru_conv_b, lru_w_a, lru_b_a, lru_w_x, lru_b_x, lru_lambda,
              ssd_conv_w, ssd_conv_b, ssd_dt_bias, ssd_a_log, ssd_d, ssd_norm_g,
              ln1_g, ln1_b, ln2_g, ln2_b,
              router_w, exp_w_gate, exp_w_up, exp_w_down):

    def layer(l, x, cond, s_rwkv, s_lru, s_ssd):
        mod = jax.nn.silu(cond) @ w_mod[l] + b_mod[l]
        sh1, sc1, gt1, sh2, sc2, gt2 = jnp.split(mod[:, None, :], 6, axis=-1)
        h = x * (1 + sc1) + sh1
        f_a, xb, gb, z, xbc, dt_f, dt_b = jnp.split(h @ w_in[l], IN_SPLITS, axis=-1)
        y_a, n_a = rwkv7_mixer(f_a, s_rwkv, rwkv_mu[l], rwkv_w0[l], rwkv_w_up[l], rwkv_a0[l], rwkv_a_up[l],
                               rwkv_g_up[l], rwkv_k_k[l], rwkv_k_a[l], rwkv_r_k[l], rwkv_gn_g[l], rwkv_gn_b[l])
        y_b, n_b = rglru_mixer(xb, gb, s_lru, lru_conv_w[l], lru_conv_b[l], lru_w_a[l], lru_b_a[l],
                               lru_w_x[l], lru_b_x[l], lru_lambda[l])
        y_c, n_c = ssd_mixer(z, xbc, dt_f, dt_b, s_ssd, ssd_conv_w[l], ssd_conv_b[l], ssd_dt_bias[l],
                             ssd_a_log[l], ssd_d[l], ssd_norm_g[l])
        o = jnp.concatenate([y_a, y_b, y_c], axis=-1).astype(x.dtype) @ w_out[l]
        x = layer_norm(ALPHA * x + gt1 * o, ln1_g[l], ln1_b[l])
        h = x * (1 + sc2) + sh2
        m = ec_moe(h, router_w[l], exp_w_gate[l], exp_w_up[l], exp_w_down[l])
        x = layer_norm(ALPHA * x + gt2 * m, ln2_g[l], ln2_b[l])
        return x, n_a, n_b, n_c

    nb = x_prompt.shape[0]
    y_prompt = x_prompt
    new_a, new_b, new_c = [], [], []
    for l in range(DEPTH):
        z_a = jnp.zeros((nb, 2, H_A, HEAD_A, HEAD_A), F32)
        z_b = jnp.zeros((nb, 2, D_B), F32)
        z_c = jnp.zeros((nb, 2, H_C, P_C, N_C), F32)
        y_prompt, s_a, s_b, s_c = layer(l, y_prompt, c_ctx[None, :], z_a, z_b, z_c)
        new_a.append(s_a)
        new_b.append(s_b)
        new_c.append(s_c)
    new_state_rwkv = jnp.stack(new_a, axis=1).astype(x_prompt.dtype)
    new_state_rglru = jnp.stack(new_b, axis=1).astype(x_prompt.dtype)
    new_state_ssd = jnp.stack(new_c, axis=1).astype(x_prompt.dtype)

    y_sample = x_sample + grid_pos_embed(x_sample.shape[1], x_sample.dtype)[None]
    for l in range(DEPTH):
        y_sample, _, _, _ = layer(l, y_sample, c, state_rwkv[:, l], state_rglru[:, l], state_ssd[:, l])

    return (y_prompt, y_sample, new_state_rwkv, new_state_rglru, new_state_ssd)


_drawn_inputs = setup_inputs


def setup_inputs(seed=0):
    import zlib

    import numpy as np

    out = dict(_drawn_inputs(seed))
    spreads = {}
    factors = {'state_rwkv': 50.136,
     'state_rglru': 2.911,
     'state_ssd': 8.0,
     'rwkv_gn_g': 35.291,
     'rwkv_gn_b': 64.0,
     'lru_b_a': 8.0,
     'lru_b_x': 7.699,
     'ssd_d': 27.676,
     'ssd_norm_g': 21.594,
     'ln1_b': 2.833,
     'ln2_b': 2.849,
     'rwkv_r_k': 2.772}
    for name, (base, spread) in spreads.items():
        noise = np.random.default_rng([zlib.crc32(name.encode()), seed]).standard_normal(out[name].shape)
        drawn = base * np.exp(spread * noise) if base else spread * noise
        out[name] = jnp.asarray(drawn.astype(out[name].dtype))
    for name, factor in factors.items():
        out[name] = (out[name] * factor).astype(out[name].dtype)
    return out
```

```python
from contextlib import ExitStack

import numpy as np

import concourse.bass as bass
from concourse import mybir

F32 = mybir.dt.float32
I32 = mybir.dt.int32
U32 = mybir.dt.uint32
ALU = mybir.AluOpType
ACT = mybir.ActivationFunctionType
AX = mybir.AxisListType

P = 128
D = 2048
KT = D // P
TC, TS = 128, 1024
T = TC + TS
NT = T // P
SEG = 384
NSEG = T // SEG
HD = 64
D_A, D_B, D_C = 512, 768, 768
A_FEAT = 3 * D_A + 4 * 64 + 128
SSD_CH = D_C + 512
N_IN = A_FEAT + 2 * D_B + D_C + SSD_CH + 24
FT = -(-N_IN // P)
F_R, F_K, F_V, F_WD, F_AD, F_GD = 0, 4, 8, 12, 13, 14
F_XB = A_FEAT // P
F_GB = F_XB + D_B // P
F_Z = F_GB + D_B // P
F_XBC = F_Z + D_C // P
F_DT = F_XBC + SSD_CH // P
DECAY = 0.606531
ALPHA = 2.0 ** 0.25
LN_EPS = 1e-5
GN_EPS = 64e-5
E = 16
FE = 1024
CAP_S, CAP_C = 2 * TS // E, 2 * TC // E
CAP = CAP_S + CAP_C
PAD_C, PAD_S = 2, 2 + TC + 1 + 2
TP = PAD_S + TS + 1


class Scope:

    def __init__(self, nc, stack, name):
        self.nc, self.stack, self.name, self.sems = nc, stack, name, []
        stack.callback(self.clear)

    def sb(self, name, shape, dt=F32):
        return self.stack.enter_context(self.nc.sbuf_tensor(f"{self.name}_{name}", shape, dt))

    def ps(self, name, shape=(P, 512)):
        return self.stack.enter_context(self.nc.psum_tensor(f"{self.name}_{name}", list(shape), F32))

    def sem(self, name):
        self.sems.append(self.nc.alloc_semaphore(f"{self.name}_{name}"))
        return self.sems[-1]

    def clear(self):
        if self.sems:
            self.nc.clear_and_free_semaphores(self.sems)
            self.nc.all_engine_barrier()


class Chain:

    def __init__(self, eng, sem, per=0):
        self.eng, self.sem, self.n, self.per, self.base = eng, sem, 0, per, 0

    def turn(self, i, start=0):
        self.n, self.base = 0, start + i * self.per

    def __call__(self, ins):
        self.n += 1
        ins.then_inc(self.sem, 1)
        self.eng.wait_ge(self.sem, self.base + self.n)

    def end(self):
        assert self.n == self.per, (self.n, self.per)


def modulation(nc, d):
    RING, CW = 3, 512
    n_col = 6 * D // CW
    w = d["w_mod"].rearrange("(t p) n -> p t n", p=P)
    with ExitStack() as stack:
        s = Scope(nc, stack, "mod")
        cond = s.sb("cond", [P, KT, 2])
        sil = s.sb("silu", [P, KT, 2])
        slab = s.sb("slab", [P, RING, KT, CW])
        bias = s.sb("bias", [2, 6 * D])
        row = s.sb("row", [2, RING, CW])
        acc = [s.ps(f"acc{i}") for i in range(RING)]
        cond_in, silu_done, bias_in = s.sem("cond_in"), s.sem("silu_done"), s.sem("bias_in")
        slab_in = [s.sem(f"slab_in{i}") for i in range(RING)]
        row_out = [s.sem(f"row_out{i}") for i in range(RING)]
        product, biased = s.sem("product"), s.sem("biased")
        block = stack.enter_context(nc.Block())

        @block.sync
        def _(sp):
            sp.dma_start(cond[:], d["cond"]).then_inc(cond_in, 16)
            sp.dma_start(bias[:], d["b_mod"]).then_inc(bias_in, 16)
            for r in range(RING):
                sp.dma_start(slab[:, r], w[:, :, r * CW:(r + 1) * CW]).then_inc(slab_in[r], 16)
            with sp.Fori(1, n_col // RING) as i:
                for r in range(RING):
                    sp.wait_ge(product, RING * (i - 1) + r + 1)
                    sp.dma_start(slab[:, r], w[:, :, bass.ds((RING * i + r) * CW, CW)]).then_inc(slab_in[r], 16)

        @block.scalar
        def _(act):
            act.wait_ge(cond_in, 16)
            act.activation(sil[:], cond[:], ACT.Silu).then_inc(silu_done, 1)
            with act.Fori(0, n_col // RING) as i:
                for r in range(RING):
                    act.wait_ge(biased, RING * i + r + 1)
                    act.dma_start(d["MOD"][:, bass.ds((RING * i + r) * CW, CW)], row[:, r]).then_inc(row_out[r], 16)
            for r in range(RING):
                act.wait_ge(row_out[r], 16 * (n_col // RING))

        @block.tensor
        def _(pe):
            pe.wait_ge(silu_done, 1)

            def column(i, r):
                pe.wait_ge(slab_in[r], 16 * (i + 1))
                for t in range(KT):
                    last = pe.matmul(acc[r][0:2, :], sil[:, t, :], slab[:, r, t, :], start=t == 0, stop=t == KT - 1)
                last.then_inc(product, 1)
            for r in range(RING):
                column(0, r)
            with pe.Fori(1, n_col // RING) as i:
                for r in range(RING):
                    pe.wait_ge(biased, RING * (i - 1) + r + 1)
                    column(i, r)

        @block.vector
        def _(dve):
            dve.wait_ge(bias_in, 16)

            def column(i, r):
                dve.wait_ge(product, RING * i + r + 1)
                dve.tensor_tensor(row[:, r], acc[r][0:2, :], bias[:, bass.ds((RING * i + r) * CW, CW)],
                                  ALU.add).then_inc(biased, 1)
            for r in range(RING):
                column(0, r)
            with dve.Fori(1, n_col // RING) as i:
                for r in range(RING):
                    dve.wait_ge(row_out[r], 16 * i)
                    column(i, r)


def projection(nc, d):
    CW, WR = 512, 2
    PER = WR * CW // P
    full = N_IN // CW
    rest = N_IN - full * CW
    w = d["w_in"].rearrange("(t p) n -> p t n", p=P)
    with ExitStack() as stack:
        s = Scope(nc, stack, "proj")
        ident = s.sb("ident", [P, P])
        shift = s.sb("shift", [P, 2, KT])
        scale = s.sb("scale", [P, 2, KT])
        hT = s.sb("hT", [P, KT, T])
        slab = s.sb("slab", [P, WR, KT, CW])
        mod_in, pos_in, x_sum = (s.sem(n) for n in ("mod_in", "pos_in", "x_sum"))
        x_out = [s.sem(f"x_out{i}") for i in range(2)]
        x_in = [s.sem(f"x_in{i}") for i in range(2)]
        ident_in, turned = s.sem("ident_in"), s.sem("turned")
        mod_turned, mod_done = s.sem("mod_turned"), s.sem("mod_done")
        h_act, h_dve = s.sem("h_act"), s.sem("h_dve")
        slab_in = [s.sem(f"slab_in{i}") for i in range(WR)]
        tile_done, copied = s.sem("tile_done"), s.sem("copied")
        out_done = [s.sem(f"out_done{i}") for i in range(2)]

        def slab_load(eng, i, r, cols):
            eng.dma_start(slab[:, r, :, 0:cols], w[:, :, bass.ds((WR * i + r) * CW, cols)]).then_inc(slab_in[r], 16)

        with ExitStack() as inner:
            s1 = Scope(nc, inner, "hid")
            x = s1.sb("x", [P, 2, D])
            pos = s1.sb("pos", [P, D])
            rows = s1.sb("rows", [4 * KT, P])
            bank = [s1.ps(f"bank{i}") for i in range(8)]
            block = inner.enter_context(nc.Block())

            @block.sync
            def _(sp):
                sp.dma_start(ident[:], d["ident"]).then_inc(ident_in, 16)
                for c in range(2):
                    sp.dma_start(rows[2 * KT * c:2 * KT * (c + 1), :],
                                 d["MOD"][c, 0:2 * D].rearrange("(t p) -> t p", p=P)).then_inc(mod_in, 16)
                for t in range(NT):
                    if t >= 2:
                        sp.wait_ge(turned, 4 * (t - 1))
                        sp.wait_ge(x_out[t % 2], 16 * (t // 2))
                    sp.dma_start(x[:, t % 2], d["x"][t * P:(t + 1) * P, :]).then_inc(x_in[t % 2], 16)
                    if t:
                        if t > 1:
                            sp.wait_ge(x_sum, t - 1)
                        sp.dma_start(pos[:], d["pos"][(t - 1) * P:t * P, :]).then_inc(pos_in, 16)
                for r in range(WR):
                    slab_load(sp, 0, r, CW)

            @block.gpsimd
            def _(pool):
                for t in range(NT):
                    pool.wait_ge(x_in[t % 2], 16 * (t // 2 + 1))
                    if t:
                        pool.wait_ge(x_sum, t)
                    pool.dma_start(d["X0"][t * P:(t + 1) * P, :], x[:, t % 2]).then_inc(x_out[t % 2], 16)
                for b in range(2):
                    pool.wait_ge(x_out[b], 16 * ((NT + 1 - b) // 2))

            @block.tensor
            def _(pe):
                pe.wait_ge(ident_in, 16)
                pe.wait_ge(mod_in, 32)
                pe.transpose(bank[7][:, 0:4 * KT], rows[:], ident[0:4 * KT, 0:4 * KT]).then_inc(mod_turned, 1)
                pe.wait_ge(mod_done, 2)
                for t in range(NT):
                    pe.wait_ge(x_in[t % 2], 16 * (t // 2 + 1))
                    if t:
                        pe.wait_ge(x_sum, t)
                    for q in range(4):
                        n = 4 * t + q
                        if n >= 8:
                            pe.wait_ge(h_act if n % 2 == 0 else h_dve, (n - 8) // 2 + 1)
                        for b in range(4):
                            k = 4 * q + b
                            last = pe.transpose(bank[n % 8][:, b * P:(b + 1) * P], x[:, t % 2, k * P:(k + 1) * P],
                                                ident[:])
                        last.then_inc(turned, 1)

            @block.scalar
            def _(act):
                act.wait_ge(mod_done, 2)
                for n in range(0, 4 * NT, 2):
                    t, q = n // 4, n % 4
                    c = min(t, 1)
                    act.wait_ge(turned, n + 1)
                    for b in range(4):
                        k = 4 * q + b
                        last = act.activation(hT[:, k, t * P:(t + 1) * P], bank[n % 8][:, b * P:(b + 1) * P],
                                              ACT.Identity, bias=shift[:, c, k:k + 1], scale=scale[:, c, k:k + 1])
                    last.then_inc(h_act, 1)

            @block.vector
            def _(dve):
                dve.wait_ge(mod_turned, 1)
                both = bank[7][:, 0:4 * KT].rearrange("p (c s t) -> p c s t", c=2, s=2)
                dve.tensor_copy(shift[:], both[:, :, 0, :]).then_inc(mod_done, 1)
                dve.tensor_scalar(scale[:], both[:, :, 1, :], 1.0, None, ALU.add).then_inc(mod_done, 1)
                dve.wait_ge(mod_done, 2)

                def embed(t):
                    dve.wait_ge(x_in[t % 2], 16 * (t // 2 + 1))
                    dve.wait_ge(pos_in, 16 * t)
                    dve.tensor_tensor(x[:, t % 2], x[:, t % 2], pos[:], ALU.add).then_inc(x_sum, 1)
                for n in range(1, 4 * NT, 2):
                    t, q = n // 4, n % 4
                    c = min(t, 1)
                    if q == 1 and t + 1 < NT:
                        embed(t + 1)
                    dve.wait_ge(turned, n + 1)
                    for b in range(4):
                        k = 4 * q + b
                        last = dve.tensor_scalar(hT[:, k, t * P:(t + 1) * P], bank[n % 8][:, b * P:(b + 1) * P],
                                                 scale[:, c, k:k + 1], shift[:, c, k:k + 1], ALU.mult, ALU.add)
                    last.then_inc(h_dve, 1)

        with ExitStack() as inner:
            s2 = Scope(nc, inner, "feat")
            out = s2.sb("out", [P, 2, T])
            acc = [s2.ps(f"acc{i}", [P, NSEG, 512]) for i in range(2)]
            passes, tail = full // WR, -(-rest // P)
            block = inner.enter_context(nc.Block())

            @block.sync
            def _(sp):
                with sp.Fori(1, passes) as i:
                    for r in range(WR):
                        sp.wait_ge(tile_done, PER * (i - 1) + 4 * (r + 1))
                        slab_load(sp, i, r, CW)
                sp.wait_ge(tile_done, PER * (passes - 1) + 4)
                slab_load(sp, passes, 0, rest)

            @block.tensor
            def _(pe):
                def tile(n, k, m, reused):
                    if reused:
                        pe.wait_ge(copied, n - 1)
                    for g in range(NSEG):
                        for t in range(KT):
                            last = pe.matmul(acc[k % 2][0:m, g, 0:SEG], slab[:, k // 4, t, k % 4 * P:k % 4 * P + m],
                                             hT[:, t, g * SEG:(g + 1) * SEG], start=t == 0, stop=t == KT - 1)
                    last.then_inc(tile_done, 1)

                def one_pass(i, first):
                    for k in range(PER):
                        if k % 4 == 0:
                            pe.wait_ge(slab_in[k // 4], 16 * (i + 1))
                        tile(PER * i + k, k, P, not first or k >= 2)
                one_pass(0, True)
                with pe.Fori(1, passes) as i:
                    one_pass(i, False)
                pe.wait_ge(slab_in[0], 16 * (passes + 1))
                for k in range(tail):
                    tile(PER * passes + k, k, min(P, rest - k * P), True)

            @block.scalar
            def _(act):
                def tile(n, k, m, reused):
                    act.wait_ge(tile_done, n + 1)
                    if reused is not None:
                        act.wait_ge(out_done[k % 2], 16 * reused)
                    act.activation(out[0:m, k % 2].rearrange("p (g c) -> p g c", g=NSEG), acc[k % 2][0:m, :, 0:SEG],
                                   ACT.Copy).then_inc(copied, 1)
                    act.wait_ge(copied, n + 1)
                    act.dma_start(d["FEAT"][bass.ds(n * P, m), :], out[0:m, k % 2]).then_inc(out_done[k % 2], 16)
                for k in range(PER):
                    tile(k, k, P, k // 2 if k >= 2 else None)
                with act.Fori(1, passes) as i:
                    for k in range(PER):
                        tile(PER * i + k, k, P, PER // 2 * i + k // 2)
                for k in range(tail):
                    tile(PER * passes + k, k, min(P, rest - k * P), PER // 2 * passes + k // 2)
                for b in range(2):
                    act.wait_ge(out_done[b], 16 * (FT // 2))


class Steps:

    def __init__(self, sem, names):
        self.sem, self.names, self.k = sem, names.split(), 0

    def at(self, name, i=0):
        return i * len(self.names) + self.names.index(name) + 1

    def done(self, ins, name):
        assert self.names[self.k % len(self.names)] == name, (name, self.k)
        self.k += 1
        ins.then_inc(self.sem, 1)


def padded(ap):
    return ap[:, PAD_C:PAD_C + TC], ap[:, PAD_S:PAD_S + TS]


def zero_pads(eng, ap, sem):
    eng.memset(ap[:, 0:PAD_C], 0.0)
    eng.memset(ap[:, PAD_C + TC:PAD_S], 0.0)
    eng.memset(ap[:, PAD_S + TS:TP], 0.0).then_inc(sem, 1)


def rglru(nc, d):
    NJ = D_B // P
    W = PAD_S + TS - PAD_C
    with ExitStack() as stack:
        s = Scope(nc, stack, "lru")
        par = s.sb("par", [P, 7, NJ])
        bias = s.sb("bias", [P, 4, NJ])
        h0 = s.sb("h0", [P, 2, NJ])
        sp8 = s.sb("sp8", [P, 2, NJ])
        nsp8 = s.sb("nsp8", [P, 2, NJ])
        nsp16 = s.sb("nsp16", [P, 2, NJ])
        tmp = s.sb("tmp", [P, 2, NJ])
        ident = s.sb("ident", [P, P])
        gates = s.sb("gates", [P, 4, P])
        xb = s.sb("xb", [P, TP])
        gb = s.sb("gb", [P, T])
        cv = s.sb("cv", [P, TP])
        cv2 = s.sb("cv2", [P, TP])
        xc = s.sb("xc", [P, T])
        rg = s.sb("rg", [P, 2, T])
        ig = s.sb("ig", [P, 2, T])
        av = s.sb("av", [P, 2, T])
        th = s.sb("th", [P, 2, T])
        h = s.sb("h", [P, 2, T])
        ge = s.sb("ge", [P, T])
        y = s.sb("y", [P, T])
        fin = s.sb("fin", [P, 2, NJ])
        finT = s.sb("finT", [2 * NJ, P])
        acc = [s.ps(f"acc{i}", [P, NSEG, 512]) for i in range(2)]
        par_in, pads, sp_done = s.sem("par_in"), s.sem("pads"), s.sem("sp_done")
        xb_in, gb_in, gates_in, y_out = s.sem("xb_in"), s.sem("gb_in"), s.sem("gates_in"), s.sem("y_out")
        fin_turned, fin_copied, fin_out = s.sem("fin_turned"), s.sem("fin_copied"), s.sem("fin_out")
        pe_s = Steps(s.sem("pe_s"), "a0 x0 a1 x1")
        act_s = Steps(s.sem("act_s"), "rg0 ig0 rg1 ig1 gelu th0 av0 sq0 th1 av1 sq1 root0 root1")
        dve_s = Steps(s.sem("dve_s"), "c0 c1 c2 c3 xc q0 q1 u0 hc0 hs0 fin0 u1 hc1 hs1 fin1 sum y")
        pool_s = Steps(s.sem("pool_s"), "xi0 xi1")
        block = stack.enter_context(nc.Block())
        gsrc = d["lru_gates"]

        @block.sync
        def _(sp):
            for dst, name in ((par, "lru_par"), (bias, "lru_bias"), (h0, "lru_h0"), (ident, "ident")):
                sp.dma_start(dst[:], d[name]).then_inc(par_in, 16)
            sp.sem_inc(y_out, 16)

            def load(j):
                for dst, off, n in zip(padded(xb), (0, TC), (TC, TS)):
                    sp.dma_start(dst, d["FEAT"][bass.ds((F_XB + j) * P, P), off:off + n]).then_inc(xb_in, 16)
                sp.dma_start(gb[:], d["FEAT"][bass.ds((F_GB + j) * P, P), :]).then_inc(gb_in, 16)
                for b in range(2):
                    sp.dma_start(gates[64 * b:64 * b + 64, :, 64 * b:64 * b + 64],
                                 gsrc[:, bass.ds(2 * j + b, 1)].rearrange("m o i k -> i (m o) k")).then_inc(gates_in, 16)

            def store(j):
                sp.wait_ge(dve_s.sem, dve_s.at("y", j))
                sp.dma_start(d["YT"][bass.ds(D_A + j * P, P), :], y[:]).then_inc(y_out, 16)
            sp.wait_ge(pads, 2)
            load(0)
            with sp.Fori(1, NJ) as j:
                sp.wait_ge(act_s.sem, act_s.at("gelu", j - 1))
                load(j)
                store(j - 1)
            store(NJ - 1)
            sp.wait_ge(fin_copied, 1)
            sp.dma_start(d["new_rglru"], finT[:]).then_inc(fin_out, 16)
            sp.wait_ge(fin_out, 16)
            sp.wait_ge(y_out, 16 * (NJ + 1))

        @block.gpsimd
        def _(pool):
            zero_pads(pool, xb, pads)
            pool.memset(gates[:], 0.0).then_inc(pads, 1)
            with pool.Fori(0, NJ) as j:
                for r in range(2):
                    pool.wait_ge(act_s.sem, act_s.at(f"ig{r}", j))
                    pool.wait_ge(dve_s.sem, dve_s.at("xc", j))
                    pool_s.done(pool.tensor_tensor(ig[:, r], ig[:, r], xc[:], ALU.mult), f"xi{r}")

        @block.tensor
        def _(pe):
            with pe.Fori(0, NJ) as j:
                pe.wait_ge(gates_in, 32 * (j + 1))
                pe.wait_ge(dve_s.sem, dve_s.at("xc", j))
                for n, (g, r) in enumerate((("a", 0), ("x", 0), ("a", 1), ("x", 1))):
                    if n >= 2:
                        pe.wait_ge(act_s.sem, act_s.at(("rg0", "ig0")[n - 2], j))
                    for q in range(NSEG):
                        last = pe.matmul(acc[n % 2][:, q, 0:SEG], gates[:, (2 if g == "x" else 0) + r, :],
                                         xc[:, q * SEG:(q + 1) * SEG], start=True, stop=True)
                    pe_s.done(last, f"{g}{r}")
            pe.wait_ge(dve_s.sem, dve_s.at("fin1", NJ - 1))
            pe.wait_ge(par_in, 64)
            pe.wait_ge(act_s.sem, act_s.at("ig1", NJ - 1))
            pe.transpose(acc[0][0:2 * NJ, 0, 0:P], fin[:].rearrange("p r j -> p (r j)"), ident[:]).then_inc(fin_turned, 1)

        @block.scalar
        def _(act):
            act.wait_ge(par_in, 64)
            act.activation(tmp[:], par[:, 5:7, :], ACT.Abs).then_inc(sp_done, 1)
            act.wait_ge(sp_done, 1)
            act.activation(tmp[:], tmp[:], ACT.Exp, scale=-1.0).then_inc(sp_done, 1)
            act.wait_ge(sp_done, 2)
            act.activation(tmp[:], tmp[:], ACT.Ln, bias=1.0).then_inc(sp_done, 1)
            act.wait_ge(sp_done, 8)
            with act.Fori(0, NJ) as j:
                for n, (g, r, dst) in enumerate((("rg", 0, rg), ("ig", 0, ig), ("rg", 1, rg), ("ig", 1, ig))):
                    act.wait_ge(pe_s.sem, pe_s.at(pe_s.names[n], j))
                    act_s.done(act.activation(dst[:, r].rearrange("p (q c) -> p q c", q=NSEG), acc[n % 2][:, :, 0:SEG],
                                              ACT.Sigmoid, bias=bias[:, (2 if g == "ig" else 0) + r, bass.ds(j, 1)]), f"{g}{r}")
                act.wait_ge(gb_in, 16 * (j + 1))
                act_s.done(act.activation(ge[:], gb[:], ACT.Gelu_apprx_tanh), "gelu")
                for r in range(2):
                    act.wait_ge(act_s.sem, act_s.at(f"rg{r}", j))
                    act_s.done(act.activation(th[:, r], rg[:, r], ACT.Tanh, scale=sp8[:, r, bass.ds(j, 1)]), f"th{r}")
                    act_s.done(act.activation(av[:, r], rg[:, r], ACT.Exp, scale=nsp8[:, r, bass.ds(j, 1)]), f"av{r}")
                    act_s.done(act.activation(h[:, r], rg[:, r], ACT.Exp, scale=nsp16[:, r, bass.ds(j, 1)]), f"sq{r}")
                for r in range(2):
                    act.wait_ge(dve_s.sem, dve_s.at(f"q{r}", j))
                    act_s.done(act.activation(th[:, r], th[:, r], ACT.Sqrt), f"root{r}")

        @block.vector
        def _(dve):
            dve.wait_ge(sp_done, 3)
            dve.tensor_scalar(sp8[:], par[:, 5:7, :], -1.0, 0.0, ALU.mult, ALU.max).then_inc(sp_done, 1)
            dve.wait_ge(sp_done, 4)
            dve.tensor_tensor(sp8[:], sp8[:], tmp[:], ALU.add).then_inc(sp_done, 1)
            dve.wait_ge(sp_done, 5)
            dve.tensor_scalar(nsp8[:], sp8[:], -8.0, None, ALU.mult).then_inc(sp_done, 1)
            dve.tensor_scalar(nsp16[:], sp8[:], -16.0, None, ALU.mult).then_inc(sp_done, 1)
            dve.wait_ge(sp_done, 7)
            dve.tensor_scalar(sp8[:], sp8[:], 8.0, None, ALU.mult).then_inc(sp_done, 1)
            dve.wait_ge(sp_done, 8)
            with dve.Fori(0, NJ) as j:
                at = lambda n: dve.wait_ge(dve_s.sem, dve_s.at(n, j))
                tap = lambda k: par[:, k, bass.ds(j, 1)]
                lo = PAD_C
                dve.wait_ge(xb_in, 32 * (j + 1))
                dve_s.done(dve.tensor_scalar(cv[:, lo:lo + W], xb[:, lo - 2:lo - 2 + W], tap(0), tap(4), ALU.mult, ALU.add), "c0")
                at("c0")
                dve_s.done(dve.scalar_tensor_tensor(cv2[:, lo:lo + W], xb[:, lo - 1:lo - 1 + W], tap(1), cv[:, lo:lo + W],
                                                    ALU.mult, ALU.add), "c1")
                at("c1")
                dve_s.done(dve.scalar_tensor_tensor(cv[:, lo:lo + W], xb[:, lo:lo + W], tap(2), cv2[:, lo:lo + W],
                                                    ALU.mult, ALU.add), "c2")
                at("c2")
                for n, off, w, name in ((PAD_C, 0, TC, "c3"), (PAD_S, TC, TS, "xc")):
                    dve_s.done(dve.scalar_tensor_tensor(xc[:, off:off + w], xb[:, n + 1:n + 1 + w], tap(3), cv[:, n:n + w],
                                                        ALU.mult, ALU.add), name)
                for r in range(2):
                    dve.wait_ge(act_s.sem, act_s.at(f"sq{r}", j))
                    dve_s.done(dve.scalar_tensor_tensor(th[:, r], h[:, r], 1.0, th[:, r], ALU.add, ALU.mult), f"q{r}")
                for r in range(2):
                    back = slice(None, None, -1) if r else slice(None)
                    dve.wait_ge(act_s.sem, act_s.at(f"root{r}", j))
                    dve.wait_ge(pool_s.sem, pool_s.at(f"xi{r}", j))
                    dve_s.done(dve.tensor_tensor(th[:, r], th[:, r], ig[:, r], ALU.mult), f"u{r}")
                    at(f"u{r}")
                    for lo, w, init, name in ((0, TC, 0.0, "hc"), (TC, TS, h0[:, r, bass.ds(j, 1)], "hs")):
                        cut = lambda b: b[:, r, lo:lo + w][:, back]
                        dve_s.done(dve.tensor_tensor_scan(cut(h), cut(av), cut(th), init, ALU.mult, ALU.add), f"{name}{r}")
                    at(f"hc{r}")
                    last = 0 if r else TC - 1
                    dve_s.done(dve.tensor_copy(fin[:, r, bass.ds(j, 1)], h[:, r, last:last + 1]), f"fin{r}")
                at("hs1")
                dve_s.done(dve.tensor_tensor(h[:, 0], h[:, 0], h[:, 1], ALU.add), "sum")
                at("sum")
                dve.wait_ge(act_s.sem, act_s.at("gelu", j))
                dve.wait_ge(y_out, 16 * (j + 1))
                dve_s.done(dve.tensor_tensor(y[:], h[:, 0], ge[:], ALU.mult), "y")
            dve.wait_ge(fin_turned, 1)
            dve.tensor_copy(finT[:], acc[0][0:2 * NJ, 0, 0:P]).then_inc(fin_copied, 1)


def ssd(nc, d):
    NX, NB = D_C // P, 2
    NCH = NX + 2 * NB
    H, HC = 24, 12
    W = PAD_S + TS - PAD_C
    R1 = 32
    HG = HC // 2
    GW = HG * HD
    with ExitStack() as stack:
        s0 = Scope(nc, stack, "ssd")
        ident = s0.sb("ident", [P, P])
        ones = s0.sb("ones", [P, P])
        upper = s0.sb("upper", [P, P])
        lower = s0.sb("lower", [P, P])
        dskip = s0.sb("dskip", [P, HC])
        norm_g = s0.sb("norm_g", [P, NX])
        ytok = s0.sb("ytok", [P, NT, D_C])
        st = s0.sb("st", [P, 2, NT, D_C])
        s_init = s0.sb("s_init", [P, 2, D_C])
        ea = s0.sb("ea", [P, NT, H])
        cdec = s0.sb("cdec", [P, NT, H])
        epsc = s0.sb("epsc", [P, 1])
        const_in = s0.sem("const_in")

        with ExitStack() as inner:
            s = Scope(nc, inner, "pre")
            par = s.sb("par", [P, 5, NCH])
            u = s.sb("u", [P, 2, TP])
            cv = s.sb("cv", [P, TP])
            cv2 = s.sb("cv2", [P, TP])
            xc = s.sb("xc", [P, 2, T])
            xo = s.sb("xo", [P, 2, T])
            dpar = s.sb("dpar", [64, 2])
            dt = s.sb("dt", [64, T])
            e1 = s.sb("e1", [64, T])
            mx = s.sb("mx", [64, T])
            keep = s.sb("keep", [64, T])
            acs = s.sb("acs", [64, T])
            s_raw = s.sb("s_raw", [P, 2 * NX, P])
            turn = s.ps("turn", [P, 2, 512])
            par_in, pads, u_out = s.sem("par_in"), s.sem("pads"), [s.sem(f"u_out{i}") for i in range(2)]
            u_in = [s.sem(f"u_in{i}") for i in range(2)]
            dt_in, dt_abs, dt_done, dt_out = s.sem("dt_in"), s.sem("dt_abs"), s.sem("dt_done"), s.sem("dt_out")
            conv, silu = Steps(s.sem("conv"), "c0 c1 c2 c3 xc"), s.sem("silu")
            raw_in, turned, placed = s.sem("raw_in"), s.sem("turned"), s.sem("placed")
            dt_link = s.sem("dt_link")
            block = inner.enter_context(nc.Block())

            @block.sync
            def _(sp):
                for dst, name in ((par, "ssd_par"), (ident, "ident"), (ones, "ones"), (upper, "upper"), (lower, "lower"),
                                  (dskip, "ssd_d"), (norm_g, "ssd_norm_g")):
                    sp.dma_start(dst[:], d[name]).then_inc(const_in, 16)

                def load(b, j):
                    for dst, off, n in zip(padded(u[:, b]), (0, TC), (TC, TS)):
                        sp.dma_start(dst, d["FEAT"][bass.ds((F_XBC + j) * P, P), off:off + n]).then_inc(u_in[b], 16)
                sp.wait_ge(pads, 4)
                for b in range(2):
                    load(b, b)
                for r in range(2):
                    sp.dma_start(dt[R1 * r:R1 * r + HC, :], d["FEAT"][F_DT * P + HC * r:F_DT * P + HC * (r + 1), :]).then_inc(dt_in, 16)
                    sp.dma_start(dpar[R1 * r:R1 * r + HC, :], d["ssd_dt"][HC * r:HC * (r + 1), :]).then_inc(dt_in, 16)
                sp.dma_start(s_raw[:], d["ssd_s0"].rearrange("(n p) k -> p n k", p=P)).then_inc(raw_in, 16)
                with sp.Fori(1, NCH // 2) as i:
                    for b in range(2):
                        sp.wait_ge(conv.sem, conv.at("xc", 2 * (i - 1) + b))
                        load(b, 2 * i + b)
                sp.wait_ge(dt_done, 1)
                for n, rows in enumerate((acs, dt)):
                    for r in range(2):
                        lo = H * n + HC * r
                        sp.dma_start(d["ROWS"][lo:lo + HC, :], rows[R1 * r:R1 * r + HC, :]).then_inc(dt_out, 16)
                sp.wait_ge(dt_out, 64)

            @block.gpsimd
            def _(pool):
                for b in range(2):
                    zero_pads(pool, u[:, b], pads)
                pool.memset(epsc[:], 1e-5)
                pool.memset(dt[:], 0.0)
                pool.memset(dpar[:], 0.0)
                pool.memset(keep[:], 1.0).then_inc(pads, 1)
                pool.wait_ge(pads, 3)
                k = keep[:].rearrange("p (c t) -> p c t", t=P)
                pool.memset(k[0:32, :, 0:1], 0.0)
                pool.memset(k[32:64, :, P - 1:P], 0.0).then_inc(pads, 1)

            @block.tensor
            def _(pe):
                pe.wait_ge(const_in, 16 * 7)
                pe.wait_ge(raw_in, 16)
                for q in range(3):
                    if q:
                        pe.wait_ge(placed, q)
                    for b in range(4):
                        last = pe.transpose(turn[:, 0, b * P:(b + 1) * P], s_raw[:, 4 * q + b, :], ident[:])
                    last.then_inc(turned, 1)

            @block.scalar
            def _(act):
                act.wait_ge(dt_in, 64)
                act.activation(e1[:], dt[:], ACT.Abs, bias=dpar[:, 0:1]).then_inc(dt_abs, 1)
                act.wait_ge(dt_abs, 1)
                act.activation(e1[:], e1[:], ACT.Exp, scale=-1.0).then_inc(dt_abs, 1)
                act.wait_ge(dt_abs, 2)
                act.activation(e1[:], e1[:], ACT.Ln, bias=1.0).then_inc(dt_abs, 1)
                act.activation(dpar[:, 1:2], dpar[:, 1:2], ACT.Exp).then_inc(dt_abs, 1)
                flat = s_init[:].rearrange("p r c -> p (r c)")
                for q in range(3):
                    act.wait_ge(turned, q + 1)
                    act.activation(flat[:, q * 512:(q + 1) * 512], turn[:, 0, :], ACT.Copy).then_inc(placed, 1)
                act.sem_inc(silu, 2)
                for b in range(2):
                    act.sem_inc(u_out[b], 16)
                with act.Fori(0, NCH // 2) as i:
                    for b in range(2):
                        act.wait_ge(conv.sem, conv.at("xc", 2 * i + b))
                        act.wait_ge(u_out[b], 16 * (i + 1))
                        act.activation(xo[:, b], xc[:, b], ACT.Silu).then_inc(silu, 1)
                        act.wait_ge(silu, 2 * i + b + 3)
                        act.dma_start(d["XBC"][bass.ds((2 * i + b) * P, P), :], xo[:, b]).then_inc(u_out[b], 16)
                for b in range(2):
                    act.wait_ge(u_out[b], 16 * (NCH // 2 + 1))

            @block.vector
            def _(dve):
                link = Chain(dve, dt_link)
                dve.wait_ge(pads, 4)
                dve.wait_ge(dt_in, 64)
                dve.wait_ge(dt_abs, 4)
                link(dve.tensor_scalar(mx[:], dt[:], dpar[:, 0:1], 0.0, ALU.add, ALU.max))
                link(dve.tensor_tensor(dt[:], mx[:], e1[:], ALU.add))
                link(dve.tensor_scalar(mx[:], dt[:], dpar[:, 1:2], -1.0, ALU.mult, ALU.mult))
                dve.tensor_tensor_scan(acs[0:32, :], keep[0:32, :], mx[0:32, :], 0.0, ALU.mult, ALU.add)
                dve.tensor_tensor_scan(acs[32:64, ::-1], keep[32:64, ::-1], mx[32:64, ::-1], 0.0, ALU.mult,
                                       ALU.add).then_inc(dt_done, 1)
                dve.wait_ge(const_in, 16 * 7)
                with dve.Fori(0, NCH // 2) as i:
                    for b in range(2):
                        j = 2 * i + b
                        tap = lambda k: par[:, k, bass.ds(j, 1)]
                        at = lambda n: dve.wait_ge(conv.sem, conv.at(n, j))
                        ub, lo = u[:, b], PAD_C
                        dve.wait_ge(u_in[b], 32 * (i + 1))
                        conv.done(dve.tensor_scalar(cv[:, lo:lo + W], ub[:, lo - 2:lo - 2 + W], tap(0), tap(4), ALU.mult, ALU.add), "c0")
                        at("c0")
                        conv.done(dve.scalar_tensor_tensor(cv2[:, lo:lo + W], ub[:, lo - 1:lo - 1 + W], tap(1), cv[:, lo:lo + W],
                                                           ALU.mult, ALU.add), "c1")
                        at("c1")
                        conv.done(dve.scalar_tensor_tensor(cv[:, lo:lo + W], ub[:, lo:lo + W], tap(2), cv2[:, lo:lo + W],
                                                           ALU.mult, ALU.add), "c2")
                        at("c2")
                        dve.wait_ge(silu, 2 * i + b + 1)
                        for n, off, w, name in ((PAD_C, 0, TC, "c3"), (PAD_S, TC, TS, "xc")):
                            conv.done(dve.scalar_tensor_tensor(xc[:, b, off:off + w], ub[:, n + 1:n + 1 + w], tap(3), cv[:, n:n + w],
                                                               ALU.mult, ALU.add), name)
                        at("xc")

        with ExitStack() as inner:
            s = Scope(nc, inner, "chunk")
            xbc = s.sb("xbc", [P, NCH, P])
            rows = s.sb("rows", [2 * H, P])
            bc = s.sb("bc", [P, H, P])
            lm = s.sb("lm", [P, H, P])
            cols = s.sb("cols", [P, 2 * H])
            g = s.sb("g", [P, 2, NB, P])
            xt = s.sb("xt", [P, D_C])
            bt = s.sb("bt", [P, NB, P])
            xd = s.sb("xd", [P, 2, D_C])
            xe = s.sb("xe", [P, 2, D_C])
            dec = s.sb("dec", [P, 2, HC])
            skip = s.sb("skip", [P, D_C])
            tp = s.ps("tp", [P, 2, 512])
            gp = s.ps("gp")
            yp = s.ps("yp", [P, 2, 512])
            sp0 = s.ps("sp0", [P, 2, 512])
            xbc_in, rows_in, bc_in = s.sem("xbc_in"), s.sem("rows_in"), s.sem("bc_in")
            pe_s = Steps(s.sem("pe_s"), "turn g y st0 st1")
            act_s = Steps(s.sem("act_s"), "xt bt ea cdf cdb dec L st0 st1")
            dve_s = Steps(s.sem("dve_s"), "cols gf gb clamp d0 d1 m xd0 xd1 xe0 xe1 y")
            pool_s = Steps(s.sem("pool_s"), "skip")
            block = inner.enter_context(nc.Block())

            @block.sync
            def _(sp):
                def load(c):
                    sp.dma_start(xbc[:], d["XBC"].rearrange("(n p) t -> p n t", p=P)[:, :, bass.ds(c * P, P)]).then_inc(xbc_in, 16)
                    sp.dma_start(rows[:], d["ROWS"][:, bass.ds(c * P, P)]).then_inc(rows_in, 16)

                def load_bc(c):
                    sp.dma_start(bc[:], d["ROWS"][0:H, bass.ds(c * P, P)].partition_broadcast(P)).then_inc(bc_in, 16)
                load(0)
                load_bc(0)
                with sp.Fori(1, NT) as c:
                    sp.wait_ge(pe_s.sem, pe_s.at("g", c - 1))
                    load(c)
                    sp.wait_ge(dve_s.sem, dve_s.at("d1", c - 1))
                    sp.wait_ge(act_s.sem, act_s.at("cdb", c - 1))
                    load_bc(c)

            @block.gpsimd
            def _(pool):
                with pool.Fori(0, NT) as c:
                    pool.wait_ge(act_s.sem, act_s.at("xt", c))
                    pool_s.done(pool.tensor_tensor(skip[:].rearrange("p (h k) -> p h k", h=HC), xt[:].rearrange("p (h k) -> p h k", h=HC),
                                                   dskip[:].unsqueeze(2).broadcast_to([P, HC, HD]), ALU.mult), "skip")

            @block.tensor
            def _(pe):
                with pe.Fori(0, NT) as c:
                    pe.wait_ge(xbc_in, 16 * (c + 1))
                    pe.wait_ge(rows_in, 16 * (c + 1))
                    for n in range(8):
                        pe.transpose(tp[:, n // 4, n % 4 * P:(n % 4 + 1) * P], xbc[:, n, :], ident[:])
                    last = pe.transpose(gp[:, 2 * P:2 * P + 2 * H], rows[:], ident[0:2 * H, 0:2 * H])
                    pe_s.done(last, "turn")
                    for b in range(NB):
                        last = pe.matmul(gp[:, b * P:(b + 1) * P], xbc[:, NX + b, :], xbc[:, NX + NB + b, :], start=True, stop=True)
                    pe_s.done(last, "g")
                    pe.wait_ge(dve_s.sem, dve_s.at("xd1", c))
                    for h in range(HC):
                        for r in range(2):
                            last = pe.matmul(yp[:, h // HG, h % HG * HD:(h % HG + 1) * HD], lm[:, HC * r + h, :],
                                             xd[:, r, h * HD:(h + 1) * HD], start=r == 0, stop=r == 1)
                    pe_s.done(last, "y")
                    pe.wait_ge(act_s.sem, act_s.at("bt", c))
                    for r, dst in ((0, sp0), (1, tp)):
                        pe.wait_ge(dve_s.sem, dve_s.at(f"xe{r}", c))
                        for b in range(NB):
                            last = pe.matmul(dst[:, b, 0:GW], bt[:, b, :], xe[:, r, b * GW:(b + 1) * GW], start=True, stop=True)
                        pe_s.done(last, f"st{r}")
                    pe.wait_ge(act_s.sem, act_s.at("st1", c))
                    pe.wait_ge(dve_s.sem, dve_s.at("y", c))

            @block.scalar
            def _(act):
                with act.Fori(0, NT) as c:
                    cc = bass.ds(c, 1)
                    act.wait_ge(pe_s.sem, pe_s.at("turn", c))
                    flat = tp[:].rearrange("p a b -> p (a b)")
                    act_s.done(act.activation(xt[:], flat[:, 0:D_C], ACT.Copy), "xt")
                    act_s.done(act.activation(bt[:].rearrange("p a b -> p (a b)"), flat[:, D_C:1024], ACT.Copy), "bt")
                    act.wait_ge(dve_s.sem, dve_s.at("cols", c))
                    act_s.done(act.activation(ea[:, cc, :].rearrange("p o h -> p (o h)"), cols[:, 0:H], ACT.Exp), "ea")
                    act.wait_ge(bc_in, 16 * (c + 1))
                    cd = cdec[:, cc, :].rearrange("p o h -> p (o h)")
                    act_s.done(act.activation(cd[:, 0:HC], bc[:, 0:HC, P - 1], ACT.Exp), "cdf")
                    act_s.done(act.activation(cd[:, HC:H], bc[:, HC:H, 0], ACT.Exp), "cdb")
                    act.wait_ge(dve_s.sem, dve_s.at("d1", c))
                    act_s.done(act.activation(dec[:], dec[:], ACT.Exp), "dec")
                    act.wait_ge(dve_s.sem, dve_s.at("clamp", c))
                    act_s.done(act.activation(lm[:], lm[:], ACT.Exp), "L")
                    for r, src in ((0, sp0), (1, tp)):
                        act.wait_ge(pe_s.sem, pe_s.at(f"st{r}", c))
                        act_s.done(act.activation(st[:, r, cc, :].rearrange("p o (b k) -> p (o b) k", b=NB), src[:, :, 0:GW], ACT.Copy), f"st{r}")

            @block.vector
            def _(dve):
                with dve.Fori(0, NT) as c:
                    cc = bass.ds(c, 1)
                    heads = lambda ap: ap.rearrange("p (h k) -> p h k", h=HC)
                    at = lambda n: dve.wait_ge(dve_s.sem, dve_s.at(n, c))
                    dve.wait_ge(pe_s.sem, pe_s.at("g", c))
                    dve_s.done(dve.tensor_copy(cols[:], gp[:, 2 * P:2 * P + 2 * H]), "cols")
                    for r, (m, name) in enumerate(((upper, "gf"), (lower, "gb"))):
                        dve_s.done(dve.tensor_tensor(g[:, r], gp[:, 0:2 * P].rearrange("p (b l) -> p b l", b=NB),
                                                     m[:].unsqueeze(1).broadcast_to([P, NB, P]), ALU.mult), name)
                    dve.wait_ge(bc_in, 16 * (c + 1))
                    at("cols")
                    for h in range(H):
                        last = dve.tensor_scalar(lm[:, h, :], bc[:, h, :], cols[:, h:h + 1], 0.0, ALU.subtract, ALU.min)
                    dve_s.done(last, "clamp")
                    dve_s.done(dve.tensor_tensor(dec[:, 0], bc[:, 0:HC, P - 1], cols[:, 0:HC], ALU.subtract), "d0")
                    dve_s.done(dve.tensor_tensor(dec[:, 1], bc[:, HC:H, 0], cols[:, HC:H], ALU.subtract), "d1")
                    dve.wait_ge(act_s.sem, act_s.at("L", c))
                    at("gb")
                    for q in range(4):
                        part = lm[:, q * HG:(q + 1) * HG, :]
                        last = dve.tensor_tensor(part, part, g[:, q // 2, q % 2].unsqueeze(1).broadcast_to([P, HG, P]), ALU.mult)
                    dve_s.done(last, "m")
                    for r in range(2):
                        dve_s.done(dve.tensor_tensor(heads(xd[:, r]), heads(xt[:]), cols[:, H + HC * r:H + HC * (r + 1)].unsqueeze(2)
                                                     .broadcast_to([P, HC, HD]), ALU.mult), f"xd{r}")
                    for r in range(2):
                        at(f"xd{r}")
                        dve_s.done(dve.tensor_tensor(heads(xe[:, r]), heads(xd[:, r]), dec[:, r].unsqueeze(2)
                                                     .broadcast_to([P, HC, HD]), ALU.mult), f"xe{r}")
                    dve.wait_ge(pe_s.sem, pe_s.at("y", c))
                    dve.wait_ge(pool_s.sem, pool_s.at("skip", c))
                    dve_s.done(dve.tensor_tensor(ytok[:, cc, :].rearrange("p o (b k) -> p (o b) k", b=NB), yp[:, :, 0:GW],
                                                 skip[:].rearrange("p (b k) -> p b k", b=NB), ALU.add), "y")

        with ExitStack() as inner:
            s = Scope(nc, inner, "scan")
            cur = s.sb("cur", [P, 2, 2, D_C])
            tmp = s.sb("tmp", [P, 2, D_C])
            fin = s.sb("fin", [P, 2 * NX, P])
            turn = s.ps("turn", [P, 3, 512])
            moved, kept, made = s.sem("moved"), s.sem("kept"), [s.sem(f"made{r}") for r in range(2)]
            fin_turned, fin_copied, fin_out = s.sem("fin_turned"), s.sem("fin_copied"), s.sem("fin_out")
            block = inner.enter_context(nc.Block())

            @block.tensor
            def _(pe):
                for n in range(2 * NX):
                    r, j = n // NX, n % NX
                    last = pe.transpose(turn[:, n // 4, n % 4 * P:(n % 4 + 1) * P], st[:, r, 0, j * P:(j + 1) * P], ident[:])
                last.then_inc(fin_turned, 1)

            @block.scalar
            def _(act):
                act.wait_ge(fin_turned, 1)
                act.activation(fin[:].rearrange("p (a b) k -> p a (b k)", a=3), turn[:], ACT.Copy).then_inc(fin_copied, 1)
                act.wait_ge(fin_copied, 1)
                act.dma_start(d["new_ssd"].rearrange("(n p) k -> p n k", p=P), fin[:]).then_inc(fin_out, 16)
                n = 0
                for k in range(1, NT):
                    for r in range(2):
                        c = k if r == 0 else NT - k
                        src = s_init[:, r] if k == 1 else cur[:, r, (k - 1) % 2]
                        if k < NT - 1:
                            act.wait_ge(made[r], 2 * k)
                        act.activation(st[:, r, c, :], src, ACT.Copy).then_inc(kept, 1)
                act.wait_ge(fin_out, 16)

            @block.vector
            def _(dve):
                dve.wait_ge(fin_turned, 1)
                dve.memset(st[:, :, 0, :], 0.0)
                heads = lambda ap: ap.rearrange("p (h k) -> p h k", h=HC)
                for k in range(1, NT - 1):
                    for r in range(2):
                        c = k if r == 0 else NT - k
                        src = s_init[:, r] if k == 1 else cur[:, r, (k - 1) % 2]
                        if k > 1:
                            dve.wait_ge(made[r], 2 * k - 2)
                        dve.tensor_tensor(heads(tmp[:, r]), heads(src), cdec[:, c, HC * r:HC * (r + 1)].unsqueeze(2)
                                          .broadcast_to([P, HC, HD]), ALU.mult).then_inc(made[r], 1)
                    for r in range(2):
                        c = k if r == 0 else NT - k
                        dve.wait_ge(made[r], 2 * k - 1)
                        if k > 2:
                            dve.wait_ge(kept, 2 * (k - 2) + r + 1)
                        dve.tensor_tensor(cur[:, r, k % 2], tmp[:, r], st[:, r, c, :], ALU.add).then_inc(made[r], 1)

        with ExitStack() as inner:
            s = Scope(nc, inner, "off")
            ct = s.sb("ct", [P, NB, P])
            z = s.sb("z", [P, NX, P])
            sz = s.sb("sz", [P, NX, P])
            t0 = s.sb("t0", [P, 2, D_C])
            yt = s.sb("yt", [P, D_C])
            yg = s.sb("yg", [P, NX, P])
            sq = s.sb("sq", [P, NX, P])
            rt = s.sb("rt", [P, P])
            ri = s.sb("ri", [P, P])
            yn = s.sb("yn", [P, NX, P])
            off = [s.ps(f"off{r}", [P, 2, 512]) for r in range(2)]
            turn = s.ps("turn", [P, 2, 512])
            ms = s.ps("ms")
            in_s, out_s = s.sem("in_s"), s.sem("out_s")
            pe_s = Steps(s.sem("pe_s"), "off0 off1 turn ms")
            act_s = Steps(s.sem("act_s"), "sz sq root")
            dve_s = Steps(s.sem("dve_s"), "t0 t1 a0 a1 yg inv yn0 yn")
            block = inner.enter_context(nc.Block())

            @block.sync
            def _(sp):
                sp.sem_inc(out_s, 16)
                xbc_v = d["XBC"].rearrange("(n p) t -> p n t", p=P)
                z_v = d["FEAT"].rearrange("(n p) t -> p n t", p=P)

                def load(c):
                    sp.dma_start(ct[:], xbc_v[:, NX + NB:NCH, bass.ds(c * P, P)]).then_inc(in_s, 16)
                    sp.dma_start(z[:], z_v[:, F_Z:F_Z + NX, bass.ds(c * P, P)]).then_inc(in_s, 16)

                def store(c):
                    sp.wait_ge(dve_s.sem, dve_s.at("yn", c))
                    sp.dma_start(d["YT"].rearrange("(n p) t -> p n t", p=P)[:, (D_A + D_B) // P:KT, bass.ds(c * P, P)], yn[:]
                                 ).then_inc(out_s, 16)
                load(0)
                with sp.Fori(1, NT) as c:
                    sp.wait_ge(pe_s.sem, pe_s.at("off1", c - 1))
                    sp.wait_ge(act_s.sem, act_s.at("sz", c - 1))
                    load(c)
                    store(c - 1)
                store(NT - 1)
                sp.wait_ge(out_s, 16 * (NT + 1))

            @block.tensor
            def _(pe):
                with pe.Fori(0, NT) as c:
                    pe.wait_ge(in_s, 32 * (c + 1))
                    for r in range(2):
                        for b in range(NB):
                            last = pe.matmul(off[r][:, b, 0:GW], ct[:, b, :],
                                             st[:, r, bass.ds(c, 1), b * GW:(b + 1) * GW].rearrange("p o k -> p (o k)"), start=True, stop=True)
                        pe_s.done(last, f"off{r}")
                    pe.wait_ge(dve_s.sem, dve_s.at("a1", c))
                    for n in range(NX):
                        last = pe.transpose(turn[:, n // 4, n % 4 * P:(n % 4 + 1) * P], yt[:, n * P:(n + 1) * P], ident[:])
                    pe_s.done(last, "turn")
                    pe.wait_ge(act_s.sem, act_s.at("sq", c))
                    for n in range(NX):
                        last = pe.matmul(ms[:, 0:P], ones[:], sq[:, n, :], start=n == 0, stop=n == NX - 1)
                    pe_s.done(last, "ms")

            @block.scalar
            def _(act):
                with act.Fori(0, NT) as c:
                    act.wait_ge(in_s, 32 * (c + 1))
                    act_s.done(act.activation(sz[:], z[:], ACT.Silu), "sz")
                    act.wait_ge(dve_s.sem, dve_s.at("yg", c))
                    act_s.done(act.activation(sq[:], yg[:], ACT.Square), "sq")
                    act.wait_ge(pe_s.sem, pe_s.at("ms", c))
                    act_s.done(act.activation(rt[:], ms[:, 0:P], ACT.Sqrt, bias=epsc[:, 0:1], scale=1.0 / D_C), "root")

            @block.vector
            def _(dve):
                with dve.Fori(0, NT) as c:
                    heads = lambda ap: ap.rearrange("p (h k) -> p h k", h=HC)
                    at = lambda n: dve.wait_ge(dve_s.sem, dve_s.at(n, c))
                    for r in range(2):
                        dve.wait_ge(pe_s.sem, pe_s.at(f"off{r}", c))
                        for b in range(NB):
                            last = dve.tensor_tensor(heads(t0[:, r])[:, b * HG:(b + 1) * HG, :],
                                                     off[r][:, b, 0:GW].rearrange("p (h k) -> p h k", h=HG),
                                                     ea[:, bass.ds(c, 1), HC * r + b * HG:HC * r + (b + 1) * HG].rearrange("p o h -> p (o h)")
                                                     .unsqueeze(2).broadcast_to([P, HG, HD]), ALU.mult)
                        dve_s.done(last, f"t{r}")
                    at("t1")
                    dve_s.done(dve.tensor_tensor(t0[:, 0], t0[:, 0], t0[:, 1], ALU.add), "a0")
                    at("a0")
                    dve_s.done(dve.tensor_tensor(yt[:], t0[:, 0], ytok[:, bass.ds(c, 1), :].rearrange("p o k -> p (o k)"), ALU.add), "a1")
                    dve.wait_ge(pe_s.sem, pe_s.at("turn", c))
                    dve.wait_ge(act_s.sem, act_s.at("sz", c))
                    dve_s.done(dve.tensor_tensor(yg[:].rearrange("p n k -> p (n k)"), turn[:].rearrange("p a b -> p (a b)")[:, 0:D_C],
                                                 sz[:].rearrange("p n k -> p (n k)"), ALU.mult), "yg")
                    dve.wait_ge(act_s.sem, act_s.at("root", c))
                    dve_s.done(dve.reciprocal(ri[:], rt[:]), "inv")
                    at("inv")
                    dve.wait_ge(out_s, 16 * (c + 1))
                    dve_s.done(dve.tensor_tensor(yn[:], yg[:], ri[:].unsqueeze(1).broadcast_to([P, NX, P]), ALU.mult), "yn0")
                    at("yn0")
                    dve_s.done(dve.tensor_tensor(yn[:], yn[:], norm_g[:].unsqueeze(2).broadcast_to([P, NX, P]), ALU.mult), "yn")


RC = 64
NJ_A = D_A // P


def rwkv_features(nc, d):
    NJ = NJ_A
    W = PAD_S + TS - PAD_C
    with ExitStack() as stack:
        s = Scope(nc, stack, "rf")
        mu = s.sb("mu", [P, 15])
        hmu = s.sb("hmu", [P, 15])
        omu = s.sb("omu", [P, 15])
        par = s.sb("par", [P, 7, NJ])
        oka = s.sb("oka", [P, NJ])
        bd = s.sb("bd", [P, P])
        up = s.sb("up", [P, 3, P])
        keep = s.sb("keep", [P, 2, T])
        u = s.sb("u", [P, 3, TP])
        sm = s.sb("sm", [P, TP])
        lora = s.sb("lora", [P, 3, T])
        m = s.sb("m", [P, 3, T])
        kk = s.sb("kk", [P, T])
        t1 = s.sb("t1", [P, T])
        sg = s.sb("sg", [P, 2, T])
        a = s.sb("a", [P, 2, T])
        kd = s.sb("kd", [P, 2, T])
        ls = s.sb("ls", [P, 2, T])
        pt = s.sb("pt", [P, 3, T])
        o = s.sb("o", [P, 4, T])
        g = s.sb("g", [P, T])
        bv = s.sb("bv", [P, T])
        pc = s.sb("pc", [P, 2, NJ, T // RC])
        acc = [s.ps(f"acc{i}", [P, NSEG, 512]) for i in range(2)]
        par_in, pads, prep, u0_in, u_in, up_in = (s.sem(n) for n in ("par_in", "pads", "prep", "u0_in", "u_in", "up_in"))
        o_out, g_out, b_out, pc_out = s.sem("o_out"), s.sem("g_out"), s.sem("b_out"), s.sem("pc_out")
        mixed, lora_act = s.sem("mixed"), s.sem("lora_act")
        link_s, bv_s = s.sem("link"), s.sem("bv_s")
        pe_s = Steps(s.sem("pe_s"), "w0 a0 w1 a1 ss g bonus")
        act_s = Steps(s.sem("act_s"), "sg0 a0 sg1 a1 sq root g p0 i0 q0 p1 i1 q1")
        dve_s = Steps(s.sem("dve_s"), "mr mk mv kk rec kkn km0 kd0 km1 kd1 bsum b0 b1 L0 L1 D0 D1 pc0 r0 x0 y0 z0 pc1 r1 x1 y1 z1 bv")
        block = stack.enter_context(nc.Block())
        seg = lambda ap: ap.rearrange("p (q c) -> p q c", q=NSEG)

        @block.sync
        def _(sp):
            for dst, name in ((mu, "rw_mu"), (par, "rw_par"), (bd, "bd_ones")):
                sp.dma_start(dst[:], d[name]).then_inc(par_in, 16)

            def load(b, tile, sem):
                for dst, off, n in zip(padded(u[:, b]), (0, TC), (TC, TS)):
                    sp.dma_start(dst, d["FEAT"][bass.ds(tile * P, P), off:off + n]).then_inc(sem, 16)

            def load_up(j):
                sp.dma_start(up[:], d["rw_up"][:, :, bass.ds(j * P, P)]).then_inc(up_in, 16)
            sp.wait_ge(pads, 4)
            for b in range(3):
                load(b, F_WD + b, u0_in)
            load_up(0)
            sp.wait_ge(mixed, 3)
            for b in range(3):
                load(b, NJ * b, u_in)

            def store(r, j):
                dst = lambda n: d["RW"][n, r, bass.ds(j * P, P), :]
                for n, step in ((0, "x"), (1, "y"), (2, "z")):
                    sp.wait_ge(dve_s.sem, dve_s.at(f"{step}{r}", j))
                    sp.dma_start(dst(n), o[:, n]).then_inc(o_out, 16)
                sp.dma_start(d["RT"][r, bass.ds(j * P, P), :], o[:, 3]).then_inc(o_out, 16)
                sp.dma_start(dst(3), m[:, 2]).then_inc(o_out, 16)

            def tile(j, more):
                if more:
                    sp.wait_ge(dve_s.sem, dve_s.at("mv", j))
                    for b in range(3):
                        load(b, NJ * b + j + 1, u_in)
                sp.wait_ge(act_s.sem, act_s.at("g", j))
                sp.dma_start(d["GATE"][bass.ds(j * P, P), :], g[:]).then_inc(g_out, 16)
                if more:
                    load_up(j + 1)
                store(0, j)
                store(1, j)
                sp.wait_ge(dve_s.sem, dve_s.at("bv", j))
                sp.dma_start(d["BONUS"][bass.ds(j * P, P), :], bv[:]).then_inc(b_out, 16)
            with sp.Fori(0, NJ - 1) as j:
                tile(j, True)
            tile(NJ - 1, False)
            sp.wait_ge(o_out, 160 * NJ + 80)
            sp.wait_ge(g_out, 16 * (NJ + 1))
            sp.wait_ge(b_out, 16 * (NJ + 1))
            sp.wait_ge(dve_s.sem, dve_s.at("pc1", NJ - 1))
            sp.dma_start(d["PC"], pc[:].rearrange("p r j c -> p (r j c)")).then_inc(pc_out, 16)
            sp.wait_ge(pc_out, 16)

        @block.gpsimd
        def _(pool):
            for b in range(3):
                zero_pads(pool, u[:, b], pads)
            pool.memset(keep[:], 1.0).then_inc(pads, 1)
            pool.wait_ge(pads, 4)
            k = keep[:].rearrange("p r (c t) -> p r c t", t=RC)
            pool.memset(k[:, 0, :, 0:1], 0.0)
            pool.memset(k[:, 1, :, RC - 1:RC], 0.0).then_inc(pads, 1)

        @block.tensor
        def _(pe):
            pe.wait_ge(par_in, 48)
            with pe.Fori(0, NJ) as j:
                def product(n, name, lhs, rhs, wait):
                    for sem, val in wait:
                        pe.wait_ge(sem, val)
                    for q in range(NSEG):
                        last = pe.matmul(acc[n % 2][:, q, 0:SEG], lhs, rhs[:, q * SEG:(q + 1) * SEG], start=True, stop=True)
                    pe_s.done(last, name)
                done_act = lambda n: (act_s.sem, act_s.at(n, j))
                done_dve = lambda n: (dve_s.sem, dve_s.at(n, j))
                half = (slice(0, 64), slice(64, P))
                product(0, "w0", up[half[0], 0, :], lora[half[0], 0], [(up_in, 16 * (j + 1)), (lora_act, 2), (mixed, 3), done_dve("mv")])
                product(1, "a0", up[half[0], 1, :], lora[half[0], 1], [])
                product(2, "w1", up[half[1], 0, :], lora[half[1], 0], [done_act("sg0")])
                product(3, "a1", up[half[1], 1, :], lora[half[1], 1], [done_act("a0")])
                product(4, "ss", bd[:], t1, [done_act("sq")])
                product(5, "g", up[:, 2, :], lora[:, 2], [done_act("a1")])
                product(6, "bonus", bd[:], t1, [done_dve("bsum"), done_act("root")])

        @block.scalar
        def _(act):
            act.wait_ge(mixed, 3)
            act.activation(lora[:, 0], lora[:, 0], ACT.Tanh).then_inc(lora_act, 1)
            act.activation(lora[:, 2], lora[:, 2], ACT.Sigmoid).then_inc(lora_act, 1)
            act.wait_ge(prep, 3)
            act.sem_inc(g_out, 16)
            act.sem_inc(b_out, 16)
            with act.Fori(0, NJ) as j:
                col = lambda n: par[:, n, bass.ds(j, 1)]
                for n, (name, dst, r) in enumerate((("sg0", sg, 0), ("a0", a, 0), ("sg1", sg, 1), ("a1", a, 1))):
                    act.wait_ge(pe_s.sem, pe_s.at(pe_s.names[n], j))
                    act_s.done(act.activation(seg(dst[:, r]), acc[n % 2][:, :, 0:SEG], ACT.Sigmoid,
                                              bias=col((0, 2, 1, 3)[n])), name)
                act.wait_ge(dve_s.sem, dve_s.at("kk", j))
                act_s.done(act.activation(t1[:], kk[:], ACT.Square), "sq")
                act.wait_ge(pe_s.sem, pe_s.at("ss", j))
                act_s.done(act.activation(seg(t1[:]), acc[0][:, :, 0:SEG], ACT.Sqrt), "root")
                act.wait_ge(pe_s.sem, pe_s.at("g", j))
                act.wait_ge(g_out, 16 * (j + 1))
                act_s.done(act.activation(seg(g[:]), acc[1][:, :, 0:SEG], ACT.Copy), "g")
                for r in range(2):
                    act.wait_ge(dve_s.sem, dve_s.at(f"D{r}", j))
                    if r:
                        act.wait_ge(dve_s.sem, dve_s.at("z0", j))
                    act_s.done(act.activation(pt[:, 0], ls[:, r], ACT.Exp, scale=-DECAY), f"p{r}")
                    act_s.done(act.activation(pt[:, 1], ls[:, r], ACT.Exp, scale=DECAY), f"i{r}")
                    act_s.done(act.activation(pt[:, 2], sg[:, r], ACT.Exp, scale=-DECAY), f"q{r}")

        @block.vector
        def _(dve):
            link = Chain(dve, link_s)

            def mix(out, ub, col, name=None, step=None):
                lo = PAD_C
                link(dve.tensor_tensor(sm[:, lo:lo + W], ub[:, lo - 1:lo - 1 + W], ub[:, lo + 1:lo + 1 + W], ALU.add))
                link(dve.tensor_scalar(sm[:, lo:lo + W], sm[:, lo:lo + W], col(hmu), None, ALU.mult))
                dve.scalar_tensor_tensor(out[:, 0:TC], ub[:, PAD_C:PAD_C + TC], col(omu), sm[:, PAD_C:PAD_C + TC], ALU.mult, ALU.add)
                return dve.scalar_tensor_tensor(out[:, TC:T], ub[:, PAD_S:PAD_S + TS], col(omu), sm[:, PAD_S:PAD_S + TS],
                                                ALU.mult, ALU.add)
            dve.wait_ge(par_in, 48)
            dve.wait_ge(pads, 5)
            dve.tensor_scalar(hmu[:], mu[:], 0.5, None, ALU.mult).then_inc(prep, 1)
            dve.tensor_scalar(omu[:], mu[:], -1.0, 1.0, ALU.mult, ALU.add).then_inc(prep, 1)
            dve.tensor_scalar(oka[:], par[:, 5], -1.0, 1.0, ALU.mult, ALU.add).then_inc(prep, 1)
            dve.wait_ge(prep, 3)
            dve.wait_ge(u0_in, 96)
            for b in range(3):
                mix(lora[:, b], u[:, b], lambda p, b=b: p[:, F_WD + b:F_WD + b + 1]).then_inc(mixed, 1)
                dve.wait_ge(mixed, b + 1)
            start = link.n
            PER = 2 * 3
            link.per = PER
            dve.sem_inc(o_out, 80)
            with dve.Fori(0, NJ) as j:
                link.turn(j, start)
                at = lambda n: dve.wait_ge(dve_s.sem, dve_s.at(n, j))
                act_at = lambda n: dve.wait_ge(act_s.sem, act_s.at(n, j))
                done = dve_s.done
                col = lambda n: par[:, n, bass.ds(j, 1)]
                r_, k_, v_ = m[:, 0], m[:, 1], m[:, 2]
                dve.wait_ge(u_in, 96 * (j + 1))
                dve.wait_ge(o_out, 160 * j + 80)
                for b, name in enumerate(("mr", "mk", "mv")):
                    done(mix(m[:, b], u[:, b], lambda p, b=b: p[:, bass.ds(NJ * b + j, 1)]), name)
                    at(name)
                link.end()
                done(dve.tensor_scalar(kk[:], k_, col(4), None, ALU.mult), "kk")
                act_at("root")
                done(dve.tensor_scalar(t1[:], t1[:], 1e-12, None, ALU.max), "rec")
                at("rec")
                dve.reciprocal(t1[:], t1[:]).then_inc(mixed, 1)
                dve.wait_ge(mixed, j + 4)
                done(dve.tensor_tensor(kk[:], kk[:], t1[:], ALU.mult), "kkn")
                for r in range(2):
                    act_at(f"a{r}")
                    done(dve.tensor_scalar(kd[:, r], a[:, r], col(5), oka[:, bass.ds(j, 1)], ALU.mult, ALU.add), f"km{r}")
                    at(f"km{r}")
                    done(dve.tensor_tensor(kd[:, r], kd[:, r], k_, ALU.mult), f"kd{r}")
                at("kd1")
                dve.tensor_tensor(sm[:, 0:T], kd[:, 0], kd[:, 1], ALU.add).then_inc(bv_s, 1)
                dve.wait_ge(bv_s, 2 * j + 1)
                dve.tensor_tensor(sm[:, 0:T], sm[:, 0:T], r_, ALU.mult).then_inc(bv_s, 1)
                dve.wait_ge(bv_s, 2 * j + 2)
                at("kkn")
                done(dve.tensor_scalar(t1[:], sm[:, 0:T], col(6), None, ALU.mult), "bsum")
                for r in range(2):
                    done(dve.tensor_tensor(a[:, r], a[:, r], kk[:], ALU.mult), f"b{r}")
                for r in range(2):
                    back = slice(None, None, -1) if r else slice(None)
                    done(dve.tensor_tensor_scan(ls[:, r][:, back], keep[:, r][:, back], sg[:, r][:, back], 0.0, ALU.mult, ALU.add), f"L{r}")
                for r in range(2):
                    at(f"L{r}")
                    done(dve.tensor_tensor(sg[:, r], ls[:, r], sg[:, r], ALU.subtract), f"D{r}")
                for r in range(2):
                    act_at(f"q{r}")
                    end = pt[:, 0].rearrange("p (c t) -> p c t", t=RC)[:, :, 0 if r else RC - 1]
                    done(dve.tensor_copy(pc[:, r, bass.ds(j, 1), :].rearrange("p o c -> p (o c)"), end), f"pc{r}")
                    dve.wait_ge(o_out, 160 * j + 80 * (r + 1))
                    done(dve.tensor_tensor(o[:, 3], r_, pt[:, 0], ALU.mult), f"r{r}")
                    done(dve.scalar_tensor_tensor(o[:, 0], kk[:], -1.0, pt[:, 2], ALU.mult, ALU.mult), f"x{r}")
                    at(f"b{r}")
                    done(dve.tensor_tensor(o[:, 1], a[:, r], pt[:, 1], ALU.mult), f"y{r}")
                    done(dve.tensor_tensor(o[:, 2], kd[:, r], pt[:, 1], ALU.mult), f"z{r}")
                dve.wait_ge(pe_s.sem, pe_s.at("bonus", j))
                dve.wait_ge(b_out, 16 * (j + 1))
                done(dve.tensor_tensor(seg(bv[:]), acc[0][:, :, 0:SEG], seg(v_), ALU.mult), "bv")
                at("bv")


PRODUCTS = [
    ("T", "dve", ""), ("Tt", "dve", ""), ("Bt", "dve", ""), ("A2", "dve", ""),
    ("W2", "dve", "T Tt"), ("bT", "act", ""), ("X2", "act", "W2 Tt"), ("Y2", "act", "W2 Tt"),
    ("W4", "dve", "X2"), ("kT", "act", ""), ("X4", "act", "W4 Y2"), ("Y4", "act", "W4 Y2"),
    ("W8", "dve", "X4"), ("vT", "act", ""), ("X8", "act", "W8 Y4"), ("Y8", "act", "W8 Y4"),
    ("W16", "dve", "X8"), ("X16", "act", "W16 Y8"), ("Y16", "act", "W16 Y8"),
    ("W32", "dve", "X16"), ("R", "dve", "Bt vT -S"), ("Y32", "act", "W32 Y16"), 
    ("U", "dve", "R Y32"), ("Yo", "act", "U A2 vT -S"), ("S", "dve", "U bT kT vT"),
]
NAMES = [p[0] for p in PRODUCTS]
TAKER = {p[0]: p[1] for p in PRODUCTS}
NP_ = len(PRODUCTS)


def taken(name):
    return [n for n in NAMES if TAKER[n] == TAKER[name]].index(name) + 1


TAKEN = {e: sum(t == e for t in TAKER.values()) for e in ("dve", "act")}


def rwkv_recurrence(nc, d):
    with ExitStack() as stack:
        s = Scope(nc, stack, "rr")
        ident = s.sb("ident", [P, P])
        masks = s.sb("masks", [P, 2, 9, P])
        pc = s.sb("pc", [P, 2, NJ_A, T // RC])
        S = s.sb("S", [P, 2, 4, P])
        Stmp = s.sb("Stmp", [P, 2, 4, P])
        bdt = s.sb("bdt", [P, 2, 4, 2, 4, P])
        rt = s.sb("rt", [P, 2, 2, 4, RC])
        names = "X1 Y1 Tt Bt A2 bT kT vT W X Y R U"
        buf = {n: s.sb(n, [P, 2, 4, P]) for n in names.split()}
        yo = s.sb("yo", [P, 2, 2, 4, RC])
        sio = s.sb("sio", [P, 2, 4, P])
        pre = s.sb("pre", [P, 2, 2, 4, P])
        const_in, zeroed = s.sem("const_in"), s.sem("zeroed")
        W_MASK = {"W2": 0, "W4": 1, "W8": 2, "W16": 3, "W32": 4}
        M_STRICT, M_INCL, M_ONE, M_ONET = 5, 6, 7, 8
        rep = lambda ap, n=4: ap.unsqueeze(1).broadcast_to([P, n, ap.shape[-1]])

        def run(tag, chunk0, n_chunks):
            pairs = n_chunks // 2
            with ExitStack() as inner:
                q = Scope(nc, inner, tag)
                bank = [[q.ps(f"bank{g}{i}") for i in range(4)] for g in range(2)]
                slot_in = [q.sem(f"slot_in{i}") for i in range(2)]
                product = [q.sem(f"product{g}") for g in range(2)]
                took = {e: [q.sem(f"{e}_took{g}") for g in range(2)] for e in ("dve", "act")}
                y_out = [q.sem(f"y_out{i}") for i in range(2)]
                s_sum = q.sem("s_sum")
                masked = [q.sem(f"masked{g}") for g in range(2)]
                block = inner.enter_context(nc.Block())

                def pairs_loop(eng, body):
                    if pairs == 1:
                        body(0)
                    else:
                        with eng.Fori(0, pairs) as i:
                            body(i)

                def bank_of(slot, k):
                    return (k + NP_ * slot) % 4

                def in_bank_before(slot, k):
                    for back in range(1, 2 * NP_):
                        kk, sl, ago = k - back, slot, 0
                        while kk < 0:
                            kk, sl, ago = kk + NP_, 1 - sl, ago + 1
                        if bank_of(sl, kk) == bank_of(slot, k):
                            return NAMES[kk], ago

                def wait_taken(eng, g, n, name, ago=0):
                    e = TAKER[name]
                    eng.wait_ge(took[e][g], TAKEN[e] * (n + 1 - ago) + taken(name))

                def chunk(g, n):
                    return chunk0 + n if g == 0 else n * -1 + (chunk0 + n_chunks - 1)

                @block.sync
                def _(sp):
                    def load(n, slot):
                        for g in range(2):
                            t0 = bass.ds(chunk(g, n) * RC, RC)
                            for h in range(2):
                                hs = slice(64 * h, 64 * h + 64)
                                for ar in range(4):
                                    sp.dma_start(bdt[hs, slot, ar, g, :, hs],
                                                 d["RW"][ar, g].rearrange("(j p) t -> p j t", p=P)[hs, :, t0]
                                                 ).then_inc(slot_in[slot], 16)
                            sp.dma_start(rt[:, slot, g], d["RT"][g].rearrange("(j p) t -> p j t", p=P)[:, :, t0]
                                         ).then_inc(slot_in[slot], 16)
                    for slot in range(2):
                        load(slot, slot)
                    if pairs > 1:
                        with sp.Fori(1, pairs) as i:
                            for slot in range(2):
                                for g in range(2):
                                    sp.wait_ge(product[g], NP_ * (2 * (i - 1) + slot + 1))
                                load(2 * i + slot, slot)

                @block.tensor
                def _(pe):
                    def step(i, slot):
                        n = 2 * i + slot
                        pe.wait_ge(slot_in[slot], 16 * 18 * (i + 1))
                        for k, (name, _, deps) in enumerate(PRODUCTS):
                            for g in range(2):
                                need = [(dep.strip("-"), int(dep[0] == "-")) for dep in deps.split()] + [in_bank_before(slot, k)]
                                for e in ("dve", "act"):
                                    last_of = max((taken(nm) - TAKEN[e] * ago for nm, ago in need if TAKER[nm] == e), default=None)
                                    if last_of is not None:
                                        pe.wait_ge(took[e][g], TAKEN[e] * (n + 1) + last_of)
                                out = bank[g][bank_of(slot, k)]
                                B = lambda nm, c: buf[nm][:, g, c, :]
                                I = lambda ar, c: bdt[:, slot, ar, g, c, :]
                                KKT, BH, KH, V = range(4)
                                m = int(name[1:]) if name[1:].isdigit() else 0
                                first = m == 2
                                x, y = ("X1", "Y1") if first else ("X", "Y")
                                for c in range(4):
                                    o = out[:, c * P:(c + 1) * P]
                                    mm = lambda lhs, rhs, a=True, b=True, o=o: pe.matmul(o, lhs, rhs, start=a, stop=b)
                                    if name == "T":
                                        last = mm(I(KKT, c), I(BH, c))
                                    elif name == "Tt":
                                        last = mm(I(BH, c), I(KKT, c))
                                    elif name == "Bt":
                                        last = mm(I(KH, c), I(KKT, c))
                                    elif name == "A2":
                                        r = rt[:, slot, g, c, :]
                                        pe.matmul(out[:, c * RC:(c + 1) * RC], I(BH, c), r, start=True, stop=True)
                                        last = pe.matmul(out[:, (4 + c) * RC:(5 + c) * RC], I(KH, c), r, start=True, stop=True)
                                    elif name in ("bT", "kT", "vT"):
                                        last = pe.transpose(o, I({"b": BH, "k": KH, "v": V}[name[0]], c), ident[:])
                                    elif name[0] == "W":
                                        last = mm(B("Tt", c), B(x, c))
                                    elif name[0] == "X":
                                        last = mm(B(y, c), B("W", c))
                                    elif name == "Yo":
                                        o = out[:, c * RC:(c + 1) * RC]
                                        a2 = buf["A2"][:, g].rearrange("p c t -> p (c t)")
                                        mm(B("U", c), a2[:, c * RC:(c + 1) * RC], True, False, o)
                                        mm(B("vT", c), a2[:, (4 + c) * RC:(5 + c) * RC], False, False, o)
                                        last = mm(S[:, g, c, :], rt[:, slot, g, c, :], False, True, o)
                                    elif name[0] == "Y":
                                        last = mm(B("W", c), B(y, c))
                                    elif name == "R":
                                        mm(I(KKT, c), S[:, g, c, :], True, False)
                                        last = mm(B("Bt", c), B("vT", c), False, True)
                                    elif name == "U":
                                        last = mm(B("Y", c), B("R", c))
                                    elif name == "S":
                                        mm(B("bT", c), B("U", c), True, False)
                                        last = mm(B("kT", c), B("vT", c), False, True)
                                last.then_inc(product[g], 1)
                    pairs_loop(pe, lambda i: [step(i, slot) for slot in range(2)])

                def wait_product(eng, g, n, name):
                    eng.wait_ge(product[g], NP_ * n + NAMES.index(name) + 1)

                @block.scalar
                def _(act):
                    for g in range(2):
                        act.sem_inc(took["act"][g], TAKEN["act"])

                    def step(i, slot):
                        n = 2 * i + slot
                        for k, name in enumerate(NAMES):
                            if TAKER[name] != "act":
                                continue
                            for g in range(2):
                                wait_product(act, g, n, name)
                                out = bank[g][bank_of(slot, k)]
                                if name == "Yo":
                                    act.wait_ge(y_out[slot], 32 * (i + 1))
                                    act.activation(yo[:, slot, g].rearrange("p c t -> p (c t)"), out[:, 0:4 * RC], ACT.Copy
                                                   ).then_inc(took["act"][g], 1)
                                    wait_taken(act, g, n, "Yo")
                                    act.dma_start(d["YD"][g].rearrange("(j p) t -> p j t", p=P)[:, :, bass.ds(chunk(g, n) * RC, RC)],
                                                  yo[:, slot, g]).then_inc(y_out[slot], 16)
                                else:
                                    dst = buf[name if name[1] == "T" else name[0]]
                                    act.activation(dst[:, g].rearrange("p c t -> p (c t)"), out[:], ACT.Copy
                                                   ).then_inc(took["act"][g], 1)
                    for slot in range(2):
                        act.sem_inc(y_out[slot], 32)
                    pairs_loop(act, lambda i: [step(i, slot) for slot in range(2)])
                    for slot in range(2):
                        act.wait_ge(y_out[slot], 32 * (pairs + 1))

                @block.vector
                def _(dve):
                    for g in range(2):
                        dve.sem_inc(took["dve"][g], TAKEN["dve"])

                    def step(i, slot):
                        n = 2 * i + slot
                        for k, name in enumerate(NAMES):
                            if TAKER[name] != "dve":
                                continue
                            for g in range(2):
                                wait_product(dve, g, n, name)
                                out = bank[g][bank_of(slot, k)]
                                o4 = out[:].rearrange("p (c t) -> p c t", c=4)
                                eye = rep(ident[:])
                                inc = lambda ins: ins.then_inc(took["dve"][g], 1)
                                if name == "T":
                                    dve.tensor_tensor(pre[:, g, 0], o4, rep(masks[:, g, M_ONE]), ALU.mult).then_inc(masked[g], 1)
                                    dve.wait_ge(masked[g], 2 * n + 1)
                                    inc(dve.tensor_tensor(buf["X1"][:, g], pre[:, g, 0], eye, ALU.add))
                                elif name == "Tt":
                                    dve.tensor_tensor(pre[:, g, 0], o4, rep(masks[:, g, M_STRICT]), ALU.mult)
                                    dve.tensor_tensor(pre[:, g, 1], o4, rep(masks[:, g, M_ONET]), ALU.mult).then_inc(masked[g], 1)
                                    dve.wait_ge(masked[g], 2 * n + 2)
                                    dve.tensor_tensor(buf["Tt"][:, g], pre[:, g, 0], eye, ALU.add)
                                    inc(dve.tensor_tensor(buf["Y1"][:, g], pre[:, g, 1], eye, ALU.add))
                                elif name == "Bt":
                                    inc(dve.tensor_tensor(buf["Bt"][:, g], o4, rep(masks[:, g, M_STRICT]), ALU.mult))
                                elif name == "A2":
                                    inc(dve.tensor_tensor(buf["A2"][:, g].rearrange("p c (b t) -> p (c b) t", b=2),
                                                          out[:].rearrange("p (c t) -> p c t", c=8), rep(masks[:, g, M_INCL, 0:RC], 8), ALU.mult))
                                elif name[0] == "W":
                                    inc(dve.tensor_tensor(buf["W"][:, g], o4, rep(masks[:, g, W_MASK[name]]), ALU.mult))
                                elif name in ("R", "U"):
                                    inc(dve.tensor_copy(buf[name][:, g], o4))
                                elif name == "S":
                                    dve.tensor_tensor(Stmp[:, g], o4, S[:, g], ALU.add).then_inc(s_sum, 1)
                                    dve.wait_ge(s_sum, 2 * n + g + 1)
                                    inc(dve.tensor_tensor(S[:, g], Stmp[:, g], pc[:, g, :, bass.ds(chunk(g, n), 1)]
                                                          .broadcast_to([P, 4, P]), ALU.mult))
                    pairs_loop(dve, lambda i: [step(i, slot) for slot in range(2)])

        with ExitStack() as inner:
            block = inner.enter_context(nc.Block())

            @block.sync
            def _(sp):
                sp.dma_start(ident[:], d["ident"]).then_inc(const_in, 16)
                sp.dma_start(masks[:], d["rw_masks"]).then_inc(const_in, 16)
                sp.dma_start(pc[:].rearrange("p r j c -> p (r j c)"), d["PC"]).then_inc(const_in, 16)
                sp.wait_ge(const_in, 48)

            @block.vector
            def _(dve):
                dve.memset(bdt[:], 0.0)
                dve.memset(S[:], 0.0)
                dve.memset(sio[:], 0.0).then_inc(zeroed, 1)
        run("rc", 0, TC // RC)

        with ExitStack() as inner:
            q = Scope(nc, inner, "sw")
            turn = q.ps("turn", [P, 2, 512])
            turned, copied, moved, fin_in = q.sem("turned"), q.sem("copied"), q.sem("moved"), q.sem("fin_in")
            block = inner.enter_context(nc.Block())
            ext = lambda ap, h: ap[:, h::2].rearrange("r j v k -> v (r j) k")

            @block.tensor
            def _(pe):
                for c in range(8):
                    last = pe.transpose(turn[:, c // 4, c % 4 * P:(c % 4 + 1) * P], S[:, c // 4, c % 4, :], ident[:])
                last.then_inc(turned, 1)
                pe.wait_ge(fin_in, 32)
                for c in range(8):
                    last = pe.transpose(turn[:, c // 4, c % 4 * P:(c % 4 + 1) * P], sio[:, c // 4, c % 4, :], ident[:])
                last.then_inc(turned, 1)

            @block.scalar
            def _(act):
                t4 = turn[:].rearrange("p g (c t) -> p g c t", c=4)
                act.wait_ge(turned, 1)
                act.activation(sio[:], t4, ACT.Copy).then_inc(copied, 1)
                act.wait_ge(copied, 1)
                for h in range(2):
                    hs = slice(64 * h, 64 * h + 64)
                    act.dma_start(ext(d["new_rwkv"], h), sio[hs, :, :, hs].rearrange("p g c t -> p (g c) t")).then_inc(moved, 16)
                act.wait_ge(moved, 32)
                for h in range(2):
                    hs = slice(64 * h, 64 * h + 64)
                    act.dma_start(sio[hs, :, :, hs].rearrange("p g c t -> p (g c) t"), ext(d["rw_s0"], h)).then_inc(fin_in, 16)
                act.wait_ge(turned, 2)
                act.activation(S[:], t4, ACT.Copy).then_inc(copied, 1)
        run("rs", TC // RC, TS // RC)


def rwkv_output(nc, d):
    NJ = NJ_A
    with ExitStack() as stack:
        s = Scope(nc, stack, "ro")
        par = s.sb("par", [P, 2, NJ])
        bdm = s.sb("bdm", [P, P])
        epsc = s.sb("epsc", [P, 1])
        y = s.sb("y", [P, 4, T])
        c = s.sb("c", [P, T])
        sq = s.sb("sq", [P, T])
        rs = s.sb("rs", [P, T])
        o = s.sb("o", [P, T])
        acc = [s.ps(f"acc{i}", [P, NSEG, 512]) for i in range(2)]
        par_in, eps_set, y_in, y_out = s.sem("par_in"), s.sem("eps_set"), s.sem("y_in"), s.sem("y_out")
        pe_s = Steps(s.sem("pe_s"), "mean var")
        act_s = Steps(s.sem("act_s"), "sq root")
        dve_s = Steps(s.sem("dve_s"), "sum cent inv norm aff bonus out")
        block = stack.enter_context(nc.Block())
        seg = lambda ap: ap.rearrange("p (q c) -> p q c", q=NSEG)

        @block.sync
        def _(sp):
            sp.dma_start(par[:], d["rw_gn"]).then_inc(par_in, 16)
            sp.dma_start(bdm[:], d["bd_mean"]).then_inc(par_in, 16)

            def load(j):
                rows = bass.ds(j * P, P)
                for n, src in enumerate((d["YD"][0], d["YD"][1], d["BONUS"], d["GATE"])):
                    sp.dma_start(y[:, n], src[rows, :]).then_inc(y_in, 16)

            def store(j):
                sp.wait_ge(dve_s.sem, dve_s.at("out", j))
                sp.dma_start(d["YT"][bass.ds(j * P, P), :], o[:]).then_inc(y_out, 16)
            sp.sem_inc(y_out, 16)
            load(0)
            with sp.Fori(1, NJ) as j:
                store(j - 1)
                load(j)
            store(NJ - 1)
            sp.wait_ge(y_out, 16 * (NJ + 1))

        @block.gpsimd
        def _(pool):
            pool.memset(epsc[:], GN_EPS).then_inc(eps_set, 1)

        @block.tensor
        def _(pe):
            pe.wait_ge(par_in, 32)
            with pe.Fori(0, NJ) as j:
                for n, (src, name) in enumerate(((y[:, 0], "mean"), (sq, "var"))):
                    if n:
                        pe.wait_ge(act_s.sem, act_s.at("sq", j))
                    else:
                        pe.wait_ge(dve_s.sem, dve_s.at("sum", j))
                    for q in range(NSEG):
                        last = pe.matmul(acc[n][:, q, 0:SEG], bdm[:], src[:, q * SEG:(q + 1) * SEG], start=True, stop=True)
                    pe_s.done(last, name)

        @block.scalar
        def _(act):
            act.wait_ge(eps_set, 1)
            with act.Fori(0, NJ) as j:
                act.wait_ge(dve_s.sem, dve_s.at("cent", j))
                act_s.done(act.activation(sq[:], c[:], ACT.Square), "sq")
                act.wait_ge(pe_s.sem, pe_s.at("var", j))
                act_s.done(act.activation(seg(rs[:]), acc[1][:, :, 0:SEG], ACT.Sqrt, bias=epsc[:, 0:1]), "root")

        @block.vector
        def _(dve):
            with dve.Fori(0, NJ) as j:
                at = lambda n: dve.wait_ge(dve_s.sem, dve_s.at(n, j))
                done = dve_s.done
                dve.wait_ge(y_in, 64 * (j + 1))
                done(dve.tensor_tensor(y[:, 0], y[:, 0], y[:, 1], ALU.add), "sum")
                dve.wait_ge(pe_s.sem, pe_s.at("mean", j))
                done(dve.tensor_tensor(seg(c[:]), seg(y[:, 0]), acc[0][:, :, 0:SEG], ALU.subtract), "cent")
                dve.wait_ge(act_s.sem, act_s.at("root", j))
                done(dve.reciprocal(rs[:], rs[:]), "inv")
                at("inv")
                done(dve.tensor_tensor(c[:], c[:], rs[:], ALU.mult), "norm")
                at("norm")
                done(dve.tensor_scalar(c[:], c[:], par[:, 0, bass.ds(j, 1)], par[:, 1, bass.ds(j, 1)], ALU.mult, ALU.add), "aff")
                at("aff")
                done(dve.tensor_tensor(c[:], c[:], y[:, 2], ALU.add), "bonus")
                at("bonus")
                dve.wait_ge(y_out, 16 * (j + 1))
                done(dve.tensor_tensor(o[:], c[:], y[:, 3], ALU.mult), "out")


def output_projection(nc, d):
    with ExitStack() as stack:
        s = Scope(nc, stack, "op")
        w = s.sb("w", [P, KT, D])
        gt, sc, sh, lg, lb = (s.sb(n, [P, D]) for n in ("gt", "sc", "sh", "lg", "lb"))
        yT = s.sb("yT", [P, 2, KT, P])
        x = s.sb("x", [P, D])
        a = s.sb("a", [P, D])
        stats = s.sb("stats", [P, 4, 6])
        mv = s.sb("mv", [P, 2])
        rstd = s.sb("rstd", [P, 1])
        epsc = s.sb("epsc", [P, 1])
        acc = [s.ps(f"acc{i}", [P, 4, 512]) for i in range(2)]
        w_in = [s.sem(f"w_in{k}") for k in range(4)]
        ln_in, row_in, x_in, eps_set = s.sem("ln_in"), s.sem("row_in"), s.sem("x_in"), s.sem("eps_set")
        y_in = [s.sem(f"y_in{i}") for i in range(2)]
        x1_out, h2_out = s.sem("x1_out"), s.sem("h2_out")
        product, root = s.sem("product"), s.sem("root")
        scale1, stats_in = s.sem("scale1"), s.sem("stats_in")
        dve_s = Steps(s.sem("dve_s"), "gate res st0 st1 st2 st3 aggr inv norm g x1 hs h2")
        block = stack.enter_context(nc.Block())
        slot_of = lambda t: t % 2

        @block.sync
        def _(sp):
            def load_y(t, slot):
                sp.dma_start(yT[:, slot], d["YT"].rearrange("(k p) t -> p k t", p=P)[:, :, bass.ds(t * P, P)]).then_inc(y_in[slot], 16)

            def load_rows(c):
                for dst, seg in ((gt, 2), (sc, 4), (sh, 3)):
                    sp.dma_start(dst[:], d["MOD"][c, seg * D:(seg + 1) * D].partition_broadcast(P)).then_inc(row_in, 16)

            def load_x(t):
                sp.dma_start(x[:], d["X0"][bass.ds(t * P, P), :]).then_inc(x_in, 16)
            load_y(0, 0)
            for q in range(4):
                sp.dma_start(w[:, :, q * 512:(q + 1) * 512], d["w_out"].rearrange("(k p) n -> p k n", p=P)[:, :, q * 512:(q + 1) * 512]
                             ).then_inc(w_in[q], 16)
            load_rows(0)
            load_x(0)
            for dst, name in ((lg, "ln1_g"), (lb, "ln1_b")):
                sp.dma_start(dst[:], d[name].partition_broadcast(P)).then_inc(ln_in, 16)
            load_y(1, 1)

            def tile(t, slot, more_y, rows):
                if more_y:
                    sp.wait_ge(product, t + 1)
                    load_y(t + 2, slot)
                sp.wait_ge(dve_s.sem, dve_s.at("x1", t))
                sp.dma_start(d["X1"][bass.ds(t * P, P), :], a[:]).then_inc(x1_out, 16)
                sp.wait_ge(dve_s.sem, dve_s.at("h2", t))
                sp.dma_start(d["H2"][bass.ds(t * P, P), :], x[:]).then_inc(h2_out, 16)
                if rows:
                    load_rows(1)
                sp.wait_ge(h2_out, 16 * (t + 1))
            tile(0, 0, True, True)
            load_x(1)
            with sp.Fori(0, (NT - 3) // 2) as i:
                for b in range(2):
                    t = 2 * i + 1 + b
                    tile(t, (1 + b) % 2, True, False)
                    load_x(t + 1)
            for t in range(NT - 2, NT):
                tile(t, t % 2, False, False)
                if t + 1 < NT:
                    load_x(t + 1)
            sp.wait_ge(x1_out, 16 * NT)

        @block.gpsimd
        def _(pool):
            pool.memset(epsc[:], LN_EPS).then_inc(eps_set, 1)

        @block.tensor
        def _(pe):
            def one(wait_y, slot, bank_free, first):
                wait_y()
                bank_free()
                for q in range(4):
                    if first:
                        pe.wait_ge(w_in[q], 16)
                    for k in range(KT):
                        last = pe.matmul(acc[slot][:, q, :], yT[:, slot, k, :], w[:, k, q * 512:(q + 1) * 512],
                                         start=k == 0, stop=k == KT - 1)
                last.then_inc(product, 1)
            one(lambda: pe.wait_ge(y_in[0], 16), 0, lambda: None, True)
            one(lambda: pe.wait_ge(y_in[1], 16), 1, lambda: None, False)
            with pe.Fori(0, (NT - 3) // 2) as i:
                for b in range(2):
                    t = 2 * i + 2 + b
                    one(lambda: pe.wait_ge(y_in[b], 16 * (i + 2)), b, lambda: pe.wait_ge(dve_s.sem, dve_s.at("gate", t - 2)), False)
            one(lambda: pe.wait_ge(y_in[0], 16 * ((NT + 1) // 2)), 0, lambda: pe.wait_ge(dve_s.sem, dve_s.at("gate", NT - 3)), False)

        @block.scalar
        def _(act):
            act.wait_ge(eps_set, 1)
            with act.Fori(0, NT) as t:
                act.wait_ge(dve_s.sem, dve_s.at("aggr", t))
                act.activation(rstd[:], mv[:, 1:2], ACT.Sqrt, bias=epsc[:, 0:1]).then_inc(root, 1)

        @block.vector
        def _(dve):
            def tile(t, slot, rows):
                at = lambda n: dve.wait_ge(dve_s.sem, dve_s.at(n, t))
                done = dve_s.done
                if rows is not None:
                    dve.wait_ge(row_in, 48 * (rows + 1))
                    dve.tensor_scalar(sc[:], sc[:], 1.0, None, ALU.add).then_inc(scale1, 1)
                    dve.wait_ge(scale1, rows + 1)
                dve.wait_ge(product, t + 1)
                if not isinstance(t, int) or t:
                    dve.wait_ge(x1_out, 16 * t)
                done(dve.tensor_tensor(a[:].rearrange("p (q c) -> p q c", q=4), acc[slot][:], gt[:].rearrange("p (q c) -> p q c", q=4),
                                       ALU.mult), "gate")
                at("gate")
                dve.wait_ge(x_in, 16 * (t + 1))
                done(dve.scalar_tensor_tensor(a[:], x[:], ALPHA, a[:], ALU.mult, ALU.add), "res")
                at("res")
                for q in range(4):
                    done(dve.bn_stats(stats[:, q, :], a[:, q * 512:(q + 1) * 512]), f"st{q}")
                at("st3")
                dve.sem_inc(stats_in, 1)
                done(dve.bn_aggr(mv[:], stats[:].rearrange("p q s -> p (q s)")), "aggr")
                dve.wait_ge(root, t + 1)
                done(dve.reciprocal(rstd[:], rstd[:]), "inv")
                at("inv")
                done(dve.tensor_scalar(a[:], a[:], mv[:, 0:1], rstd[:, 0:1], ALU.subtract, ALU.mult), "norm")
                at("norm")
                dve.wait_ge(ln_in, 32)
                done(dve.tensor_tensor(a[:], a[:], lg[:], ALU.mult), "g")
                at("g")
                done(dve.tensor_tensor(a[:], a[:], lb[:], ALU.add), "x1")
                at("x1")
                done(dve.tensor_tensor(x[:], a[:], sc[:], ALU.mult), "hs")
                at("hs")
                done(dve.tensor_tensor(x[:], x[:], sh[:], ALU.add), "h2")
                at("h2")
            tile(0, 0, 0)
            tile(1, 1, 1)
            with dve.Fori(0, (NT - 3) // 2) as i:
                for b in range(2):
                    tile(2 * i + 2 + b, b, None)
            tile(NT - 1, 0, None)


def routing(nc, d, keep):
    idx_s, idx_c, gate_s, gate_c = keep
    with ExitStack() as stack:
        s = Scope(nc, stack, "rt")
        ident = s.sb("ident", [P, P])
        rw = s.sb("rw", [P, KT, E])
        h = s.sb("h", [P, D])
        hT = s.sb("hT", [P, KT, P])
        lg = s.sb("lg", [P, E])
        nmax = s.sb("nmax", [P, 1])
        ssum = s.sb("ssum", [P, 1])
        aff = s.sb("aff", [P, E])
        affT = s.sb("affT", [E, T])
        vals = s.sb("vals", [E, P + E])
        idx = s.sb("idx", [E, P + E], U32)
        idxf = s.sb("idxf", [E, P + E])
        zero = s.sb("zero", [P, D])
        tb = [s.ps(f"tb{i}") for i in range(4)]
        lp, ap = s.ps("lp"), s.ps("ap")
        const_in, h_in, zeroed, cleared = s.sem("const_in"), s.sem("h_in"), s.sem("zeroed"), s.sem("cleared")
        pe_s = Steps(s.sem("pe_s"), "t0 t1 t2 t3 logit affT")
        act_s = Steps(s.sem("act_s"), "c0 c2 exp")
        dve_s = Steps(s.sem("dve_s"), "c1 c3 max rec aff affT")
        picked, chosen, turned = s.sem("picked"), s.sem("chosen"), s.sem("turned")
        block = stack.enter_context(nc.Block())

        @block.sync
        def _(sp):
            sp.dma_start(h[:], d["H2"][0:P, :]).then_inc(h_in, 16)
            sp.dma_start(ident[:], d["ident"]).then_inc(const_in, 16)
            sp.dma_start(rw[:], d["router_w"].rearrange("(k p) e -> p k e", p=P)).then_inc(const_in, 16)
            with sp.Fori(1, NT) as t:
                sp.wait_ge(pe_s.sem, pe_s.at("t3", t - 1))
                sp.dma_start(h[:], d["H2"][bass.ds(t * P, P), :]).then_inc(h_in, 16)
            sp.wait_ge(zeroed, 1)
            for t in range(NT):
                sp.dma_start(d["ACC"][t * P:(t + 1) * P, :], zero[:]).then_inc(cleared, 16)
            sp.wait_ge(cleared, 16 * NT)

        @block.gpsimd
        def _(pool):
            pool.memset(zero[:], 0.0).then_inc(zeroed, 1)

        @block.tensor
        def _(pe):
            pe.wait_ge(const_in, 32)
            with pe.Fori(0, NT) as t:
                pe.wait_ge(h_in, 16 * (t + 1))
                for q in range(4):
                    for b in range(4):
                        k = 4 * q + b
                        last = pe.transpose(tb[q][:, b * P:(b + 1) * P], h[:, k * P:(k + 1) * P], ident[:])
                    pe_s.done(last, f"t{q}")
                pe.wait_ge(act_s.sem, act_s.at("c2", t))
                pe.wait_ge(dve_s.sem, dve_s.at("c3", t))
                for k in range(KT):
                    last = pe.matmul(lp[:, 0:E], hT[:, k, :], rw[:, k, :], start=k == 0, stop=k == KT - 1)
                pe_s.done(last, "logit")
                pe.wait_ge(dve_s.sem, dve_s.at("aff", t))
                pe_s.done(pe.transpose(ap[0:E, 0:P], aff[:], ident[:]), "affT")
            pe.wait_ge(chosen, 1)
            pe.transpose(tb[0][:, 0:E], idxf[:, 0:P], ident[0:E, 0:E])
            pe.transpose(tb[0][:, E:2 * E], vals[:, 0:P], ident[0:E, 0:E])
            pe.transpose(tb[0][0:E, 2 * E:3 * E], idxf[:, P:P + E], ident[0:E, 0:E])
            pe.transpose(tb[0][0:E, 3 * E:4 * E], vals[:, P:P + E], ident[0:E, 0:E]).then_inc(turned, 1)

        @block.scalar
        def _(act):
            with act.Fori(0, NT) as t:
                for q in (0, 2):
                    act.wait_ge(pe_s.sem, pe_s.at(f"t{q}", t))
                    act_s.done(act.activation(hT[:, 4 * q:4 * q + 4, :].rearrange("p k t -> p (k t)"), tb[q][:], ACT.Copy), f"c{q}")
                act.wait_ge(dve_s.sem, dve_s.at("max", t))
                act_s.done(act.activation(lg[:], lp[:, 0:E], ACT.Exp, bias=nmax[:, 0:1], accum_out=ssum[:, 0:1]), "exp")

        @block.vector
        def _(dve):
            with dve.Fori(0, NT) as t:
                at = lambda n: dve.wait_ge(dve_s.sem, dve_s.at(n, t))
                for q in (1, 3):
                    dve.wait_ge(pe_s.sem, pe_s.at(f"t{q}", t))
                    dve_s.done(dve.tensor_copy(hT[:, 4 * q:4 * q + 4, :].rearrange("p k t -> p (k t)"), tb[q][:]), f"c{q}")
                dve.wait_ge(pe_s.sem, pe_s.at("logit", t))
                dve_s.done(dve.tensor_reduce(nmax[:], lp[:, 0:E], AX.X, ALU.max, negate=True), "max")
                dve.wait_ge(act_s.sem, act_s.at("exp", t))
                dve_s.done(dve.reciprocal(ssum[:], ssum[:]), "rec")
                at("rec")
                dve_s.done(dve.tensor_scalar(aff[:], lg[:], ssum[:, 0:1], None, ALU.mult), "aff")
                dve.wait_ge(pe_s.sem, pe_s.at("affT", t))
                dve_s.done(dve.tensor_copy(affT[:, bass.ds(t * P, P)], ap[0:E, 0:P]), "affT")
            link = Chain(dve, picked)
            dve.wait_ge(dve_s.sem, dve_s.at("affT", NT - 1))
            for rounds, lo, n, at_col in ((CAP_S // 8, TC, TS, 0), (CAP_C // 8, 0, TC, P)):
                cur = affT[:, lo:lo + n]
                for r in range(rounds):
                    c8 = slice(at_col + 8 * r, at_col + 8 * r + 8)
                    link(dve.max(vals[:, c8], cur))
                    link(dve.max_index(idx[:, c8], vals[:, c8], cur))
                    link(dve.match_replace(cur, vals[:, c8], cur, -1.0))
            link(dve.tensor_copy(idxf[:], idx[:]))
            dve.tensor_scalar(idxf[:, 0:P], idxf[:, 0:P], float(TC), None, ALU.add).then_inc(chosen, 1)
            dve.wait_ge(turned, 1)
            dve.tensor_copy(idx_s[:, 0:E], tb[0][:, 0:E])
            dve.tensor_copy(gate_s[:, 0:E], tb[0][:, E:2 * E])
            dve.tensor_copy(idx_c[:, 0:E], tb[0][0:E, 2 * E:3 * E])
            dve.tensor_copy(gate_c[:, 0:E], tb[0][0:E, 3 * E:4 * E])
            dve.tensor_copy(idx_s[:, E:E + 1], tb[0][:, 0:1])
            dve.tensor_copy(idx_c[:, E:E + 1], tb[0][0:E, 2 * E:2 * E + 1]).then_inc(chosen, 1)


def experts(nc, d, keep):
    idx_s, idx_c, gate_s, gate_c = keep
    RING, NF = 12, FE // P
    GU, SLABS = KT, KT + NF
    ROUNDS = SLABS // RING
    C = CAP
    TPB = 3
    with ExitStack() as stack:
        s = Scope(nc, stack, "ex")
        ident = s.sb("ident", [P, P])
        ring = s.sb("ring", [P, RING, D])
        xs, xc = s.sb("xs", [P, D]), s.sb("xc", [E, D])
        xT = s.sb("xT", [P, KT, C])
        sg = s.sb("sg", [P, NF, C])
        at_ = s.sb("act", [P, NF, C])
        yT = s.sb("yT", [P, KT, C])
        ys, yc = s.sb("ys", [P, D]), s.sb("yc", [E, D])
        gi_s, gi_c = s.sb("gi_s", [P, 1], I32), s.sb("gi_c", [E, 1], I32)
        si_s, si_c = s.sb("si_s", [P, 1], I32), s.sb("si_c", [E, 1], I32)
        gt_s, gt_c = s.sb("gt_s", [P, 1]), s.sb("gt_c", [E, 1])
        bank = [s.ps(f"bank{i}") for i in range(8)]
        tb = bank[6:8]
        ident_in = s.sem("ident_in")
        slab_in = [s.sem(f"slab_in{i}") for i in range(RING)]
        slab_used = s.sem("slab_used")
        gathered, scattered, x_turned, y_turned = s.sem("gathered"), s.sem("scattered"), s.sem("x_turned"), s.sem("y_turned")
        gu_done, down_done = s.sem("gu_done"), s.sem("down_done")
        x_act, x_dve = s.sem("x_act"), s.sem("x_dve")
        silu, acted = s.sem("silu"), s.sem("acted")
        yT_act, yT_dve = s.sem("yT_act"), s.sem("yT_dve")
        y_act, y_dve = s.sem("y_act"), s.sem("y_dve")
        gidx, sidx, drained, begun = (s.sem(n) for n in ("gidx", "sidx", "drained", "begun"))
        block = stack.enter_context(nc.Block())
        XG = -(-KT // TPB)
        YG = 8
        tiles = lambda b, n: range(TPB * b, min(TPB * b + TPB, n))

        @block.sync
        def _(sp):
            sp.dma_start(ident[:], d["ident"]).then_inc(ident_in, 16)

            def load(e, k):
                slot = k % RING
                if k < GU:
                    for n, name in enumerate(("w_gate", "w_up")):
                        sp.dma_start(ring[:, slot, n * FE:(n + 1) * FE], d[name][bass.ds(e * D + k * P, P), :]).then_inc(slab_in[slot], 16)
                else:
                    for n in range(2):
                        sp.dma_start(ring[:, slot, n * FE:(n + 1) * FE],
                                     d["w_down"][bass.ds(e * FE + (k - GU) * P, P), n * FE:(n + 1) * FE]).then_inc(slab_in[slot], 16)
            for k in range(RING):
                load(0, k)

            def refill(e, k):
                if k == GU - 1:
                    sp.wait_ge(gu_done, e * 6 + 6)
                elif k == SLABS - 1:
                    sp.wait_ge(down_done, e * 6 + 6)
                else:
                    sp.wait_ge(slab_used, e * (SLABS - 2) + k - (k >= GU) + 1)
                if k + RING < SLABS:
                    load(e, k + RING)
                else:
                    load(e + 1, k + RING - SLABS)
            with sp.Fori(0, E - 1) as e:
                for k in range(SLABS):
                    refill(e, k)
            for k in range(SLABS - RING):
                refill(E - 1, k)

        @block.gpsimd
        def _(pool):
            def gather(e):
                pool.wait_ge(gidx, e + 1)
                pool.sem_inc(begun, 1)
                for dst, src in ((xs, gi_s), (xc, gi_c)):
                    pool.indirect_dma_start(out=dst[:], out_offset=None, in_=d["H2"],
                                            in_offset=bass.IndirectOffsetOnAxis(ap=src[:, 0:1], axis=0)).then_inc(gathered, 16)
            pool.sem_inc(drained, 1)
            gather(0)
            with pool.Fori(0, E) as e:
                gather(e + 1)
                pool.wait_ge(sidx, e + 1)
                pool.wait_ge(y_act, (e + 1) * YG // 2)
                pool.wait_ge(y_dve, (e + 1) * YG // 2)
                pool.sem_inc(begun, 1)
                for src, ix in ((ys, si_s), (yc, si_c)):
                    pool.indirect_dma_start(out=d["ACC"], out_offset=bass.IndirectOffsetOnAxis(ap=ix[:, 0:1], axis=0),
                                            in_=src[:], in_offset=None, compute_op=ALU.add).then_inc(scattered, 16)
                pool.wait_ge(scattered, 32 * (e + 1))
                pool.sem_inc(drained, 1)

        @block.tensor
        def _(pe):
            pe.wait_ge(ident_in, 16)

            def turn_x(e):
                pe.wait_ge(gathered, 32 * (e + 1))
                for i in range(XG):
                    if i >= 2:
                        pe.wait_ge(x_act if i % 2 == 0 else x_dve, e * XG // 2 + i // 2)
                    for n, k in enumerate(tiles(i, KT)):
                        pe.transpose(tb[i % 2][:, n * C:n * C + P], xs[:, k * P:(k + 1) * P], ident[:])
                        last = pe.transpose(tb[i % 2][:, n * C + P:(n + 1) * C], xc[:, k * P:(k + 1) * P], ident[0:E, 0:E])
                    last.then_inc(x_turned, 1)

            def slab(e, k):
                pe.wait_ge(slab_in[k % RING], (e * ROUNDS + k // RING + 1) * 32)
            turn_x(0)
            with pe.Fori(0, E) as e:
                pe.wait_ge(x_act, (e + 1) * XG // 2)
                pe.wait_ge(x_dve, (e + 1) * XG // 2)
                pe.wait_ge(yT_act, e * 3 + 3)
                pe.wait_ge(yT_dve, e * 3 + 3)
                for k in range(GU):
                    slab(e, k)
                    for h in range(2):
                        for f in range(NF):
                            b, n = 3 * h + f // TPB, f % TPB
                            last = pe.matmul(bank[b][:, n * C:(n + 1) * C], ring[:, k % RING, h * FE + f * P:h * FE + (f + 1) * P],
                                             xT[:, k, :], start=k == 0 and n == 0, stop=k == GU - 1, skip_group_check=True)
                            if k == GU - 1 and (n == TPB - 1 or f == NF - 1):
                                last.then_inc(gu_done, 1)
                    if k < GU - 1:
                        last.then_inc(slab_used, 1)
                turn_x(e + 1)
                pe.wait_ge(acted, (e + 1) * 3)
                for f in range(NF):
                    slab(e, GU + f)
                    for t in range(KT):
                        b, n = t // TPB, t % TPB
                        last = pe.matmul(bank[b][:, n * C:(n + 1) * C], ring[:, (GU + f) % RING, t * P:(t + 1) * P],
                                         at_[:, f, :], start=f == 0 and n == 0, stop=f == NF - 1, skip_group_check=True)
                        if f == NF - 1 and (n == TPB - 1 or t == KT - 1):
                            last.then_inc(down_done, 1)
                    if f < NF - 1:
                        last.then_inc(slab_used, 1)
                for i in range(YG):
                    if i < 2:
                        pe.wait_ge(x_act if i == 0 else x_dve, (e + 2) * XG // 2)
                    else:
                        pe.wait_ge(y_act if i % 2 == 0 else y_dve, e * YG // 2 + i // 2)
                    pe.wait_ge(yT_act, e * 3 + 6)
                    pe.wait_ge(yT_dve, e * 3 + 6)
                    g = i // 2
                    for n in range(4):
                        k = 4 * g + n
                        if i % 2 == 0:
                            last = pe.transpose(tb[0][:, n * P:(n + 1) * P], yT[:, k, 0:P], ident[:])
                        else:
                            last = pe.transpose(tb[1][0:E, n * P:(n + 1) * P], yT[:, k, P:C], ident[:])
                    last.then_inc(y_turned, 1)

        @block.scalar
        def _(act):
            act.sem_inc(yT_act, 3)

            def copy_x(e):
                for i in range(0, XG, 2):
                    act.wait_ge(x_turned, e * XG + i + 1)
                    k = tiles(i, KT)
                    act.activation(xT[:, k[0]:k[-1] + 1, :].rearrange("p k c -> p (k c)"), tb[0][:, 0:len(k) * C], ACT.Copy).then_inc(x_act, 1)
            copy_x(0)
            with act.Fori(0, E) as e:
                for b in range(3):
                    act.wait_ge(gu_done, e * 6 + b + 1)
                    f = tiles(b, NF)
                    act.activation(sg[:, f[0]:f[-1] + 1, :].rearrange("p f c -> p (f c)"), bank[b][:, 0:len(f) * C], ACT.Silu).then_inc(silu, 1)
                copy_x(e + 1)
                for b in range(0, 6, 2):
                    act.wait_ge(down_done, e * 6 + b + 1)
                    k = tiles(b, KT)
                    act.activation(yT[:, k[0]:k[-1] + 1, :].rearrange("p k c -> p (k c)"), bank[b][:, 0:len(k) * C], ACT.Copy).then_inc(yT_act, 1)
                act.wait_ge(sidx, e + 1)
                for g in range(YG // 2):
                    act.wait_ge(y_turned, e * YG + 2 * g + 1)
                    act.activation(ys[:, g * 512:(g + 1) * 512], tb[0][:], ACT.Copy, scale=gt_s[:, 0:1]).then_inc(y_act, 1)

        @block.vector
        def _(dve):
            dve.sem_inc(yT_dve, 3)

            def rows(dst, src, e, n=None):
                return dve.tensor_copy(dst[:], src[:, bass.ds(e, 1)])

            def copy_x(e):
                for i in range(1, XG, 2):
                    dve.wait_ge(x_turned, e * XG + i + 1)
                    k = tiles(i, KT)
                    dve.tensor_copy(xT[:, k[0]:k[-1] + 1, :].rearrange("p k c -> p (k c)"), tb[1][:, 0:len(k) * C]).then_inc(x_dve, 1)
            rows(gi_s, idx_s, 0)
            rows(gi_c, idx_c, 0).then_inc(gidx, 1)
            copy_x(0)
            with dve.Fori(0, E) as e:
                dve.wait_ge(gathered, 32 * (e + 1))
                dve.wait_ge(x_turned, (e + 1) * XG)
                rows(gi_s, idx_s, e + 1)
                rows(gi_c, idx_c, e + 1).then_inc(gidx, 1)
                for b in range(3):
                    dve.wait_ge(silu, e * 3 + b + 1)
                    dve.wait_ge(gu_done, e * 6 + 3 + b + 1)
                    f = tiles(b, NF)
                    flat = lambda x: x[:, f[0]:f[-1] + 1, :].rearrange("p f c -> p (f c)")
                    dve.tensor_tensor(flat(at_), bank[3 + b][:, 0:len(f) * C], flat(sg), ALU.mult).then_inc(acted, 1)
                copy_x(e + 1)
                for b in range(1, 6, 2):
                    dve.wait_ge(down_done, e * 6 + b + 1)
                    k = tiles(b, KT)
                    dve.tensor_copy(yT[:, k[0]:k[-1] + 1, :].rearrange("p k c -> p (k c)"), bank[b][:, 0:len(k) * C]).then_inc(yT_dve, 1)
                dve.wait_ge(drained, e + 1)
                rows(si_s, idx_s, e)
                rows(si_c, idx_c, e)
                rows(gt_s, gate_s, e)
                rows(gt_c, gate_c, e).then_inc(sidx, 1)
                dve.wait_ge(sidx, e + 1)
                for g in range(YG // 2):
                    dve.wait_ge(y_turned, e * YG + 2 * g + 2)
                    dve.tensor_scalar(yc[:, g * 512:(g + 1) * 512], tb[1][0:E, :], gt_c[:, 0:1], None, ALU.mult).then_inc(y_dve, 1)


def final_norm(nc, d):
    with ExitStack() as stack:
        s = Scope(nc, stack, "fn")
        gt, lg, lb = s.sb("gt", [P, 2, D]), s.sb("lg", [P, D]), s.sb("lb", [P, D])
        x, m = s.sb("x", [P, 3, D]), s.sb("m", [P, 3, D])
        stats, mv, rstd, epsc = s.sb("stats", [P, 4, 6]), s.sb("mv", [P, 2, 2]), s.sb("rstd", [P, 2]), s.sb("epsc", [P, 1])
        ln_in, eps_set = s.sem("ln_in"), s.sem("eps_set")
        x_in = [s.sem(f"x_in{i}") for i in range(3)]
        out = [s.sem(f"out{i}") for i in range(3)]
        root = s.sem("root")
        dve_s = Steps(s.sem("dve_s"), "res st0 st1 st2 st3 aggr inv norm b")
        pool_s = Steps(s.sem("pool_s"), "gate")
        block = stack.enter_context(nc.Block())

        @block.sync
        def _(sp):
            for t in range(NT):
                if t == 1:
                    for c in range(2):
                        sp.dma_start(gt[:, c], d["MOD"][c, 5 * D:6 * D].partition_broadcast(P)).then_inc(ln_in, 16)
                    for dst, name in ((lg, "ln2_g"), (lb, "ln2_b")):
                        sp.dma_start(dst[:], d[name].partition_broadcast(P)).then_inc(ln_in, 16)
                if t >= 3:
                    sp.wait_ge(out[t % 3], 16 * (t // 3))
                for dst, src in ((x, "X1"), (m, "ACC")):
                    sp.dma_start(dst[:, t % 3], d[src][t * P:(t + 1) * P, :]).then_inc(x_in[t % 3], 16)

        @block.gpsimd
        def _(pool):
            pool.memset(epsc[:], LN_EPS).then_inc(eps_set, 1)
            pool.wait_ge(ln_in, 64)
            for t in range(NT):
                pool.wait_ge(x_in[t % 3], 32 * (t // 3 + 1))
                pool_s.done(pool.tensor_tensor(m[:, t % 3], m[:, t % 3], gt[:, min(t, 1)], ALU.mult), "gate")

        @block.scalar
        def _(act):
            act.wait_ge(eps_set, 1)
            for t in range(NT):
                act.wait_ge(dve_s.sem, dve_s.at("aggr", t))
                act.activation(rstd[:, t % 2:t % 2 + 1], mv[:, t % 2, 1:2], ACT.Sqrt, bias=epsc[:, 0:1]).then_inc(root, 1)
                act.wait_ge(dve_s.sem, dve_s.at("b", t))
                dst = d["y_prompt"] if t == 0 else d["y_sample"][(t - 1) * P:t * P, :]
                act.dma_start(dst, x[:, t % 3]).then_inc(out[t % 3], 16)
            for i in range(3):
                act.wait_ge(out[i], 16 * (NT // 3))

        @block.vector
        def _(dve):
            for t in range(NT):
                at = lambda n: dve.wait_ge(dve_s.sem, dve_s.at(n, t))
                done = dve_s.done
                a = x[:, t % 3]
                dve.wait_ge(pool_s.sem, pool_s.at("gate", t))
                done(dve.scalar_tensor_tensor(a, a, ALPHA, m[:, t % 3], ALU.mult, ALU.add), "res")
                at("res")
                for q in range(4):
                    done(dve.bn_stats(stats[:, q, :], a[:, q * 512:(q + 1) * 512]), f"st{q}")
                at("st3")
                done(dve.bn_aggr(mv[:, t % 2], stats[:].rearrange("p q s -> p (q s)")), "aggr")
                dve.wait_ge(root, t + 1)
                r = rstd[:, t % 2:t % 2 + 1]
                done(dve.reciprocal(r, r), "inv")
                at("inv")
                done(dve.scalar_tensor_tensor(a, a, mv[:, t % 2, 0:1], lg[:], ALU.subtract, ALU.mult), "norm")
                at("norm")
                done(dve.scalar_tensor_tensor(a, a, r, lb[:], ALU.mult, ALU.add), "b")


def moe(nc, d):
    with ExitStack() as stack:
        s = Scope(nc, stack, "moe")
        keep = (s.sb("idx_s", [P, E + 1], I32), s.sb("idx_c", [E, E + 1], I32), s.sb("gate_s", [P, E]), s.sb("gate_c", [E, E]))
        routing(nc, d, keep)
        experts(nc, d, keep)


def rwkv_masks():
    t, u = np.arange(64)[:, None], np.arange(64)[None, :]
    level = lambda m: (t // (2 * m) == u // (2 * m)) & (t % (2 * m) >= m) & (u % (2 * m) < m)
    forward = [level(m) | (t == u) for m in (2, 4, 8, 16, 32)] + [t < u, t <= u, level(1), level(1).T]
    both = [forward, [m.T for m in forward]]
    out = np.stack([np.stack([np.kron(np.eye(2), m) for m in ms]) for ms in both]).astype(np.float32)
    for r, ms in enumerate(both):
        out[r, 6, :, 0:64] = np.concatenate([ms[6], ms[6]], 0)
    return out.transpose(2, 0, 1, 3)


def layout(**a):
    col = lambda v: np.ascontiguousarray(v.reshape(-1, P).T)
    quarter = D // 4
    omega = 1.0 / (10000.0 ** (np.arange(quarter, dtype=np.float32) / quarter)).astype(np.float32)
    ids = np.arange(TS)
    ang = [(ids // 64).astype(np.float32)[:, None] * omega[None], (ids % 64).astype(np.float32)[:, None] * omega[None]]
    out = {
        "x": np.concatenate([a["x_prompt"][0], a["x_sample"][0]], 0),
        "pos": np.concatenate([f(v) for v in ang for f in (np.sin, np.cos)], -1).astype(np.float32),
        "cond": np.stack([col(a["c_ctx"]), col(a["c"][0])], -1),
        "b_mod": np.stack([a["b_mod"][0]] * 2),
        "w_mod": a["w_mod"][0],
        "w_in": a["w_in"][0],
        "lru_par": np.stack([col(v) for v in [*a["lru_conv_w"][0], a["lru_conv_b"][0], *a["lru_lambda"][0]]], 1),
        "lru_bias": np.stack([col(v) for v in [*a["lru_b_a"][0], *a["lru_b_x"][0]]], 1),
        "lru_h0": np.stack([col(v) for v in a["state_rglru"][0, 0]], 1),
        "lru_gates": np.concatenate([a["lru_w_a"][0], a["lru_w_x"][0]], 0),
        "ssd_par": np.stack([col(v) for v in [*a["ssd_conv_w"][0], a["ssd_conv_b"][0]]], 1),
        "ssd_dt": np.stack([a["ssd_dt_bias"][0].reshape(-1), a["ssd_a_log"][0].reshape(-1)], 1),
        "ssd_d": np.broadcast_to(a["ssd_d"][0], (P, 12)),
        "ssd_norm_g": col(a["ssd_norm_g"][0]),
        "ssd_s0": a["state_ssd"][0, 0].reshape(-1, P),
        "ones": np.ones((P, P), np.float32),
        "upper": np.triu(np.ones((P, P), np.float32)),
        "lower": np.tril(np.ones((P, P), np.float32)),
        "rw_mu": col(a["rwkv_mu"][0]),
        "rw_par": np.stack([col(v) for v in [*a["rwkv_w0"][0], *a["rwkv_a0"][0], a["rwkv_k_k"][0], a["rwkv_k_a"][0],
                                             a["rwkv_r_k"][0]]], 1),
        "rw_up": np.stack([a["rwkv_w_up"][0].reshape(P, -1), a["rwkv_a_up"][0].reshape(P, -1), a["rwkv_g_up"][0]], 1),
        "rw_gn": np.stack([col(a["rwkv_gn_g"][0]), col(a["rwkv_gn_b"][0])], 1),
        "rw_s0": a["state_rwkv"][0, 0],
        "rw_masks": rwkv_masks(),
        "bd_ones": np.kron(np.eye(2, dtype=np.float32), np.ones((64, 64), np.float32)),
        "bd_mean": np.kron(np.eye(2, dtype=np.float32), np.full((64, 64), 1 / 64, np.float32)),
        "w_out": a["w_out"][0],
        "ln1_g": a["ln1_g"][0], "ln1_b": a["ln1_b"][0], "ln2_g": a["ln2_g"][0], "ln2_b": a["ln2_b"][0],
        "router_w": a["router_w"][0],
        "w_gate": a["exp_w_gate"].reshape(E * D, FE),
        "w_up": a["exp_w_up"].reshape(E * D, FE),
        "w_down": a["exp_w_down"].reshape(E * FE, D),
        "ident": np.eye(P, dtype=np.float32),
    }
    return {n: np.ascontiguousarray(v) for n, v in out.items()}


SCRATCH = {
    "MOD": [2, 6 * D],
    "X0": [T, D],
    "FEAT": [FT * P, T],
    "YT": [D, T],
    "RW": [4, 2, 512, T],
    "RT": [2, 512, T],
    "PC": [P, 2 * 4 * (T // 64)],
    "GATE": [512, T],
    "BONUS": [512, T],
    "YD": [2, 512, T],
    "X1": [T, D],
    "H2": [T, D],
    "ACC": [T, D],
    "XBC": [SSD_CH, T],
    "ROWS": [48, T],
}
OUTS = {"y_prompt": [TC, D], "y_sample": [TS, D], "new_rwkv": [2, 8, 64, 64], "new_ssd": [2 * 12 * 64, 128], "new_rglru": [2 * (D_B // P), P]}


STAGES = (modulation, projection, rwkv_features, rwkv_recurrence, rwkv_output, rglru, ssd, output_projection, moe, final_norm)


def program(nc, d):
    for stage in STAGES:
        stage(nc, d)


def kernel(**inputs):
    import concourse.bacc as bacc
    from concourse.bass_utils import run_bass_kernel_spmd

    nc = bacc.Bacc("TRN2", target_bir_lowering=False, num_devices=1)
    arrays, d = {}, {}
    for name, a in layout(**{n: np.asarray(v) for n, v in inputs.items()}).items():
        arrays[f"in_{name}"] = a
        d[name] = nc.dram_tensor(f"in_{name}", a.shape, mybir.dt.from_np(a.dtype), kind="ExternalInput").ap()
    for name, shape in SCRATCH.items():
        d[name] = nc.dram_tensor(f"scratch_{name}", shape, F32, kind="Internal").ap()
    for name, shape in OUTS.items():
        d[name] = nc.dram_tensor(f"out_{name}", shape, F32, kind="ExternalOutput").ap()
    program(nc, d)
    got = run_bass_kernel_spmd(nc, [arrays], core_ids=[0]).results[0]
    out = lambda name, shape: got[f"out_{name}"].reshape(shape)
    return (out("y_prompt", (1, TC, D)), out("y_sample", (1, TS, D)), out("new_rwkv", (1, 1, 2, 8, 64, 64)),
            out("new_rglru", (1, 1, 2, D_B)), out("new_ssd", (1, 1, 2, 12, 64, 128)))
```

```python
from contextlib import ExitStack

import numpy as np

import concourse.bass as bass
from concourse import mybir

F32 = mybir.dt.float32
F32R = mybir.dt.float32r
I32 = mybir.dt.int32
U32 = mybir.dt.uint32
ALU = mybir.AluOpType
ACT = mybir.ActivationFunctionType
AX = mybir.AxisListType

P = 128
D = 2048
KT = D // P
TC, TS = 128, 1024
T = TC + TS
NT = T // P
SEG = 384
NSEG = T // SEG
HD = 64
D_A, D_B, D_C = 512, 768, 768
A_FEAT = 3 * D_A + 4 * 64 + 128
SSD_CH = D_C + 512
N_IN = A_FEAT + 2 * D_B + D_C + SSD_CH + 24
FT = -(-N_IN // P)
F_R, F_K, F_V, F_WD, F_AD, F_GD = 0, 4, 8, 12, 13, 14
F_XB = A_FEAT // P
F_GB = F_XB + D_B // P
F_Z = F_GB + D_B // P
F_XBC = F_Z + D_C // P
F_DT = F_XBC + SSD_CH // P
DECAY = 0.606531
ALPHA = 2.0 ** 0.25
LN_EPS = 1e-5
GN_EPS = 64e-5
E = 16
FE = 1024
CAP_S, CAP_C = 2 * TS // E, 2 * TC // E
CAP = CAP_S + CAP_C
PAD_C, PAD_S = 2, 2 + TC + 1 + 2
TP = PAD_S + TS + 1


class Scope:

    def __init__(self, nc, stack, name):
        self.nc, self.stack, self.name, self.sems = nc, stack, name, []
        stack.callback(self.clear)

    def sb(self, name, shape, dt=F32):
        return self.stack.enter_context(self.nc.sbuf_tensor(f"{self.name}_{name}", shape, dt))

    def ps(self, name, shape=(P, 512)):
        return self.stack.enter_context(self.nc.psum_tensor(f"{self.name}_{name}", list(shape), F32))

    def sem(self, name):
        self.sems.append(self.nc.alloc_semaphore(f"{self.name}_{name}"))
        return self.sems[-1]

    def clear(self):
        if self.sems:
            self.nc.clear_and_free_semaphores(self.sems)
            self.nc.all_engine_barrier()


class Chain:

    def __init__(self, eng, sem, per=0):
        self.eng, self.sem, self.n, self.per, self.base = eng, sem, 0, per, 0

    def turn(self, i, start=0):
        self.n, self.base = 0, start + i * self.per

    def __call__(self, ins):
        self.n += 1
        ins.then_inc(self.sem, 1)
        self.eng.wait_ge(self.sem, self.base + self.n)

    def end(self):
        assert self.n == self.per, (self.n, self.per)


MW = 512
QUAD = 4
MOD_FIRST = 2 * D // MW


def modulation(nc, d):
    RING, CW = 4, MW
    n_col = MOD_FIRST
    w = d["w_mod"].rearrange("(t p) n -> p t n", p=P)
    with ExitStack() as stack:
        s = Scope(nc, stack, "mod")
        cond = s.sb("cond", [P, KT, 2])
        sil = s.sb("silu", [P, KT, 2])
        slab = s.sb("slab", [P, RING, KT, CW])
        bias = s.sb("bias", [2, 2 * D])
        row = s.sb("row", [2, RING, CW])
        acc = [s.ps(f"acc{i}") for i in range(RING)]
        cond_in, silu_done, bias_in = s.sem("cond_in"), s.sem("silu_done"), s.sem("bias_in")
        slab_in = [s.sem(f"slab_in{i}") for i in range(RING)]
        row_out = [s.sem(f"row_out{i}") for i in range(RING)]
        product, summed, biased = s.sem("product"), s.sem("summed"), s.sem("biased")
        block = stack.enter_context(nc.Block())

        @block.sync
        def _(sp):
            sp.dma_start(cond[:], d["cond"]).then_inc(cond_in, 16)
            sp.dma_start(bias[:], d["b_mod"][:, 0:2 * D]).then_inc(bias_in, 16)
            for r in range(RING):
                sp.dma_start(slab[:, r], w[:, :, r * CW:(r + 1) * CW]).then_inc(slab_in[r], 16)
            with sp.Fori(1, n_col // RING) as i:
                for r in range(RING):
                    sp.wait_ge(product, RING * (i - 1) + r + 1)
                    sp.dma_start(slab[:, r], w[:, :, bass.ds((RING * i + r) * CW, CW)]).then_inc(slab_in[r], 16)

        @block.scalar
        def _(act):
            act.wait_ge(cond_in, 16)
            act.activation(sil[:], cond[:], ACT.Silu).then_inc(silu_done, 1)
            with act.Fori(0, n_col // RING) as i:
                for r in range(RING):
                    act.wait_ge(biased, RING * i + r + 1)
                    act.dma_start(d["MOD"][:, bass.ds((RING * i + r) * CW, CW)], row[:, r]).then_inc(row_out[r], 16)
            for r in range(RING):
                act.wait_ge(row_out[r], 16 * (n_col // RING))

        @block.tensor
        def _(pe):
            pe.wait_ge(silu_done, 1)

            def column(i, r):
                pe.wait_ge(slab_in[r], 16 * (i + 1))
                for t in range(KT):
                    g = t % QUAD
                    last = pe.matmul(acc[r][32 * g:32 * g + 2, :], sil[:, t, :], slab[:, r, t, :], start=t < QUAD,
                                     stop=t >= KT - QUAD, tile_position=(0, 32 * g))
                last.then_inc(product, 1)
            for r in range(RING):
                column(0, r)
            with pe.Fori(1, n_col // RING) as i:
                for r in range(RING):
                    pe.wait_ge(biased, RING * (i - 1) + r + 1)
                    column(i, r)

        @block.vector
        def _(dve):
            dve.wait_ge(bias_in, 16)

            def column(i, r):
                dve.wait_ge(product, RING * i + r + 1)
                dve.tensor_tensor(row[:, r], acc[r][0:2, :], bias[:, bass.ds((RING * i + r) * CW, CW)],
                                  ALU.add).then_inc(summed, 1)
                for g in range(1, QUAD):
                    dve.wait_ge(summed, (QUAD - 1) * (RING * i + r) + g)
                    dve.tensor_tensor(row[:, r], row[:, r], acc[r][32 * g:32 * g + 2, :],
                                      ALU.add).then_inc(summed if g < QUAD - 1 else biased, 1)
            for r in range(RING):
                column(0, r)
            with dve.Fori(1, n_col // RING) as i:
                for r in range(RING):
                    dve.wait_ge(row_out[r], 16 * i)
                    column(i, r)


def projection(nc, d):
    GR = 4 * P
    w = d["w_in"].rearrange("(t p) n -> p t n", p=P)
    with ExitStack() as stack:
        s = Scope(nc, stack, "proj")
        hH = s.sb("hH", [P, KT, T], F32R)
        hL = s.sb("hL", [P, KT, T], F32R)
        raw = s.sb("raw", [P, 2, KT, P])
        raw_in = [s.sem(f"raw_in{i}") for i in range(2)]

        def raw_load(eng, n, slot, m=P):
            eng.dma_start(raw[:, slot, :, 0:m], w[:, :, bass.ds(n * P, m)]).then_inc(raw_in[slot], 16)

        with ExitStack() as inner:
            s1 = Scope(nc, inner, "hid")
            ident = s1.sb("ident", [P, P])
            shift = s1.sb("shift", [P, 2, KT])
            scale = s1.sb("scale", [P, 2, KT])
            x = s1.sb("x", [P, 2, D])
            pos = s1.sb("pos", [P, D])
            h = s1.sb("h", [P, 3, GR])
            rows = s1.sb("rows", [4 * KT, P])
            bank = [s1.ps(f"bank{i}") for i in range(8)]
            mod_in, pos_in, x_sum, ident_in, turned = (s1.sem(n) for n in ("mod_in", "pos_in", "x_sum", "ident_in", "turned"))
            mod_turned, mod_done = s1.sem("mod_turned"), s1.sem("mod_done")
            hidden, high, low = s1.sem("hidden"), s1.sem("high"), s1.sem("low")
            x_out = [s1.sem(f"x_out{i}") for i in range(2)]
            x_in = [s1.sem(f"x_in{i}") for i in range(2)]
            place = lambda buf, n: buf[:, n % 4 * 4:n % 4 * 4 + 4, n // 4 * P:(n // 4 + 1) * P]
            group = lambda n: h[:, n % 3, :].rearrange("p (b t) -> p b t", b=4)
            block = inner.enter_context(nc.Block())

            @block.sync
            def _(sp):
                sp.dma_start(ident[:], d["ident"]).then_inc(ident_in, 16)
                for c in range(2):
                    sp.dma_start(rows[2 * KT * c:2 * KT * (c + 1), :],
                                 d["MOD"][c, 0:2 * D].rearrange("(t p) -> t p", p=P)).then_inc(mod_in, 16)
                for t in range(NT):
                    if t >= 2:
                        sp.wait_ge(turned, 4 * (t - 1))
                        sp.wait_ge(x_out[t % 2], 16 * (t // 2))
                    sp.dma_start(x[:, t % 2], d["x"][t * P:(t + 1) * P, :]).then_inc(x_in[t % 2], 16)
                    if t:
                        if t > 1:
                            sp.wait_ge(x_sum, t - 1)
                        sp.dma_start(pos[:], d["pos"][(t - 1) * P:t * P, :]).then_inc(pos_in, 16)
                for n in range(2):
                    raw_load(sp, n, n)

            @block.tensor
            def _(pe):
                pe.wait_ge(ident_in, 16)
                pe.wait_ge(mod_in, 32)
                pe.transpose(bank[7][:, 0:4 * KT], rows[:], ident[0:4 * KT, 0:4 * KT]).then_inc(mod_turned, 1)
                pe.wait_ge(mod_done, 2)
                for t in range(NT):
                    pe.wait_ge(x_in[t % 2], 16 * (t // 2 + 1))
                    if t:
                        pe.wait_ge(x_sum, t)
                    for q in range(4):
                        n = 4 * t + q
                        if n >= 8:
                            pe.wait_ge(hidden, n - 7)
                        for b in range(4):
                            k = 4 * q + b
                            last = pe.transpose(bank[n % 8][:, b * P:(b + 1) * P], x[:, t % 2, k * P:(k + 1) * P],
                                                ident[:])
                        last.then_inc(turned, 1)

            @block.vector
            def _(dve):
                dve.wait_ge(mod_turned, 1)
                both = bank[7][:, 0:4 * KT].rearrange("p (c s t) -> p c s t", c=2, s=2)
                dve.tensor_copy(shift[:], both[:, :, 0, :]).then_inc(mod_done, 1)
                dve.tensor_scalar(scale[:], both[:, :, 1, :], 1.0, None, ALU.add).then_inc(mod_done, 1)
                dve.wait_ge(mod_done, 2)

                def embed(t):
                    dve.wait_ge(x_in[t % 2], 16 * (t // 2 + 1))
                    dve.wait_ge(pos_in, 16 * t)
                    dve.tensor_tensor(x[:, t % 2], x[:, t % 2], pos[:], ALU.add).then_inc(x_sum, 1)
                for n in range(4 * NT):
                    t, q = n // 4, n % 4
                    c = min(t, 1)
                    if q == 1 and t + 1 < NT:
                        embed(t + 1)
                    dve.wait_ge(turned, n + 1)
                    if n >= 3:
                        dve.wait_ge(low, n - 2)
                    for b in range(4):
                        k = 4 * q + b
                        last = dve.tensor_scalar(h[:, n % 3, b * P:(b + 1) * P], bank[n % 8][:, b * P:(b + 1) * P],
                                                 scale[:, c, k:k + 1], shift[:, c, k:k + 1], ALU.mult, ALU.add)
                    last.then_inc(hidden, 1)

            @block.scalar
            def _(act):
                for n in range(4 * NT):
                    t = n // 4
                    if n % 4 == 0:
                        act.wait_ge(x_in[t % 2], 16 * (t // 2 + 1))
                        if t:
                            act.wait_ge(x_sum, t)
                        act.dma_start(d["X0"][t * P:(t + 1) * P, :], x[:, t % 2]).then_inc(x_out[t % 2], 16)
                    act.wait_ge(hidden, n + 1)
                    act.activation(place(hH, n), group(n), ACT.Copy).then_inc(high, 1)
                for b in range(2):
                    act.wait_ge(x_out[b], 16 * ((NT + 1 - b) // 2))

            @block.gpsimd
            def _(pool):
                for n in range(4 * NT):
                    pool.wait_ge(high, n + 1)
                    pool.tensor_tensor(place(hL, n), group(n), place(hH, n), ALU.subtract).then_inc(low, 1)

        with ExitStack() as inner:
            s2 = Scope(nc, inner, "feat")
            wH = s2.sb("wH", [P, 2, KT, P], F32R)
            wL = s2.sb("wL", [P, 2, KT, P], F32R)
            out = s2.sb("out", [P, 2, T])
            acc = [s2.ps(f"acc{i}", [P, NSEG, 512]) for i in range(2)]
            high, low, tile_done, copied = (s2.sem(n) for n in ("high", "low", "tile_done", "copied"))
            out_done = [s2.sem(f"out_done{i}") for i in range(2)]
            rest = N_IN % P
            pairs = FT // 2 - 1
            block = inner.enter_context(nc.Block())

            @block.sync
            def _(sp):
                def load(n, k, m=P):
                    sp.wait_ge(low, n - 1)
                    raw_load(sp, n, k, m)
                with sp.Fori(1, pairs) as i:
                    for k in range(2):
                        load(2 * i + k, k)
                load(FT - 2, 0)
                load(FT - 1, 1, rest)

            @block.scalar
            def _(act):
                act.sem_inc(tile_done, 2)
                for k in range(2):
                    act.sem_inc(out_done[k], 16)

                def split(i, k, m=P):
                    act.wait_ge(raw_in[k], 16 * (i + 1))
                    act.wait_ge(tile_done, 2 * i + k + 1)
                    act.activation(wH[:, k, :, 0:m], raw[:, k, :, 0:m], ACT.Copy).then_inc(high, 1)

                def store(i, k, m=P):
                    n = 2 * i + k
                    act.wait_ge(tile_done, n + 3)
                    act.wait_ge(out_done[k], 16 * (i + 1))
                    act.activation(out[0:m, k].rearrange("p (g c) -> p g c", g=NSEG), acc[k][0:m, :, 0:SEG],
                                   ACT.Copy).then_inc(copied, 1)
                    act.wait_ge(copied, n + 3)
                    act.dma_start(d["FEAT"][bass.ds(n * P, m), :], out[0:m, k]).then_inc(out_done[k], 16)
                act.sem_inc(copied, 2)
                split(0, 0)
                with act.Fori(0, pairs) as i:
                    split(i, 1)
                    store(i, 0)
                    split(i + 1, 0)
                    store(i, 1)
                split(pairs, 1, rest)
                store(pairs, 0)
                store(pairs, 1, rest)
                for k in range(2):
                    act.wait_ge(out_done[k], 16 * (pairs + 2))

            @block.vector
            def _(dve):
                def split(n, k, m=P):
                    dve.wait_ge(high, n + 1)
                    dve.tensor_tensor(wL[:, k, :, 0:m], raw[:, k, :, 0:m], wH[:, k, :, 0:m], ALU.subtract).then_inc(low, 1)
                with dve.Fori(0, pairs) as i:
                    for k in range(2):
                        split(2 * i + k, k)
                split(FT - 2, 0)
                split(FT - 1, 1, rest)

            @block.tensor
            def _(pe):
                def tile(n, k):
                    pe.wait_ge(low, n + 1)
                    pe.wait_ge(copied, n + 1)
                    for g in range(NSEG):
                        for t in range(KT):
                            cols = slice(g * SEG, (g + 1) * SEG)
                            for j, (a, b) in enumerate(((wH, hH), (wH, hL), (wL, hH))):
                                last = pe.matmul(acc[k][:, g, 0:SEG], a[:, k, t, :], b[:, t, cols],
                                                 start=t == 0 and j == 0, stop=t == KT - 1 and j == 2)
                    last.then_inc(tile_done, 1)
                with pe.Fori(0, pairs) as i:
                    for k in range(2):
                        tile(2 * i + k, k)
                tile(FT - 2, 0)
                tile(FT - 1, 1)


class Steps:

    def __init__(self, sem, names):
        self.sem, self.names, self.k = sem, names.split(), 0

    def at(self, name, i=0):
        return i * len(self.names) + self.names.index(name) + 1

    def done(self, ins, name):
        assert self.names[self.k % len(self.names)] == name, (name, self.k)
        self.k += 1
        ins.then_inc(self.sem, 1)


def padded(ap):
    return ap[:, PAD_C:PAD_C + TC], ap[:, PAD_S:PAD_S + TS]


def zero_pads(eng, ap, sem):
    eng.memset(ap[:, 0:PAD_C], 0.0)
    eng.memset(ap[:, PAD_C + TC:PAD_S], 0.0)
    eng.memset(ap[:, PAD_S + TS:TP], 0.0).then_inc(sem, 1)


def rglru(nc, d):
    NJ = D_B // P
    W = PAD_S + TS - PAD_C
    with ExitStack() as stack:
        s = Scope(nc, stack, "lru")
        par = s.sb("par", [P, 7, NJ])
        bias = s.sb("bias", [P, 4, NJ])
        h0 = s.sb("h0", [P, 2, NJ])
        sp8 = s.sb("sp8", [P, 2, NJ])
        nsp8 = s.sb("nsp8", [P, 2, NJ])
        nsp16 = s.sb("nsp16", [P, 2, NJ])
        tmp = s.sb("tmp", [P, 2, NJ])
        ident = s.sb("ident", [P, P])
        gates = s.sb("gates", [P, 2, 4, P])
        xb = s.sb("xb", [P, 2, TP])
        gb = s.sb("gb", [P, 2, T])
        cv = s.sb("cv", [P, 2, TP])
        xc = s.sb("xc", [P, 2, T])
        rg = s.sb("rg", [P, 2, 2, T])
        ig = s.sb("ig", [P, 2, 2, T])
        av = s.sb("av", [P, 2, 2, T])
        th = s.sb("th", [P, 2, 2, T])
        sq = s.sb("sq", [P, 2, 2, T])
        ge = s.sb("ge", [P, 2, T])
        fin = s.sb("fin", [P, 2, NJ])
        finT = s.sb("finT", [2 * NJ, P])
        acc = [s.ps(f"acc{i}", [P, NSEG, 512]) for i in range(2)]
        PASS, SLOTS, KQ = 5, 5, KT // 4
        LAST = 6 * D // MW - MOD_FIRST - PASS * (NJ // 2 - 1)
        cond = s.sb("cond", [P, KT, 2])
        sil = s.sb("sil", [P, KT, 2])
        wq = s.sb("wq", [P, SLOTS, KQ, MW])
        row = s.sb("row", [2, LAST, MW])
        mod_acc = [s.ps(f"mod_acc{i}") for i in range(2)]
        cond_in, cond_silu, wq_used = (s.sem(n) for n in ("cond_in", "cond_silu", "wq_used"))
        wq_in = [s.sem(f"wq_in{i}") for i in range(SLOTS)]
        row_in, row_out, mod_sum = (s.sem(n) for n in ("row_in", "row_out", "mod_sum"))
        y_made = s.sem("y_made")
        par_in, pads, sp_done = s.sem("par_in"), s.sem("pads"), s.sem("sp_done")
        xb_in, gb_in, gates_in, y_out = ([s.sem(f"{n}{l}") for l in range(2)] for n in ("xb_in", "gb_in", "gates_in", "y_out"))
        fin_turned, fin_copied, fin_out = s.sem("fin_turned"), s.sem("fin_copied"), s.sem("fin_out")
        by_lane = lambda names: " ".join(f"{n}.{l}" for n in names.split() for l in range(2))
        pe_s = Steps(s.sem("pe_s"), by_lane("a0 x0 a1 x1"))
        act_s = Steps(s.sem("act_s"), by_lane("rg0 ig0 rg1 ig1 gelu th0 th1 av0 sq0 av1 sq1 root0 root1"))
        dve_s = Steps(s.sem("dve_s"), by_lane("q0 q1 u0 u1 hc0 hs0 fin0 hc1 hs1 fin1 sum y"))
        conv = Steps(s.sem("conv"), by_lane("c0 c1 c2 c3 xc"))
        pool_s = Steps(s.sem("pool_s"), by_lane("xi0 xi1"))
        block = stack.enter_context(nc.Block())
        gsrc = d["lru_gates"]
        LANES = range(2)

        @block.sync
        def _(sp):
            for dst, name in ((par, "lru_par"), (bias, "lru_bias"), (h0, "lru_h0"), (ident, "ident")):
                sp.dma_start(dst[:], d[name]).then_inc(par_in, 16)
            sp.dma_start(cond[:], d["cond"]).then_inc(cond_in, 16)
            sp.sem_inc(wq_used, SLOTS)
            w = d["w_mod"].rearrange("(t p) n -> p t n", p=P)
            cols = lambda i, n: bass.ds((MOD_FIRST + PASS * i) * MW, n * MW)

            def load_bias(i, n):
                sp.wait_ge(row_out, 16 * (i + 1))
                sp.dma_start(row[:, 0:n].rearrange("r m c -> r (m c)"), d["b_mod"][:, cols(i, n)]).then_inc(row_in, 16)

            def load_slabs(i, lo, hi):
                for m in range(lo, hi):
                    for k in range(4):
                        u = 4 * m + k
                        sp.wait_ge(wq_used, 4 * PASS * i + u + 1)
                        sp.dma_start(wq[:, u % SLOTS], w[:, k * KQ:(k + 1) * KQ, bass.ds((MOD_FIRST + PASS * i + m) * MW, MW)]
                                     ).then_inc(wq_in[u % SLOTS], 16)

            def store_rows(i, n):
                sp.wait_ge(mod_sum, 4 * (PASS * i + n + 1))
                sp.dma_start(d["MOD"][:, cols(i, n)], row[:, 0:n].rearrange("r m c -> r (m c)")).then_inc(row_out, 16)
            sp.sem_inc(row_out, 16)

            def load(i, l):
                j = 2 * i + l
                for dst, off, n in zip(padded(xb[:, l]), (0, TC), (TC, TS)):
                    sp.dma_start(dst, d["FEAT"][bass.ds((F_XB + j) * P, P), off:off + n]).then_inc(xb_in[l], 16)
                sp.dma_start(gb[:, l], d["FEAT"][bass.ds((F_GB + j) * P, P), :]).then_inc(gb_in[l], 16)
                for b in range(2):
                    sp.dma_start(gates[64 * b:64 * b + 64, l, :, 64 * b:64 * b + 64],
                                 gsrc[:, bass.ds(2 * j + b, 1)].rearrange("m o i k -> i (m o) k")).then_inc(gates_in[l], 16)

            def store(i, l):
                sp.wait_ge(dve_s.sem, dve_s.at(f"y.{l}", i))
                sp.dma_start(d["YT"][bass.ds(D_A + (2 * i + l) * P, P), :], cv[:, l, 0:T]).then_inc(y_out[l], 16)
            sp.wait_ge(pads, 3)
            for l in LANES:
                load(0, l)
            load_slabs(0, 0, 1)
            for i in range(NJ // 2):
                more = i < NJ // 2 - 1
                load_bias(i, PASS if more else LAST)
                load_slabs(i, 1, 3)
                if i:
                    for l in LANES:
                        store(i - 1, l)
                if more:
                    for l in LANES:
                        sp.wait_ge(act_s.sem, act_s.at(f"gelu.{l}", i))
                        load(i + 1, l)
                load_slabs(i, 3, PASS if more else LAST)
                if more:
                    load_slabs(i + 1, 0, 1)
                store_rows(i, PASS if more else LAST)
            for l in LANES:
                store(NJ // 2 - 1, l)
            sp.wait_ge(row_out, 16 * (NJ // 2 + 1))
            sp.wait_ge(fin_copied, 1)
            sp.dma_start(d["new_rglru"], finT[:]).then_inc(fin_out, 16)
            sp.wait_ge(fin_out, 16)
            for l in LANES:
                sp.wait_ge(y_out[l], 16 * NJ // 2)

        @block.gpsimd
        def _(pool):
            for l in LANES:
                zero_pads(pool, xb[:, l], pads)
            pool.memset(gates[:], 0.0).then_inc(pads, 1)
            with pool.Fori(0, NJ // 2) as i:
                for r in range(2):
                    for l in LANES:
                        pool.wait_ge(act_s.sem, act_s.at(f"ig{r}.{l}", i))
                        pool.wait_ge(conv.sem, conv.at(f"xc.{l}", i))
                        pool_s.done(pool.tensor_tensor(ig[:, l, r], ig[:, l, r], xc[:, l], ALU.mult), f"xi{r}.{l}")

        @block.tensor
        def _(pe):
            def slab(i, m):
                pe.wait_ge(mod_sum, 4 * (PASS * i + m + (m == 0)))
                for k in range(4):
                    u = 4 * m + k
                    pe.wait_ge(wq_in[u % SLOTS], 16 * (4 * i + u // SLOTS + 1))
                    for g in range(QUAD):
                        last = pe.matmul(mod_acc[m % 2][32 * g:32 * g + 2, :], sil[:, k * KQ + g, :], wq[:, u % SLOTS, g, :],
                                         start=k == 0, stop=k == 3, tile_position=(0, 32 * g))
                    last.then_inc(wq_used, 1)

            def tiles(i, slabs):
                for n, (g, r) in enumerate((("a", 0), ("x", 0), ("a", 1), ("x", 1))):
                    if n < 3:
                        slab(i, n)
                    for l in LANES:
                        if n:
                            pe.wait_ge(act_s.sem, act_s.at(("rg0", "ig0", "rg1")[n - 1] + f".{l}", i))
                        else:
                            pe.wait_ge(gates_in[l], 32 * (i + 1))
                            pe.wait_ge(conv.sem, conv.at(f"xc.{l}", i))
                        for q in range(NSEG):
                            last = pe.matmul(acc[l][:, q, 0:SEG], gates[:, l, (2 if g == "x" else 0) + r, :],
                                             xc[:, l, q * SEG:(q + 1) * SEG], start=True, stop=True)
                        pe_s.done(last, f"{g}{r}.{l}")
                for m in range(3, slabs):
                    slab(i, m)
            pe.wait_ge(cond_silu, 1)
            with pe.Fori(0, NJ // 2 - 1) as i:
                tiles(i, PASS)
            tiles(NJ // 2 - 1, LAST)
            pe.wait_ge(dve_s.sem, dve_s.at("fin1.1", NJ // 2 - 1))
            pe.wait_ge(par_in, 64)
            pe.wait_ge(act_s.sem, act_s.at("ig1.1", NJ // 2 - 1))
            pe.transpose(acc[0][0:2 * NJ, 0, 0:P], fin[:].rearrange("p r j -> p (r j)"), ident[:]).then_inc(fin_turned, 1)

        @block.scalar
        def _(act):
            act.wait_ge(par_in, 64)
            act.activation(tmp[:], par[:, 5:7, :], ACT.Abs).then_inc(sp_done, 1)
            act.wait_ge(sp_done, 1)
            act.activation(tmp[:], tmp[:], ACT.Exp, scale=-1.0).then_inc(sp_done, 1)
            act.wait_ge(sp_done, 2)
            act.activation(tmp[:], tmp[:], ACT.Ln, bias=1.0).then_inc(sp_done, 1)
            act.wait_ge(sp_done, 8)
            act.wait_ge(cond_in, 16)
            act.activation(sil[:], cond[:], ACT.Silu).then_inc(cond_silu, 1)
            act.sem_inc(y_made, 2)
            with act.Fori(0, NJ // 2) as i:
                col = lambda t, n, l: t[:, n, bass.ds(2 * i + l, 1)]
                for n, (g, r, dst) in enumerate((("rg", 0, rg), ("ig", 0, ig), ("rg", 1, rg), ("ig", 1, ig))):
                    for l in LANES:
                        act.wait_ge(pe_s.sem, pe_s.at(pe_s.names[2 * n + l], i))
                        act_s.done(act.activation(dst[:, l, r].rearrange("p (q c) -> p q c", q=NSEG), acc[l][:, :, 0:SEG],
                                                  ACT.Sigmoid, bias=col(bias, (2 if g == "ig" else 0) + r, l)), f"{g}{r}.{l}")
                for l in LANES:
                    act.wait_ge(gb_in[l], 16 * (i + 1))
                    act.wait_ge(y_made, 2 * (i + 1))
                    act_s.done(act.activation(ge[:, l], gb[:, l], ACT.Gelu_apprx_tanh), f"gelu.{l}")
                for r in range(2):
                    for l in LANES:
                        act.wait_ge(act_s.sem, act_s.at(f"rg{r}.{l}", i))
                        act_s.done(act.activation(th[:, l, r], rg[:, l, r], ACT.Tanh, scale=col(sp8, r, l)), f"th{r}.{l}")
                for r in range(2):
                    for l in LANES:
                        act_s.done(act.activation(av[:, l, r], rg[:, l, r], ACT.Exp, scale=col(nsp8, r, l)), f"av{r}.{l}")
                    for l in LANES:
                        act_s.done(act.activation(sq[:, l, r], rg[:, l, r], ACT.Exp, scale=col(nsp16, r, l)), f"sq{r}.{l}")
                for r in range(2):
                    for l in LANES:
                        act.wait_ge(dve_s.sem, dve_s.at(f"q{r}.{l}", i))
                        act_s.done(act.activation(th[:, l, r], th[:, l, r], ACT.Sqrt), f"root{r}.{l}")

        @block.vector
        def _(dve):
            dve.wait_ge(sp_done, 3)
            dve.tensor_scalar(sp8[:], par[:, 5:7, :], -1.0, 0.0, ALU.mult, ALU.max).then_inc(sp_done, 1)
            dve.wait_ge(sp_done, 4)
            dve.tensor_tensor(sp8[:], sp8[:], tmp[:], ALU.add).then_inc(sp_done, 1)
            dve.wait_ge(sp_done, 5)
            dve.tensor_scalar(nsp8[:], sp8[:], -8.0, None, ALU.mult).then_inc(sp_done, 1)
            dve.tensor_scalar(nsp16[:], sp8[:], -16.0, None, ALU.mult).then_inc(sp_done, 1)
            dve.wait_ge(sp_done, 7)
            dve.tensor_scalar(sp8[:], sp8[:], 8.0, None, ALU.mult).then_inc(sp_done, 1)
            dve.wait_ge(sp_done, 8)
            def convolve(i):
                at = lambda n, l: dve.wait_ge(conv.sem, conv.at(f"{n}.{l}", i))
                tap = lambda k, l: par[:, k, bass.ds(2 * i + l, 1)]
                lo = PAD_C
                for l in LANES:
                    dve.wait_ge(xb_in[l], 32 * (i + 1))
                    conv.done(dve.tensor_scalar(cv[:, l, lo:lo + W], xb[:, l, lo - 2:lo - 2 + W], tap(0, l), tap(4, l), ALU.mult, ALU.add),
                              f"c0.{l}")
                for k in (1, 2):
                    for l in LANES:
                        at(f"c{k - 1}", l)
                        conv.done(dve.scalar_tensor_tensor(cv[:, l, lo:lo + W], xb[:, l, lo - 2 + k:lo - 2 + k + W], tap(k, l),
                                                           cv[:, l, lo:lo + W], ALU.mult, ALU.add), f"c{k}.{l}")
                for n, off, w, name in ((PAD_C, 0, TC, "c3"), (PAD_S, TC, TS, "xc")):
                    for l in LANES:
                        at("c2", l)
                        conv.done(dve.scalar_tensor_tensor(xc[:, l, off:off + w], xb[:, l, n + 1:n + 1 + w], tap(3, l), cv[:, l, n:n + w],
                                                           ALU.mult, ALU.add), f"{name}.{l}")

            def row_sum(i, m):
                k = PASS * i + m
                dve.wait_ge(wq_used, 4 * (k + 1) + SLOTS)
                for g in range(QUAD):
                    if g:
                        dve.wait_ge(mod_sum, 4 * (k + 1) + g)
                    dve.tensor_tensor(row[:, m], row[:, m], mod_acc[m % 2][32 * g:32 * g + 2, :], ALU.add).then_inc(mod_sum, 1)

            def tiles(i, more):
                dve.wait_ge(row_in, 16 * (i + 1))
                for m in range(3):
                    row_sum(i, m)
                at = lambda n, l: dve.wait_ge(dve_s.sem, dve_s.at(f"{n}.{l}", i))
                for r in range(2):
                    for l in LANES:
                        dve.wait_ge(act_s.sem, act_s.at(f"sq{r}.{l}", i))
                        dve_s.done(dve.scalar_tensor_tensor(th[:, l, r], sq[:, l, r], 1.0, th[:, l, r], ALU.add, ALU.mult), f"q{r}.{l}")
                for r in range(2):
                    for l in LANES:
                        dve.wait_ge(act_s.sem, act_s.at(f"root{r}.{l}", i))
                        dve.wait_ge(pool_s.sem, pool_s.at(f"xi{r}.{l}", i))
                        dve_s.done(dve.tensor_tensor(th[:, l, r], th[:, l, r], ig[:, l, r], ALU.mult), f"u{r}.{l}")
                wait_stored(i)
                if more:
                    convolve(i + 1)
                row_sum(i, 3)
                for r in range(2):
                    back = slice(None, None, -1) if r else slice(None)
                    for lo, w, init, name in ((0, TC, None, "hc"), (TC, TS, h0, "hs")):
                        for l in LANES:
                            at(f"u{r}", l)
                            cut = lambda b: b[:, l, r, lo:lo + w][:, back]
                            first = 0.0 if init is None else init[:, r, bass.ds(2 * i + l, 1)]
                            dve_s.done(dve.tensor_tensor_scan(cut(sq), cut(av), cut(th), first, ALU.mult, ALU.add), f"{name}{r}.{l}")
                    last = 0 if r else TC - 1
                    for l in LANES:
                        at(f"hc{r}", l)
                        dve_s.done(dve.tensor_copy(fin[:, r, bass.ds(2 * i + l, 1)], sq[:, l, r, last:last + 1]), f"fin{r}.{l}")
                for l in LANES:
                    at("hs1", l)
                    dve_s.done(dve.tensor_tensor(sq[:, l, 0], sq[:, l, 0], sq[:, l, 1], ALU.add), f"sum.{l}")
                for m in range(4, PASS if more else LAST):
                    row_sum(i, m)
                for l in LANES:
                    at("sum", l)
                    dve_s.done(dve.tensor_tensor(cv[:, l, 0:T], sq[:, l, 0], ge[:, l], ALU.mult), f"y.{l}")
                at("y", 1)
                dve.sem_inc(y_made, 2)
            def wait_stored(i):
                if not isinstance(i, int) or i:
                    for l in LANES:
                        dve.wait_ge(y_out[l], 16 * i)
            dve.sem_inc(mod_sum, 4)
            convolve(0)
            tiles(0, True)
            with dve.Fori(1, NJ // 2 - 1) as i:
                tiles(i, True)
            tiles(NJ // 2 - 1, False)
            dve.wait_ge(fin_turned, 1)
            dve.tensor_copy(finT[:], acc[0][0:2 * NJ, 0, 0:P]).then_inc(fin_copied, 1)


def ssd(nc, d):
    NX, NB = D_C // P, 2
    NCH = NX + 2 * NB
    H, HC = 24, 12
    W = PAD_S + TS - PAD_C
    R1 = 32
    HG = HC // 2
    GW = HG * HD
    with ExitStack() as stack:
        s0 = Scope(nc, stack, "ssd")
        ident = s0.sb("ident", [P, P])
        ones = s0.sb("ones", [P, P])
        upper = s0.sb("upper", [P, P])
        lower = s0.sb("lower", [P, P])
        dskip = s0.sb("dskip", [P, HC])
        norm_g = s0.sb("norm_g", [P, NX])
        ytok = s0.sb("ytok", [P, NT, D_C])
        st = s0.sb("st", [P, 2, NT, D_C])
        s_init = s0.sb("s_init", [P, 2, D_C])
        ea = s0.sb("ea", [P, NT, H])
        cdec = s0.sb("cdec", [P, NT, H])
        epsc = s0.sb("epsc", [P, 1])
        const_in = s0.sem("const_in")

        with ExitStack() as inner:
            s = Scope(nc, inner, "pre")
            par = s.sb("par", [P, 5, NCH])
            u = s.sb("u", [P, 2, TP])
            cv = s.sb("cv", [P, TP])
            cv2 = s.sb("cv2", [P, TP])
            xc = s.sb("xc", [P, 2, T])
            xo = s.sb("xo", [P, 2, T])
            dpar = s.sb("dpar", [64, 2])
            dt = s.sb("dt", [64, T])
            e1 = s.sb("e1", [64, T])
            mx = s.sb("mx", [64, T])
            keep = s.sb("keep", [64, T])
            acs = s.sb("acs", [64, T])
            s_raw = s.sb("s_raw", [P, 2 * NX, P])
            turn = s.ps("turn", [P, 2, 512])
            par_in, pads, u_out = s.sem("par_in"), s.sem("pads"), [s.sem(f"u_out{i}") for i in range(2)]
            u_in = [s.sem(f"u_in{i}") for i in range(2)]
            dt_in, dt_abs, dt_done, dt_out = s.sem("dt_in"), s.sem("dt_abs"), s.sem("dt_done"), s.sem("dt_out")
            conv, silu = Steps(s.sem("conv"), "c0 c1 c2 c3 xc"), s.sem("silu")
            raw_in, turned, placed = s.sem("raw_in"), s.sem("turned"), s.sem("placed")
            dt_link = s.sem("dt_link")
            block = inner.enter_context(nc.Block())

            @block.sync
            def _(sp):
                for dst, name in ((par, "ssd_par"), (ident, "ident"), (ones, "ones"), (upper, "upper"), (lower, "lower"),
                                  (dskip, "ssd_d"), (norm_g, "ssd_norm_g")):
                    sp.dma_start(dst[:], d[name]).then_inc(const_in, 16)

                def load(b, j):
                    for dst, off, n in zip(padded(u[:, b]), (0, TC), (TC, TS)):
                        sp.dma_start(dst, d["FEAT"][bass.ds((F_XBC + j) * P, P), off:off + n]).then_inc(u_in[b], 16)
                sp.wait_ge(pads, 4)
                for b in range(2):
                    load(b, b)
                for r in range(2):
                    sp.dma_start(dt[R1 * r:R1 * r + HC, :], d["FEAT"][F_DT * P + HC * r:F_DT * P + HC * (r + 1), :]).then_inc(dt_in, 16)
                    sp.dma_start(dpar[R1 * r:R1 * r + HC, :], d["ssd_dt"][HC * r:HC * (r + 1), :]).then_inc(dt_in, 16)
                sp.dma_start(s_raw[:], d["ssd_s0"].rearrange("(n p) k -> p n k", p=P)).then_inc(raw_in, 16)
                with sp.Fori(1, NCH // 2) as i:
                    for b in range(2):
                        sp.wait_ge(conv.sem, conv.at("xc", 2 * (i - 1) + b))
                        load(b, 2 * i + b)
                sp.wait_ge(dt_done, 1)
                for n, rows in enumerate((acs, dt)):
                    for r in range(2):
                        lo = H * n + HC * r
                        sp.dma_start(d["ROWS"][lo:lo + HC, :], rows[R1 * r:R1 * r + HC, :]).then_inc(dt_out, 16)
                sp.wait_ge(dt_out, 64)

            @block.gpsimd
            def _(pool):
                for b in range(2):
                    zero_pads(pool, u[:, b], pads)
                pool.memset(epsc[:], 1e-5)
                pool.memset(dt[:], 0.0)
                pool.memset(dpar[:], 0.0)
                pool.memset(keep[:], 1.0).then_inc(pads, 1)
                pool.wait_ge(pads, 3)
                k = keep[:].rearrange("p (c t) -> p c t", t=P)
                pool.memset(k[0:32, :, 0:1], 0.0)
                pool.memset(k[32:64, :, P - 1:P], 0.0).then_inc(pads, 1)

            @block.tensor
            def _(pe):
                pe.wait_ge(const_in, 16 * 7)
                pe.wait_ge(raw_in, 16)
                for q in range(3):
                    if q:
                        pe.wait_ge(placed, q)
                    for b in range(4):
                        last = pe.transpose(turn[:, 0, b * P:(b + 1) * P], s_raw[:, 4 * q + b, :], ident[:])
                    last.then_inc(turned, 1)

            @block.scalar
            def _(act):
                act.wait_ge(dt_in, 64)
                act.activation(e1[:], dt[:], ACT.Abs, bias=dpar[:, 0:1]).then_inc(dt_abs, 1)
                act.wait_ge(dt_abs, 1)
                act.activation(e1[:], e1[:], ACT.Exp, scale=-1.0).then_inc(dt_abs, 1)
                act.wait_ge(dt_abs, 2)
                act.activation(e1[:], e1[:], ACT.Ln, bias=1.0).then_inc(dt_abs, 1)
                act.activation(dpar[:, 1:2], dpar[:, 1:2], ACT.Exp).then_inc(dt_abs, 1)
                flat = s_init[:].rearrange("p r c -> p (r c)")
                for q in range(3):
                    act.wait_ge(turned, q + 1)
                    act.activation(flat[:, q * 512:(q + 1) * 512], turn[:, 0, :], ACT.Copy).then_inc(placed, 1)
                act.sem_inc(silu, 2)
                for b in range(2):
                    act.sem_inc(u_out[b], 16)
                with act.Fori(0, NCH // 2) as i:
                    for b in range(2):
                        act.wait_ge(conv.sem, conv.at("xc", 2 * i + b))
                        act.wait_ge(u_out[b], 16 * (i + 1))
                        act.activation(xo[:, b], xc[:, b], ACT.Silu).then_inc(silu, 1)
                        act.wait_ge(silu, 2 * i + b + 3)
                        act.dma_start(d["XBC"][bass.ds((2 * i + b) * P, P), :], xo[:, b]).then_inc(u_out[b], 16)
                for b in range(2):
                    act.wait_ge(u_out[b], 16 * (NCH // 2 + 1))

            @block.vector
            def _(dve):
                link = Chain(dve, dt_link)
                dve.wait_ge(pads, 4)
                dve.wait_ge(dt_in, 64)
                dve.wait_ge(dt_abs, 4)
                link(dve.tensor_scalar(mx[:], dt[:], dpar[:, 0:1], 0.0, ALU.add, ALU.max))
                link(dve.tensor_tensor(dt[:], mx[:], e1[:], ALU.add))
                link(dve.tensor_scalar(mx[:], dt[:], dpar[:, 1:2], -1.0, ALU.mult, ALU.mult))
                dve.tensor_tensor_scan(acs[0:32, :], keep[0:32, :], mx[0:32, :], 0.0, ALU.mult, ALU.add)
                dve.tensor_tensor_scan(acs[32:64, ::-1], keep[32:64, ::-1], mx[32:64, ::-1], 0.0, ALU.mult,
                                       ALU.add).then_inc(dt_done, 1)
                dve.wait_ge(const_in, 16 * 7)
                with dve.Fori(0, NCH // 2) as i:
                    for b in range(2):
                        j = 2 * i + b
                        tap = lambda k: par[:, k, bass.ds(j, 1)]
                        at = lambda n: dve.wait_ge(conv.sem, conv.at(n, j))
                        ub, lo = u[:, b], PAD_C
                        dve.wait_ge(u_in[b], 32 * (i + 1))
                        conv.done(dve.tensor_scalar(cv[:, lo:lo + W], ub[:, lo - 2:lo - 2 + W], tap(0), tap(4), ALU.mult, ALU.add), "c0")
                        at("c0")
                        conv.done(dve.scalar_tensor_tensor(cv2[:, lo:lo + W], ub[:, lo - 1:lo - 1 + W], tap(1), cv[:, lo:lo + W],
                                                           ALU.mult, ALU.add), "c1")
                        at("c1")
                        conv.done(dve.scalar_tensor_tensor(cv[:, lo:lo + W], ub[:, lo:lo + W], tap(2), cv2[:, lo:lo + W],
                                                           ALU.mult, ALU.add), "c2")
                        at("c2")
                        dve.wait_ge(silu, 2 * i + b + 1)
                        for n, off, w, name in ((PAD_C, 0, TC, "c3"), (PAD_S, TC, TS, "xc")):
                            conv.done(dve.scalar_tensor_tensor(xc[:, b, off:off + w], ub[:, n + 1:n + 1 + w], tap(3), cv[:, n:n + w],
                                                               ALU.mult, ALU.add), name)
                        at("xc")

        with ExitStack() as inner:
            s = Scope(nc, inner, "chunk")
            xbc = s.sb("xbc", [P, 2, NCH, P])
            rows = s.sb("rows", [2 * H, 2, P])
            bc = s.sb("bc", [P, 2, H, P])
            lm = s.sb("lm", [P, 2, H, P])
            cols = s.sb("cols", [P, 2, 2 * H])
            g = s.sb("g", [P, 2, 2, NB, P])
            xt = s.sb("xt", [P, 2, D_C])
            bt = s.sb("bt", [P, 2, NB, P])
            dec = s.sb("dec", [P, 2, 2, HC])
            skip = s.sb("skip", [P, 2, D_C])
            xd = s.sb("xd", [P, 2, D_C])
            xe = s.sb("xe", [P, 2, D_C])
            tp = s.ps("tp", [P, 2, 512])
            gp = s.ps("gp")
            yp = s.ps("yp", [P, 2, 512])
            stp = s.ps("stp", [P, 3, 512])
            xbc_in, bc_in = ([s.sem(f"{n}{i}") for i in range(2)] for n in ("xbc_in", "bc_in"))
            pe_f, y_made, st_made = Steps(s.sem("pe_f"), "turn g"), s.sem("y_made"), s.sem("st_made")
            act_f, st_read = Steps(s.sem("act_f"), "xt ea cdf cdb dec L"), s.sem("st_read")
            b_turned = s.sem("b_turned")
            dve_f, dve_b = Steps(s.sem("dve_f"), "cols gf gb sub clamp d0 d1"), Steps(s.sem("dve_b"), "m xd0 xd1 xe0 xe1")
            pool_s, reloads, y_read = Steps(s.sem("pool_s"), "skip"), s.sem("reloads"), s.sem("y_read")
            block = inner.enter_context(nc.Block())
            heads = lambda ap: ap.rearrange("p (h k) -> p h k", h=HC)

            def skewed(first, second, third, eng):
                def turn(c, b):
                    first(c + 1, 1 - b)
                    third(c - 1, 1 - b)
                    second(c, b)
                first(0, 0)
                first(1, 1)
                second(0, 0)
                with eng.Fori(0, NT // 2 - 1) as i:
                    for b in range(2):
                        turn(2 * i + b + 1, 1 - b)
                turn(NT - 2, 1)
                third(NT - 2, 1)
                second(NT - 1, 0)
                third(NT - 1, 0)

            def reused(c):
                return not isinstance(c, int) or c >= 2

            def nothing(c, b):
                pass

            @block.sync
            def _(sp):
                def load(c, b):
                    sp.dma_start(xbc[:, b], d["XBC"].rearrange("(n p) t -> p n t", p=P)[:, :, bass.ds(c * P, P)]).then_inc(xbc_in[b], 16)
                    sp.dma_start(rows[:, b], d["ROWS"][:, bass.ds(c * P, P)]).then_inc(xbc_in[b], 16)

                def load_bc(c, b):
                    sp.dma_start(bc[:, b], d["ROWS"][0:H, bass.ds(c * P, P)].partition_broadcast(P)).then_inc(bc_in[b], 16)

                def reload(c, b):
                    turned, dve_read, act_read = pe_f.at("g", c - 2), dve_f.at("d1", c - 2), act_f.at("cdb", c - 2)
                    sp.wait_ge(pe_f.sem, turned)
                    load(c, b)
                    sp.wait_ge(dve_f.sem, dve_read)
                    sp.sem_inc(reloads, 1)
                    sp.wait_ge(act_f.sem, act_read)
                    load_bc(c, b)
                for b in range(2):
                    load(b, b)
                    load_bc(b, b)
                with sp.Fori(1, NT // 2) as i:
                    for b in range(2):
                        reload(2 * i + b, b)
                reload(NT - 1, 0)

            @block.gpsimd
            def _(pool):
                pool.sem_inc(y_read, 2)

                def make_skip(c, b):
                    pool.wait_ge(act_f.sem, act_f.at("xt", c))
                    pool.wait_ge(y_read, c + 1)
                    pool_s.done(pool.tensor_tensor(heads(skip[:, b]), heads(xt[:, b]), dskip[:].unsqueeze(2).broadcast_to([P, HC, HD]),
                                                   ALU.mult), "skip")
                with pool.Fori(0, NT // 2) as i:
                    for b in range(2):
                        make_skip(2 * i + b, b)
                make_skip(NT - 1, 0)

            @block.tensor
            def _(pe):
                def first(c, b):
                    pe.wait_ge(xbc_in[b], 32 * (c // 2 + 1) if isinstance(c, int) else 16 * (c + 2 - b))
                    if not (isinstance(c, int) and c == 0):
                        pe.wait_ge(b_turned, c)
                        pe.wait_ge(dve_f.sem, dve_f.at("gb", c - 1))
                    for n in range(8):
                        pe.transpose(tp[:, n // 4, n % 4 * P:(n % 4 + 1) * P], xbc[:, b, n, :], ident[:])
                    last = pe.transpose(gp[:, 2 * P:2 * P + 2 * H], rows[:, b, :], ident[0:2 * H, 0:2 * H])
                    pe_f.done(last, "turn")
                    for n in range(NB):
                        last = pe.matmul(gp[:, n * P:(n + 1) * P], xbc[:, b, NX + n, :], xbc[:, b, NX + NB + n, :], start=True, stop=True)
                    pe_f.done(last, "g")

                def third(c, b):
                    pe.wait_ge(dve_b.sem, dve_b.at("xd1", c + 1))
                    pe.wait_ge(y_read, c + 2)
                    for h in range(HC):
                        for r in range(2):
                            last = pe.matmul(yp[:, h // HG, h % HG * HD:(h % HG + 1) * HD], lm[:, b, HC * r + h, :],
                                             xd[:, r, h * HD:(h + 1) * HD], start=r == 0, stop=r == 1)
                    last.then_inc(y_made, 1)
                    pe.wait_ge(dve_b.sem, dve_b.at("xe1", c + 1))
                    pe.wait_ge(st_read, c + 1)
                    flat = stp[:].rearrange("p a b -> p (a b)")
                    for r in range(2):
                        for n in range(NB):
                            lo, end = (NB * r + n) * GW, (NB * r + n + 1) * GW
                            cut = min(end, -(-(lo + 1) // 512) * 512)
                            for u, v in ((lo, cut), (cut, end)):
                                if u < v:
                                    last = pe.matmul(flat[:, u:v], bt[:, b, n, :], xe[:, r, u - r * D_C:v - r * D_C], start=True, stop=True)
                    last.then_inc(st_made, 1)
                skewed(first, nothing, third, pe)

            @block.scalar
            def _(act):
                act.sem_inc(st_read, 1)

                def turn_b(b):
                    act.activation(bt[:, b].rearrange("p a b -> p (a b)"), tp[:].rearrange("p a b -> p (a b)")[:, D_C:1024], ACT.Copy
                                   ).then_inc(b_turned, 1)

                def second(c, b):
                    if not (isinstance(c, int) and c == NT - 1):
                        turn_b(1 - b)

                def first(c, b):
                    cc = bass.ds(c, 1)
                    act.wait_ge(pe_f.sem, pe_f.at("turn", c))
                    if reused(c):
                        act.wait_ge(dve_b.sem, dve_b.at("xd1", c - 1))
                        act.wait_ge(pool_s.sem, pool_s.at("skip", c - 2))
                    flat = tp[:].rearrange("p a b -> p (a b)")
                    act_f.done(act.activation(xt[:, b], flat[:, 0:D_C], ACT.Copy), "xt")
                    if isinstance(c, int) and c == 0:
                        turn_b(b)
                    act.wait_ge(dve_f.sem, dve_f.at("cols", c))
                    act_f.done(act.activation(ea[:, cc, :].rearrange("p o h -> p (o h)"), cols[:, b, 0:H], ACT.Exp), "ea")
                    act.wait_ge(bc_in[b], 16 * (c // 2 + 1) if isinstance(c, int) else (c + 2 - b) * 8)
                    cd = cdec[:, cc, :].rearrange("p o h -> p (o h)")
                    act_f.done(act.activation(cd[:, 0:HC], bc[:, b, 0:HC, P - 1], ACT.Exp), "cdf")
                    act_f.done(act.activation(cd[:, HC:H], bc[:, b, HC:H, 0], ACT.Exp), "cdb")
                    act.wait_ge(dve_f.sem, dve_f.at("d1", c))
                    act_f.done(act.activation(dec[:, b], dec[:, b], ACT.Exp), "dec")
                    act_f.done(act.activation(lm[:, b], lm[:, b], ACT.Exp), "L")

                def third(c, b):
                    act.wait_ge(st_made, c + 1)
                    act.activation(st[:, :, bass.ds(c, 1), :].rearrange("p r o k -> p r (o k)"),
                                   stp[:].rearrange("p a b -> p (a b)").rearrange("p (r k) -> p r k", r=2), ACT.Copy).then_inc(st_read, 1)
                skewed(first, second, third, act)

            @block.vector
            def _(dve):
                dve.sem_inc(dve_b.sem, len(dve_b.names))

                def first(c, b):
                    at = lambda n: dve.wait_ge(dve_f.sem, dve_f.at(n, c))
                    dve.wait_ge(pe_f.sem, pe_f.at("g", c))
                    dve_f.done(dve.tensor_copy(cols[:, b], gp[:, 2 * P:2 * P + 2 * H]), "cols")
                    for r, (m, name) in enumerate(((upper, "gf"), (lower, "gb"))):
                        dve_f.done(dve.tensor_tensor(g[:, b, r], gp[:, 0:2 * P].rearrange("p (b l) -> p b l", b=NB),
                                                     m[:].unsqueeze(1).broadcast_to([P, NB, P]), ALU.mult), name)
                    if isinstance(c, int) and c == 0:
                        differences(c, b)

                def differences(c, b):
                    at = lambda n: dve.wait_ge(dve_f.sem, dve_f.at(n, c))
                    dve.wait_ge(bc_in[b], 16 * (c // 2 + 1) if isinstance(c, int) else (c + 2 - b) * 8)
                    at("cols")
                    dve_f.done(dve.tensor_tensor(lm[:, b], bc[:, b], cols[:, b, 0:H].unsqueeze(2).broadcast_to([P, H, P]), ALU.subtract), "sub")
                    at("sub")
                    dve_f.done(dve.tensor_scalar(lm[:, b], lm[:, b], 0.0, None, ALU.min), "clamp")
                    dve_f.done(dve.tensor_tensor(dec[:, b, 0], bc[:, b, 0:HC, P - 1], cols[:, b, 0:HC], ALU.subtract), "d0")
                    dve_f.done(dve.tensor_tensor(dec[:, b, 1], bc[:, b, HC:H, 0], cols[:, b, HC:H], ALU.subtract), "d1")

                def second(c, b):
                    at = lambda n: dve.wait_ge(dve_b.sem, dve_b.at(n, c + 1))
                    if not (isinstance(c, int) and c == NT - 1):
                        differences(c + 1, 1 - b)
                    dve.wait_ge(act_f.sem, act_f.at("L", c))
                    dve.wait_ge(dve_f.sem, dve_f.at("gb", c))
                    dve.wait_ge(dve_b.sem, dve_b.at("xe1", c))
                    for q in range(4):
                        part = lm[:, b, q * HG:(q + 1) * HG, :]
                        last = dve.tensor_tensor(part, part, g[:, b, q // 2, q % 2].unsqueeze(1).broadcast_to([P, HG, P]), ALU.mult)
                    dve_b.done(last, "m")
                    for r in range(2):
                        dve_b.done(dve.tensor_tensor(heads(xd[:, r]), heads(xt[:, b]), cols[:, b, H + HC * r:H + HC * (r + 1)].unsqueeze(2)
                                                     .broadcast_to([P, HC, HD]), ALU.mult), f"xd{r}")
                    for r in range(2):
                        at(f"xd{r}")
                        if r == 0 and not (isinstance(c, int) and c == 0):
                            dve.wait_ge(st_made, c)
                        dve_b.done(dve.tensor_tensor(heads(xe[:, r]), heads(xd[:, r]), dec[:, b, r].unsqueeze(2)
                                                     .broadcast_to([P, HC, HD]), ALU.mult), f"xe{r}")

                def third(c, b):
                    dve.wait_ge(y_made, c + 1)
                    dve.wait_ge(pool_s.sem, pool_s.at("skip", c))
                    dve.tensor_tensor(ytok[:, bass.ds(c, 1), :].rearrange("p o (b k) -> p (o b) k", b=NB), yp[:, :, 0:GW],
                                      skip[:, b].rearrange("p (b k) -> p b k", b=NB), ALU.add).then_inc(y_read, 1)
                skewed(first, second, third, dve)

        with ExitStack() as inner:
            s = Scope(nc, inner, "scan")
            cur = s.sb("cur", [P, 2, 2, D_C])
            tmp = s.sb("tmp", [P, 2, D_C])
            fin = s.sb("fin", [P, 2 * NX, P])
            turn = s.ps("turn", [P, 3, 512])
            moved, kept, made = s.sem("moved"), s.sem("kept"), [s.sem(f"made{r}") for r in range(2)]
            fin_turned, fin_copied, fin_out = s.sem("fin_turned"), s.sem("fin_copied"), s.sem("fin_out")
            block = inner.enter_context(nc.Block())

            @block.tensor
            def _(pe):
                for n in range(2 * NX):
                    r, j = n // NX, n % NX
                    last = pe.transpose(turn[:, n // 4, n % 4 * P:(n % 4 + 1) * P], st[:, r, 0, j * P:(j + 1) * P], ident[:])
                last.then_inc(fin_turned, 1)

            @block.scalar
            def _(act):
                act.wait_ge(fin_turned, 1)
                act.activation(fin[:].rearrange("p (a b) k -> p a (b k)", a=3), turn[:], ACT.Copy).then_inc(fin_copied, 1)
                act.wait_ge(fin_copied, 1)
                act.dma_start(d["new_ssd"].rearrange("(n p) k -> p n k", p=P), fin[:]).then_inc(fin_out, 16)
                n = 0
                for k in range(1, NT):
                    for r in range(2):
                        c = k if r == 0 else NT - k
                        src = s_init[:, r] if k == 1 else cur[:, r, (k - 1) % 2]
                        if k < NT - 1:
                            act.wait_ge(made[r], 2 * k)
                        act.activation(st[:, r, c, :], src, ACT.Copy).then_inc(kept, 1)
                act.wait_ge(fin_out, 16)

            @block.vector
            def _(dve):
                dve.wait_ge(fin_turned, 1)
                dve.memset(st[:, :, 0, :], 0.0)
                heads = lambda ap: ap.rearrange("p (h k) -> p h k", h=HC)
                for k in range(1, NT - 1):
                    for r in range(2):
                        c = k if r == 0 else NT - k
                        src = s_init[:, r] if k == 1 else cur[:, r, (k - 1) % 2]
                        if k > 1:
                            dve.wait_ge(made[r], 2 * k - 2)
                        dve.tensor_tensor(heads(tmp[:, r]), heads(src), cdec[:, c, HC * r:HC * (r + 1)].unsqueeze(2)
                                          .broadcast_to([P, HC, HD]), ALU.mult).then_inc(made[r], 1)
                    for r in range(2):
                        c = k if r == 0 else NT - k
                        dve.wait_ge(made[r], 2 * k - 1)
                        if k > 2:
                            dve.wait_ge(kept, 2 * (k - 2) + r + 1)
                        dve.tensor_tensor(cur[:, r, k % 2], tmp[:, r], st[:, r, c, :], ALU.add).then_inc(made[r], 1)

        with ExitStack() as inner:
            s = Scope(nc, inner, "off")
            ct = s.sb("ct", [P, NB, P])
            z = s.sb("z", [P, NX, P])
            sz = s.sb("sz", [P, NX, P])
            t0 = s.sb("t0", [P, 2, D_C])
            yt = s.sb("yt", [P, D_C])
            yg = s.sb("yg", [P, NX, P])
            sq = s.sb("sq", [P, NX, P])
            rt = s.sb("rt", [P, P])
            ri = s.sb("ri", [P, P])
            yn = s.sb("yn", [P, NX, P])
            off = [s.ps(f"off{r}", [P, 2, 512]) for r in range(2)]
            turn = s.ps("turn", [P, 2, 512])
            ms = s.ps("ms")
            in_s, out_s = s.sem("in_s"), s.sem("out_s")
            pe_s = Steps(s.sem("pe_s"), "off0 off1 turn ms")
            act_s = Steps(s.sem("act_s"), "sz sq root")
            dve_s = Steps(s.sem("dve_s"), "t0 t1 a0 a1 yg inv yn0 yn")
            block = inner.enter_context(nc.Block())

            @block.sync
            def _(sp):
                sp.sem_inc(out_s, 16)
                xbc_v = d["XBC"].rearrange("(n p) t -> p n t", p=P)
                z_v = d["FEAT"].rearrange("(n p) t -> p n t", p=P)

                def load(c):
                    sp.dma_start(ct[:], xbc_v[:, NX + NB:NCH, bass.ds(c * P, P)]).then_inc(in_s, 16)
                    sp.dma_start(z[:], z_v[:, F_Z:F_Z + NX, bass.ds(c * P, P)]).then_inc(in_s, 16)

                def store(c):
                    sp.wait_ge(dve_s.sem, dve_s.at("yn", c))
                    sp.dma_start(d["YT"].rearrange("(n p) t -> p n t", p=P)[:, (D_A + D_B) // P:KT, bass.ds(c * P, P)], yn[:]
                                 ).then_inc(out_s, 16)
                load(0)
                with sp.Fori(1, NT) as c:
                    sp.wait_ge(pe_s.sem, pe_s.at("off1", c - 1))
                    sp.wait_ge(act_s.sem, act_s.at("sz", c - 1))
                    load(c)
                    store(c - 1)
                store(NT - 1)
                sp.wait_ge(out_s, 16 * (NT + 1))

            @block.tensor
            def _(pe):
                with pe.Fori(0, NT) as c:
                    pe.wait_ge(in_s, 32 * (c + 1))
                    for r in range(2):
                        for b in range(NB):
                            last = pe.matmul(off[r][:, b, 0:GW], ct[:, b, :],
                                             st[:, r, bass.ds(c, 1), b * GW:(b + 1) * GW].rearrange("p o k -> p (o k)"), start=True, stop=True)
                        pe_s.done(last, f"off{r}")
                    pe.wait_ge(dve_s.sem, dve_s.at("a1", c))
                    for n in range(NX):
                        last = pe.transpose(turn[:, n // 4, n % 4 * P:(n % 4 + 1) * P], yt[:, n * P:(n + 1) * P], ident[:])
                    pe_s.done(last, "turn")
                    pe.wait_ge(act_s.sem, act_s.at("sq", c))
                    for n in range(NX):
                        last = pe.matmul(ms[:, 0:P], ones[:], sq[:, n, :], start=n == 0, stop=n == NX - 1)
                    pe_s.done(last, "ms")

            @block.scalar
            def _(act):
                with act.Fori(0, NT) as c:
                    act.wait_ge(in_s, 32 * (c + 1))
                    act_s.done(act.activation(sz[:], z[:], ACT.Silu), "sz")
                    act.wait_ge(dve_s.sem, dve_s.at("yg", c))
                    act_s.done(act.activation(sq[:], yg[:], ACT.Square), "sq")
                    act.wait_ge(pe_s.sem, pe_s.at("ms", c))
                    act_s.done(act.activation(rt[:], ms[:, 0:P], ACT.Sqrt, bias=epsc[:, 0:1], scale=1.0 / D_C), "root")

            @block.vector
            def _(dve):
                with dve.Fori(0, NT) as c:
                    heads = lambda ap: ap.rearrange("p (h k) -> p h k", h=HC)
                    at = lambda n: dve.wait_ge(dve_s.sem, dve_s.at(n, c))
                    for r in range(2):
                        dve.wait_ge(pe_s.sem, pe_s.at(f"off{r}", c))
                        for b in range(NB):
                            last = dve.tensor_tensor(heads(t0[:, r])[:, b * HG:(b + 1) * HG, :],
                                                     off[r][:, b, 0:GW].rearrange("p (h k) -> p h k", h=HG),
                                                     ea[:, bass.ds(c, 1), HC * r + b * HG:HC * r + (b + 1) * HG].rearrange("p o h -> p (o h)")
                                                     .unsqueeze(2).broadcast_to([P, HG, HD]), ALU.mult)
                        dve_s.done(last, f"t{r}")
                    at("t1")
                    dve_s.done(dve.tensor_tensor(t0[:, 0], t0[:, 0], t0[:, 1], ALU.add), "a0")
                    at("a0")
                    dve_s.done(dve.tensor_tensor(yt[:], t0[:, 0], ytok[:, bass.ds(c, 1), :].rearrange("p o k -> p (o k)"), ALU.add), "a1")
                    dve.wait_ge(pe_s.sem, pe_s.at("turn", c))
                    dve.wait_ge(act_s.sem, act_s.at("sz", c))
                    dve_s.done(dve.tensor_tensor(yg[:].rearrange("p n k -> p (n k)"), turn[:].rearrange("p a b -> p (a b)")[:, 0:D_C],
                                                 sz[:].rearrange("p n k -> p (n k)"), ALU.mult), "yg")
                    dve.wait_ge(act_s.sem, act_s.at("root", c))
                    dve_s.done(dve.reciprocal(ri[:], rt[:]), "inv")
                    at("inv")
                    dve.wait_ge(out_s, 16 * (c + 1))
                    dve_s.done(dve.tensor_tensor(yn[:], yg[:], ri[:].unsqueeze(1).broadcast_to([P, NX, P]), ALU.mult), "yn0")
                    at("yn0")
                    dve_s.done(dve.tensor_tensor(yn[:], yn[:], norm_g[:].unsqueeze(2).broadcast_to([P, NX, P]), ALU.mult), "yn")


RC = 64
NJ_A = D_A // P


def rwkv_features(nc, d):
    NJ = NJ_A
    W = PAD_S + TS - PAD_C
    with ExitStack() as stack:
        s = Scope(nc, stack, "rf")
        mu = s.sb("mu", [P, 15])
        hmu = s.sb("hmu", [P, 15])
        omu = s.sb("omu", [P, 15])
        par = s.sb("par", [P, 7, NJ])
        oka = s.sb("oka", [P, NJ])
        bd = s.sb("bd", [P, P])
        up = s.sb("up", [P, 3, P])
        keep = s.sb("keep", [P, 2, T])
        u = s.sb("u", [P, 3, TP])
        sm = s.sb("sm", [P, TP])
        lora = s.sb("lora", [P, 3, T])
        m = s.sb("m", [P, 3, T])
        kk = s.sb("kk", [P, T])
        t1 = s.sb("t1", [P, T])
        sg = s.sb("sg", [P, 2, T])
        a = s.sb("a", [P, 2, T])
        kd = s.sb("kd", [P, 2, T])
        ls = s.sb("ls", [P, 2, T])
        pt = s.sb("pt", [P, 3, T])
        o = s.sb("o", [P, 4, T])
        g = s.sb("g", [P, T])
        bv = s.sb("bv", [P, T])
        pc = s.sb("pc", [P, 2, NJ, T // RC])
        acc = [s.ps(f"acc{i}", [P, NSEG, 512]) for i in range(2)]
        par_in, pads, prep, u0_in, u_in, up_in = (s.sem(n) for n in ("par_in", "pads", "prep", "u0_in", "u_in", "up_in"))
        o_out, g_out, b_out, pc_out = s.sem("o_out"), s.sem("g_out"), s.sem("b_out"), s.sem("pc_out")
        mixed, lora_act = s.sem("mixed"), s.sem("lora_act")
        link_s, bv_s = s.sem("link"), s.sem("bv_s")
        pe_s = Steps(s.sem("pe_s"), "w0 a0 w1 a1 ss g bonus")
        act_s = Steps(s.sem("act_s"), "sg0 a0 sg1 a1 sq root g p0 i0 q0 p1 i1 q1")
        dve_s = Steps(s.sem("dve_s"), "mr mk mv kk rec kkn km0 kd0 km1 kd1 bsum b0 b1 L0 L1 D0 D1 pc0 r0 x0 y0 z0 pc1 r1 x1 y1 z1 bv")
        block = stack.enter_context(nc.Block())
        seg = lambda ap: ap.rearrange("p (q c) -> p q c", q=NSEG)

        @block.sync
        def _(sp):
            for dst, name in ((mu, "rw_mu"), (par, "rw_par"), (bd, "bd_ones")):
                sp.dma_start(dst[:], d[name]).then_inc(par_in, 16)

            def load(b, tile, sem):
                for dst, off, n in zip(padded(u[:, b]), (0, TC), (TC, TS)):
                    sp.dma_start(dst, d["FEAT"][bass.ds(tile * P, P), off:off + n]).then_inc(sem, 16)

            def load_up(j):
                sp.dma_start(up[:], d["rw_up"][:, :, bass.ds(j * P, P)]).then_inc(up_in, 16)
            sp.wait_ge(pads, 4)
            for b in range(3):
                load(b, F_WD + b, u0_in)
            load_up(0)
            sp.wait_ge(mixed, 3)
            for b in range(3):
                load(b, NJ * b, u_in)

            def store(r, j):
                dst = lambda n: d["RW"][n, r, bass.ds(j * P, P), :]
                for n, step in ((0, "x"), (1, "y"), (2, "z")):
                    sp.wait_ge(dve_s.sem, dve_s.at(f"{step}{r}", j))
                    sp.dma_start(dst(n), o[:, n]).then_inc(o_out, 16)
                sp.dma_start(d["RT"][r, bass.ds(j * P, P), :], o[:, 3]).then_inc(o_out, 16)
                sp.dma_start(dst(3), m[:, 2]).then_inc(o_out, 16)

            def tile(j, more):
                if more:
                    sp.wait_ge(dve_s.sem, dve_s.at("mv", j))
                    for b in range(3):
                        load(b, NJ * b + j + 1, u_in)
                sp.wait_ge(act_s.sem, act_s.at("g", j))
                sp.dma_start(d["GATE"][bass.ds(j * P, P), :], g[:]).then_inc(g_out, 16)
                if more:
                    load_up(j + 1)
                store(0, j)
                store(1, j)
                sp.wait_ge(dve_s.sem, dve_s.at("bv", j))
                sp.dma_start(d["BONUS"][bass.ds(j * P, P), :], bv[:]).then_inc(b_out, 16)
            with sp.Fori(0, NJ - 1) as j:
                tile(j, True)
            tile(NJ - 1, False)
            sp.wait_ge(o_out, 160 * NJ + 80)
            sp.wait_ge(g_out, 16 * (NJ + 1))
            sp.wait_ge(b_out, 16 * (NJ + 1))
            sp.wait_ge(dve_s.sem, dve_s.at("pc1", NJ - 1))
            sp.dma_start(d["PC"], pc[:].rearrange("p r j c -> p (r j c)")).then_inc(pc_out, 16)
            sp.wait_ge(pc_out, 16)

        @block.gpsimd
        def _(pool):
            for b in range(3):
                zero_pads(pool, u[:, b], pads)
            pool.memset(keep[:], 1.0).then_inc(pads, 1)
            pool.wait_ge(pads, 4)
            k = keep[:].rearrange("p r (c t) -> p r c t", t=RC)
            pool.memset(k[:, 0, :, 0:1], 0.0)
            pool.memset(k[:, 1, :, RC - 1:RC], 0.0).then_inc(pads, 1)

        @block.tensor
        def _(pe):
            pe.wait_ge(par_in, 48)
            with pe.Fori(0, NJ) as j:
                def product(n, name, lhs, rhs, wait):
                    for sem, val in wait:
                        pe.wait_ge(sem, val)
                    for q in range(NSEG):
                        last = pe.matmul(acc[n % 2][:, q, 0:SEG], lhs, rhs[:, q * SEG:(q + 1) * SEG], start=True, stop=True)
                    pe_s.done(last, name)
                done_act = lambda n: (act_s.sem, act_s.at(n, j))
                done_dve = lambda n: (dve_s.sem, dve_s.at(n, j))
                half = (slice(0, 64), slice(64, P))
                product(0, "w0", up[half[0], 0, :], lora[half[0], 0], [(up_in, 16 * (j + 1)), (lora_act, 2), (mixed, 3), done_dve("mv")])
                product(1, "a0", up[half[0], 1, :], lora[half[0], 1], [])
                product(2, "w1", up[half[1], 0, :], lora[half[1], 0], [done_act("sg0")])
                product(3, "a1", up[half[1], 1, :], lora[half[1], 1], [done_act("a0")])
                product(4, "ss", bd[:], t1, [done_act("sq")])
                product(5, "g", up[:, 2, :], lora[:, 2], [done_act("a1")])
                product(6, "bonus", bd[:], t1, [done_dve("bsum"), done_act("root")])

        @block.scalar
        def _(act):
            act.wait_ge(mixed, 3)
            act.activation(lora[:, 0], lora[:, 0], ACT.Tanh).then_inc(lora_act, 1)
            act.activation(lora[:, 2], lora[:, 2], ACT.Sigmoid).then_inc(lora_act, 1)
            act.wait_ge(prep, 3)
            act.sem_inc(g_out, 16)
            act.sem_inc(b_out, 16)
            with act.Fori(0, NJ) as j:
                col = lambda n: par[:, n, bass.ds(j, 1)]
                for n, (name, dst, r) in enumerate((("sg0", sg, 0), ("a0", a, 0), ("sg1", sg, 1), ("a1", a, 1))):
                    act.wait_ge(pe_s.sem, pe_s.at(pe_s.names[n], j))
                    act_s.done(act.activation(seg(dst[:, r]), acc[n % 2][:, :, 0:SEG], ACT.Sigmoid,
                                              bias=col((0, 2, 1, 3)[n])), name)
                act.wait_ge(dve_s.sem, dve_s.at("kk", j))
                act_s.done(act.activation(t1[:], kk[:], ACT.Square), "sq")
                act.wait_ge(pe_s.sem, pe_s.at("ss", j))
                act_s.done(act.activation(seg(t1[:]), acc[0][:, :, 0:SEG], ACT.Sqrt), "root")
                act.wait_ge(pe_s.sem, pe_s.at("g", j))
                act.wait_ge(g_out, 16 * (j + 1))
                act_s.done(act.activation(seg(g[:]), acc[1][:, :, 0:SEG], ACT.Copy), "g")
                for r in range(2):
                    act.wait_ge(dve_s.sem, dve_s.at(f"D{r}", j))
                    if r:
                        act.wait_ge(dve_s.sem, dve_s.at("z0", j))
                    act_s.done(act.activation(pt[:, 0], ls[:, r], ACT.Exp, scale=-DECAY), f"p{r}")
                    act_s.done(act.activation(pt[:, 1], ls[:, r], ACT.Exp, scale=DECAY), f"i{r}")
                    act_s.done(act.activation(pt[:, 2], sg[:, r], ACT.Exp, scale=-DECAY), f"q{r}")

        @block.vector
        def _(dve):
            link = Chain(dve, link_s)

            def mix(out, ub, col, name=None, step=None):
                lo = PAD_C
                link(dve.tensor_tensor(sm[:, lo:lo + W], ub[:, lo - 1:lo - 1 + W], ub[:, lo + 1:lo + 1 + W], ALU.add))
                link(dve.tensor_scalar(sm[:, lo:lo + W], sm[:, lo:lo + W], col(hmu), None, ALU.mult))
                dve.scalar_tensor_tensor(out[:, 0:TC], ub[:, PAD_C:PAD_C + TC], col(omu), sm[:, PAD_C:PAD_C + TC], ALU.mult, ALU.add)
                return dve.scalar_tensor_tensor(out[:, TC:T], ub[:, PAD_S:PAD_S + TS], col(omu), sm[:, PAD_S:PAD_S + TS],
                                                ALU.mult, ALU.add)
            dve.wait_ge(par_in, 48)
            dve.wait_ge(pads, 5)
            dve.tensor_scalar(hmu[:], mu[:], 0.5, None, ALU.mult).then_inc(prep, 1)
            dve.tensor_scalar(omu[:], mu[:], -1.0, 1.0, ALU.mult, ALU.add).then_inc(prep, 1)
            dve.tensor_scalar(oka[:], par[:, 5], -1.0, 1.0, ALU.mult, ALU.add).then_inc(prep, 1)
            dve.wait_ge(prep, 3)
            dve.wait_ge(u0_in, 96)
            for b in range(3):
                mix(lora[:, b], u[:, b], lambda p, b=b: p[:, F_WD + b:F_WD + b + 1]).then_inc(mixed, 1)
                dve.wait_ge(mixed, b + 1)
            start = link.n
            PER = 2 * 3
            link.per = PER
            dve.sem_inc(o_out, 80)
            with dve.Fori(0, NJ) as j:
                link.turn(j, start)
                at = lambda n: dve.wait_ge(dve_s.sem, dve_s.at(n, j))
                act_at = lambda n: dve.wait_ge(act_s.sem, act_s.at(n, j))
                done = dve_s.done
                col = lambda n: par[:, n, bass.ds(j, 1)]
                r_, k_, v_ = m[:, 0], m[:, 1], m[:, 2]
                dve.wait_ge(u_in, 96 * (j + 1))
                dve.wait_ge(o_out, 160 * j + 80)
                for b, name in enumerate(("mr", "mk", "mv")):
                    done(mix(m[:, b], u[:, b], lambda p, b=b: p[:, bass.ds(NJ * b + j, 1)]), name)
                    at(name)
                link.end()
                done(dve.tensor_scalar(kk[:], k_, col(4), None, ALU.mult), "kk")
                act_at("root")
                done(dve.tensor_scalar(t1[:], t1[:], 1e-12, None, ALU.max), "rec")
                at("rec")
                dve.reciprocal(t1[:], t1[:]).then_inc(mixed, 1)
                dve.wait_ge(mixed, j + 4)
                done(dve.tensor_tensor(kk[:], kk[:], t1[:], ALU.mult), "kkn")
                for r in range(2):
                    act_at(f"a{r}")
                    done(dve.tensor_scalar(kd[:, r], a[:, r], col(5), oka[:, bass.ds(j, 1)], ALU.mult, ALU.add), f"km{r}")
                    at(f"km{r}")
                    done(dve.tensor_tensor(kd[:, r], kd[:, r], k_, ALU.mult), f"kd{r}")
                at("kd1")
                dve.tensor_tensor(sm[:, 0:T], kd[:, 0], kd[:, 1], ALU.add).then_inc(bv_s, 1)
                dve.wait_ge(bv_s, 2 * j + 1)
                dve.tensor_tensor(sm[:, 0:T], sm[:, 0:T], r_, ALU.mult).then_inc(bv_s, 1)
                dve.wait_ge(bv_s, 2 * j + 2)
                at("kkn")
                done(dve.tensor_scalar(t1[:], sm[:, 0:T], col(6), None, ALU.mult), "bsum")
                for r in range(2):
                    done(dve.tensor_tensor(a[:, r], a[:, r], kk[:], ALU.mult), f"b{r}")
                for r in range(2):
                    back = slice(None, None, -1) if r else slice(None)
                    done(dve.tensor_tensor_scan(ls[:, r][:, back], keep[:, r][:, back], sg[:, r][:, back], 0.0, ALU.mult, ALU.add), f"L{r}")
                for r in range(2):
                    at(f"L{r}")
                    done(dve.tensor_tensor(sg[:, r], ls[:, r], sg[:, r], ALU.subtract), f"D{r}")
                for r in range(2):
                    act_at(f"q{r}")
                    end = pt[:, 0].rearrange("p (c t) -> p c t", t=RC)[:, :, 0 if r else RC - 1]
                    done(dve.tensor_copy(pc[:, r, bass.ds(j, 1), :].rearrange("p o c -> p (o c)"), end), f"pc{r}")
                    dve.wait_ge(o_out, 160 * j + 80 * (r + 1))
                    done(dve.tensor_tensor(o[:, 3], r_, pt[:, 0], ALU.mult), f"r{r}")
                    done(dve.scalar_tensor_tensor(o[:, 0], kk[:], -1.0, pt[:, 2], ALU.mult, ALU.mult), f"x{r}")
                    at(f"b{r}")
                    done(dve.tensor_tensor(o[:, 1], a[:, r], pt[:, 1], ALU.mult), f"y{r}")
                    done(dve.tensor_tensor(o[:, 2], kd[:, r], pt[:, 1], ALU.mult), f"z{r}")
                dve.wait_ge(pe_s.sem, pe_s.at("bonus", j))
                dve.wait_ge(b_out, 16 * (j + 1))
                done(dve.tensor_tensor(seg(bv[:]), acc[0][:, :, 0:SEG], seg(v_), ALU.mult), "bv")
                at("bv")


PRODUCTS = [
    ("T", "dve", ""), ("Tt", "dve", ""), ("Bt", "dve", ""), ("A2", "dve", ""),
    ("W2", "dve", "T Tt"), ("bT", "act", ""), ("X2", "act", "W2 Tt"), ("Y2", "act", "W2 Tt"),
    ("W4", "dve", "X2"), ("kT", "act", ""), ("X4", "act", "W4 Y2"), ("Y4", "act", "W4 Y2"),
    ("W8", "dve", "X4"), ("vT", "act", ""), ("X8", "act", "W8 Y4"), ("Y8", "act", "W8 Y4"),
    ("W16", "dve", "X8"), ("X16", "act", "W16 Y8"), ("Y16", "act", "W16 Y8"),
    ("W32", "dve", "X16"), ("R", "dve", "Bt vT -S"), ("Y32", "act", "W32 Y16"), 
    ("U", "dve", "R Y32"), ("Yo", "act", "U A2 vT -S"), ("S", "dve", "U bT kT vT"),
]
NAMES = [p[0] for p in PRODUCTS]
TAKER = {p[0]: p[1] for p in PRODUCTS}
NP_ = len(PRODUCTS)


def taken(name):
    return [n for n in NAMES if TAKER[n] == TAKER[name]].index(name) + 1


TAKEN = {e: sum(t == e for t in TAKER.values()) for e in ("dve", "act")}


def rwkv_recurrence(nc, d):
    with ExitStack() as stack:
        s = Scope(nc, stack, "rr")
        ident = s.sb("ident", [P, P])
        masks = s.sb("masks", [P, 2, 9, P])
        pc = s.sb("pc", [P, 2, NJ_A, T // RC])
        S = s.sb("S", [P, 2, 4, P])
        Stmp = s.sb("Stmp", [P, 2, 4, P])
        bdt = s.sb("bdt", [P, 2, 4, 2, 4, P])
        rt = s.sb("rt", [P, 2, 2, 4, RC])
        names = "X1 Y1 Tt Bt A2 bT kT vT W X Y R U"
        buf = {n: s.sb(n, [P, 2, 4, P]) for n in names.split()}
        yo = s.sb("yo", [P, 2, 2, 4, RC])
        sio = s.sb("sio", [P, 2, 4, P])
        pre = s.sb("pre", [P, 2, 2, 4, P])
        const_in, zeroed = s.sem("const_in"), s.sem("zeroed")
        W_MASK = {"W2": 0, "W4": 1, "W8": 2, "W16": 3, "W32": 4}
        M_STRICT, M_INCL, M_ONE, M_ONET = 5, 6, 7, 8
        rep = lambda ap, n=4: ap.unsqueeze(1).broadcast_to([P, n, ap.shape[-1]])

        def run(tag, chunk0, n_chunks):
            pairs = n_chunks // 2
            with ExitStack() as inner:
                q = Scope(nc, inner, tag)
                bank = [[q.ps(f"bank{g}{i}") for i in range(4)] for g in range(2)]
                slot_in = [q.sem(f"slot_in{i}") for i in range(2)]
                product = [q.sem(f"product{g}") for g in range(2)]
                took = {e: [q.sem(f"{e}_took{g}") for g in range(2)] for e in ("dve", "act")}
                y_out = [q.sem(f"y_out{i}") for i in range(2)]
                s_sum = q.sem("s_sum")
                masked = [q.sem(f"masked{g}") for g in range(2)]
                block = inner.enter_context(nc.Block())

                def pairs_loop(eng, body):
                    if pairs == 1:
                        body(0)
                    else:
                        with eng.Fori(0, pairs) as i:
                            body(i)

                def bank_of(slot, k):
                    return (k + NP_ * slot) % 4

                def in_bank_before(slot, k):
                    for back in range(1, 2 * NP_):
                        kk, sl, ago = k - back, slot, 0
                        while kk < 0:
                            kk, sl, ago = kk + NP_, 1 - sl, ago + 1
                        if bank_of(sl, kk) == bank_of(slot, k):
                            return NAMES[kk], ago

                def wait_taken(eng, g, n, name, ago=0):
                    e = TAKER[name]
                    eng.wait_ge(took[e][g], TAKEN[e] * (n + 1 - ago) + taken(name))

                def chunk(g, n):
                    return chunk0 + n if g == 0 else n * -1 + (chunk0 + n_chunks - 1)

                @block.sync
                def _(sp):
                    def load(n, slot):
                        for g in range(2):
                            t0 = bass.ds(chunk(g, n) * RC, RC)
                            for h in range(2):
                                hs = slice(64 * h, 64 * h + 64)
                                for ar in range(4):
                                    sp.dma_start(bdt[hs, slot, ar, g, :, hs],
                                                 d["RW"][ar, g].rearrange("(j p) t -> p j t", p=P)[hs, :, t0]
                                                 ).then_inc(slot_in[slot], 16)
                            sp.dma_start(rt[:, slot, g], d["RT"][g].rearrange("(j p) t -> p j t", p=P)[:, :, t0]
                                         ).then_inc(slot_in[slot], 16)
                    for slot in range(2):
                        load(slot, slot)
                    if pairs > 1:
                        with sp.Fori(1, pairs) as i:
                            for slot in range(2):
                                for g in range(2):
                                    sp.wait_ge(product[g], NP_ * (2 * (i - 1) + slot + 1))
                                load(2 * i + slot, slot)

                @block.tensor
                def _(pe):
                    def step(i, slot):
                        n = 2 * i + slot
                        pe.wait_ge(slot_in[slot], 16 * 18 * (i + 1))
                        for k, (name, _, deps) in enumerate(PRODUCTS):
                            for g in range(2):
                                need = [(dep.strip("-"), int(dep[0] == "-")) for dep in deps.split()] + [in_bank_before(slot, k)]
                                for e in ("dve", "act"):
                                    last_of = max((taken(nm) - TAKEN[e] * ago for nm, ago in need if TAKER[nm] == e), default=None)
                                    if last_of is not None:
                                        pe.wait_ge(took[e][g], TAKEN[e] * (n + 1) + last_of)
                                out = bank[g][bank_of(slot, k)]
                                B = lambda nm, c: buf[nm][:, g, c, :]
                                I = lambda ar, c: bdt[:, slot, ar, g, c, :]
                                KKT, BH, KH, V = range(4)
                                m = int(name[1:]) if name[1:].isdigit() else 0
                                first = m == 2
                                x, y = ("X1", "Y1") if first else ("X", "Y")
                                for c in range(4):
                                    o = out[:, c * P:(c + 1) * P]
                                    mm = lambda lhs, rhs, a=True, b=True, o=o: pe.matmul(o, lhs, rhs, start=a, stop=b)
                                    if name == "T":
                                        last = mm(I(KKT, c), I(BH, c))
                                    elif name == "Tt":
                                        last = mm(I(BH, c), I(KKT, c))
                                    elif name == "Bt":
                                        last = mm(I(KH, c), I(KKT, c))
                                    elif name == "A2":
                                        r = rt[:, slot, g, c, :]
                                        pe.matmul(out[:, c * RC:(c + 1) * RC], I(BH, c), r, start=True, stop=True)
                                        last = pe.matmul(out[:, (4 + c) * RC:(5 + c) * RC], I(KH, c), r, start=True, stop=True)
                                    elif name in ("bT", "kT", "vT"):
                                        last = pe.transpose(o, I({"b": BH, "k": KH, "v": V}[name[0]], c), ident[:])
                                    elif name[0] == "W":
                                        last = mm(B("Tt", c), B(x, c))
                                    elif name[0] == "X":
                                        last = mm(B(y, c), B("W", c))
                                    elif name == "Yo":
                                        o = out[:, c * RC:(c + 1) * RC]
                                        a2 = buf["A2"][:, g].rearrange("p c t -> p (c t)")
                                        mm(B("U", c), a2[:, c * RC:(c + 1) * RC], True, False, o)
                                        mm(B("vT", c), a2[:, (4 + c) * RC:(5 + c) * RC], False, False, o)
                                        last = mm(S[:, g, c, :], rt[:, slot, g, c, :], False, True, o)
                                    elif name[0] == "Y":
                                        last = mm(B("W", c), B(y, c))
                                    elif name == "R":
                                        mm(I(KKT, c), S[:, g, c, :], True, False)
                                        last = mm(B("Bt", c), B("vT", c), False, True)
                                    elif name == "U":
                                        last = mm(B("Y", c), B("R", c))
                                    elif name == "S":
                                        mm(B("bT", c), B("U", c), True, False)
                                        last = mm(B("kT", c), B("vT", c), False, True)
                                last.then_inc(product[g], 1)
                    pairs_loop(pe, lambda i: [step(i, slot) for slot in range(2)])

                def wait_product(eng, g, n, name):
                    eng.wait_ge(product[g], NP_ * n + NAMES.index(name) + 1)

                @block.scalar
                def _(act):
                    for g in range(2):
                        act.sem_inc(took["act"][g], TAKEN["act"])

                    def step(i, slot):
                        n = 2 * i + slot
                        for k, name in enumerate(NAMES):
                            if TAKER[name] != "act":
                                continue
                            for g in range(2):
                                wait_product(act, g, n, name)
                                out = bank[g][bank_of(slot, k)]
                                if name == "Yo":
                                    act.wait_ge(y_out[slot], 32 * (i + 1))
                                    act.activation(yo[:, slot, g].rearrange("p c t -> p (c t)"), out[:, 0:4 * RC], ACT.Copy
                                                   ).then_inc(took["act"][g], 1)
                                    wait_taken(act, g, n, "Yo")
                                    act.dma_start(d["YD"][g].rearrange("(j p) t -> p j t", p=P)[:, :, bass.ds(chunk(g, n) * RC, RC)],
                                                  yo[:, slot, g]).then_inc(y_out[slot], 16)
                                else:
                                    dst = buf[name if name[1] == "T" else name[0]]
                                    act.activation(dst[:, g].rearrange("p c t -> p (c t)"), out[:], ACT.Copy
                                                   ).then_inc(took["act"][g], 1)
                    for slot in range(2):
                        act.sem_inc(y_out[slot], 32)
                    pairs_loop(act, lambda i: [step(i, slot) for slot in range(2)])
                    for slot in range(2):
                        act.wait_ge(y_out[slot], 32 * (pairs + 1))

                @block.vector
                def _(dve):
                    for g in range(2):
                        dve.sem_inc(took["dve"][g], TAKEN["dve"])

                    def step(i, slot):
                        n = 2 * i + slot
                        for k, name in enumerate(NAMES):
                            if TAKER[name] != "dve":
                                continue
                            for g in range(2):
                                wait_product(dve, g, n, name)
                                out = bank[g][bank_of(slot, k)]
                                o4 = out[:].rearrange("p (c t) -> p c t", c=4)
                                eye = rep(ident[:])
                                inc = lambda ins: ins.then_inc(took["dve"][g], 1)
                                if name == "T":
                                    dve.tensor_tensor(pre[:, g, 0], o4, rep(masks[:, g, M_ONE]), ALU.mult).then_inc(masked[g], 1)
                                    dve.wait_ge(masked[g], 2 * n + 1)
                                    inc(dve.tensor_tensor(buf["X1"][:, g], pre[:, g, 0], eye, ALU.add))
                                elif name == "Tt":
                                    dve.tensor_tensor(pre[:, g, 0], o4, rep(masks[:, g, M_STRICT]), ALU.mult)
                                    dve.tensor_tensor(pre[:, g, 1], o4, rep(masks[:, g, M_ONET]), ALU.mult).then_inc(masked[g], 1)
                                    dve.wait_ge(masked[g], 2 * n + 2)
                                    dve.tensor_tensor(buf["Tt"][:, g], pre[:, g, 0], eye, ALU.add)
                                    inc(dve.tensor_tensor(buf["Y1"][:, g], pre[:, g, 1], eye, ALU.add))
                                elif name == "Bt":
                                    inc(dve.tensor_tensor(buf["Bt"][:, g], o4, rep(masks[:, g, M_STRICT]), ALU.mult))
                                elif name == "A2":
                                    inc(dve.tensor_tensor(buf["A2"][:, g].rearrange("p c (b t) -> p (c b) t", b=2),
                                                          out[:].rearrange("p (c t) -> p c t", c=8), rep(masks[:, g, M_INCL, 0:RC], 8), ALU.mult))
                                elif name[0] == "W":
                                    inc(dve.tensor_tensor(buf["W"][:, g], o4, rep(masks[:, g, W_MASK[name]]), ALU.mult))
                                elif name in ("R", "U"):
                                    inc(dve.tensor_copy(buf[name][:, g], o4))
                                elif name == "S":
                                    dve.tensor_tensor(Stmp[:, g], o4, S[:, g], ALU.add).then_inc(s_sum, 1)
                                    dve.wait_ge(s_sum, 2 * n + g + 1)
                                    inc(dve.tensor_tensor(S[:, g], Stmp[:, g], pc[:, g, :, bass.ds(chunk(g, n), 1)]
                                                          .broadcast_to([P, 4, P]), ALU.mult))
                    pairs_loop(dve, lambda i: [step(i, slot) for slot in range(2)])

        with ExitStack() as inner:
            block = inner.enter_context(nc.Block())

            @block.sync
            def _(sp):
                sp.dma_start(ident[:], d["ident"]).then_inc(const_in, 16)
                sp.dma_start(masks[:], d["rw_masks"]).then_inc(const_in, 16)
                sp.dma_start(pc[:].rearrange("p r j c -> p (r j c)"), d["PC"]).then_inc(const_in, 16)
                sp.wait_ge(const_in, 48)

            @block.vector
            def _(dve):
                dve.memset(bdt[:], 0.0)
                dve.memset(S[:], 0.0)
                dve.memset(sio[:], 0.0).then_inc(zeroed, 1)
        run("rc", 0, TC // RC)

        with ExitStack() as inner:
            q = Scope(nc, inner, "sw")
            turn = q.ps("turn", [P, 2, 512])
            turned, copied, moved, fin_in = q.sem("turned"), q.sem("copied"), q.sem("moved"), q.sem("fin_in")
            block = inner.enter_context(nc.Block())
            ext = lambda ap, h: ap[:, h::2].rearrange("r j v k -> v (r j) k")

            @block.tensor
            def _(pe):
                for c in range(8):
                    last = pe.transpose(turn[:, c // 4, c % 4 * P:(c % 4 + 1) * P], S[:, c // 4, c % 4, :], ident[:])
                last.then_inc(turned, 1)
                pe.wait_ge(fin_in, 32)
                for c in range(8):
                    last = pe.transpose(turn[:, c // 4, c % 4 * P:(c % 4 + 1) * P], sio[:, c // 4, c % 4, :], ident[:])
                last.then_inc(turned, 1)

            @block.scalar
            def _(act):
                t4 = turn[:].rearrange("p g (c t) -> p g c t", c=4)
                act.wait_ge(turned, 1)
                act.activation(sio[:], t4, ACT.Copy).then_inc(copied, 1)
                act.wait_ge(copied, 1)
                for h in range(2):
                    hs = slice(64 * h, 64 * h + 64)
                    act.dma_start(ext(d["new_rwkv"], h), sio[hs, :, :, hs].rearrange("p g c t -> p (g c) t")).then_inc(moved, 16)
                act.wait_ge(moved, 32)
                for h in range(2):
                    hs = slice(64 * h, 64 * h + 64)
                    act.dma_start(sio[hs, :, :, hs].rearrange("p g c t -> p (g c) t"), ext(d["rw_s0"], h)).then_inc(fin_in, 16)
                act.wait_ge(turned, 2)
                act.activation(S[:], t4, ACT.Copy).then_inc(copied, 1)
        run("rs", TC // RC, TS // RC)


def rwkv_output(nc, d):
    NJ = NJ_A
    with ExitStack() as stack:
        s = Scope(nc, stack, "ro")
        par = s.sb("par", [P, 2, NJ])
        bdm = s.sb("bdm", [P, P])
        epsc = s.sb("epsc", [P, 1])
        y = s.sb("y", [P, 4, T])
        c = s.sb("c", [P, T])
        sq = s.sb("sq", [P, T])
        rs = s.sb("rs", [P, T])
        o = s.sb("o", [P, T])
        acc = [s.ps(f"acc{i}", [P, NSEG, 512]) for i in range(2)]
        par_in, eps_set, y_in, y_out = s.sem("par_in"), s.sem("eps_set"), s.sem("y_in"), s.sem("y_out")
        pe_s = Steps(s.sem("pe_s"), "mean var")
        act_s = Steps(s.sem("act_s"), "sq root")
        dve_s = Steps(s.sem("dve_s"), "sum cent inv norm aff bonus out")
        block = stack.enter_context(nc.Block())
        seg = lambda ap: ap.rearrange("p (q c) -> p q c", q=NSEG)

        @block.sync
        def _(sp):
            sp.dma_start(par[:], d["rw_gn"]).then_inc(par_in, 16)
            sp.dma_start(bdm[:], d["bd_mean"]).then_inc(par_in, 16)

            def load(j):
                rows = bass.ds(j * P, P)
                for n, src in enumerate((d["YD"][0], d["YD"][1], d["BONUS"], d["GATE"])):
                    sp.dma_start(y[:, n], src[rows, :]).then_inc(y_in, 16)

            def store(j):
                sp.wait_ge(dve_s.sem, dve_s.at("out", j))
                sp.dma_start(d["YT"][bass.ds(j * P, P), :], o[:]).then_inc(y_out, 16)
            sp.sem_inc(y_out, 16)
            load(0)
            with sp.Fori(1, NJ) as j:
                store(j - 1)
                load(j)
            store(NJ - 1)
            sp.wait_ge(y_out, 16 * (NJ + 1))

        @block.gpsimd
        def _(pool):
            pool.memset(epsc[:], GN_EPS).then_inc(eps_set, 1)

        @block.tensor
        def _(pe):
            pe.wait_ge(par_in, 32)
            with pe.Fori(0, NJ) as j:
                for n, (src, name) in enumerate(((y[:, 0], "mean"), (sq, "var"))):
                    if n:
                        pe.wait_ge(act_s.sem, act_s.at("sq", j))
                    else:
                        pe.wait_ge(dve_s.sem, dve_s.at("sum", j))
                    for q in range(NSEG):
                        last = pe.matmul(acc[n][:, q, 0:SEG], bdm[:], src[:, q * SEG:(q + 1) * SEG], start=True, stop=True)
                    pe_s.done(last, name)

        @block.scalar
        def _(act):
            act.wait_ge(eps_set, 1)
            with act.Fori(0, NJ) as j:
                act.wait_ge(dve_s.sem, dve_s.at("cent", j))
                act_s.done(act.activation(sq[:], c[:], ACT.Square), "sq")
                act.wait_ge(pe_s.sem, pe_s.at("var", j))
                act_s.done(act.activation(seg(rs[:]), acc[1][:, :, 0:SEG], ACT.Sqrt, bias=epsc[:, 0:1]), "root")

        @block.vector
        def _(dve):
            with dve.Fori(0, NJ) as j:
                at = lambda n: dve.wait_ge(dve_s.sem, dve_s.at(n, j))
                done = dve_s.done
                dve.wait_ge(y_in, 64 * (j + 1))
                done(dve.tensor_tensor(y[:, 0], y[:, 0], y[:, 1], ALU.add), "sum")
                dve.wait_ge(pe_s.sem, pe_s.at("mean", j))
                done(dve.tensor_tensor(seg(c[:]), seg(y[:, 0]), acc[0][:, :, 0:SEG], ALU.subtract), "cent")
                dve.wait_ge(act_s.sem, act_s.at("root", j))
                done(dve.reciprocal(rs[:], rs[:]), "inv")
                at("inv")
                done(dve.tensor_tensor(c[:], c[:], rs[:], ALU.mult), "norm")
                at("norm")
                done(dve.tensor_scalar(c[:], c[:], par[:, 0, bass.ds(j, 1)], par[:, 1, bass.ds(j, 1)], ALU.mult, ALU.add), "aff")
                at("aff")
                done(dve.tensor_tensor(c[:], c[:], y[:, 2], ALU.add), "bonus")
                at("bonus")
                dve.wait_ge(y_out, 16 * (j + 1))
                done(dve.tensor_tensor(o[:], c[:], y[:, 3], ALU.mult), "out")


def output_projection(nc, d):
    with ExitStack() as stack:
        s = Scope(nc, stack, "op")
        w = s.sb("w", [P, KT, D])
        gt, sc, sh, lg, lb = (s.sb(n, [P, D]) for n in ("gt", "sc", "sh", "lg", "lb"))
        yT = s.sb("yT", [P, 2, KT, P])
        x = s.sb("x", [P, D])
        a = s.sb("a", [P, D])
        stats = s.sb("stats", [P, 4, 6])
        mv = s.sb("mv", [P, 2])
        rstd = s.sb("rstd", [P, 1])
        epsc = s.sb("epsc", [P, 1])
        acc = [s.ps(f"acc{i}", [P, 4, 512]) for i in range(2)]
        w_in = [s.sem(f"w_in{k}") for k in range(4)]
        ln_in, row_in, x_in, eps_set = s.sem("ln_in"), s.sem("row_in"), s.sem("x_in"), s.sem("eps_set")
        y_in = [s.sem(f"y_in{i}") for i in range(2)]
        x1_out, h2_out = s.sem("x1_out"), s.sem("h2_out")
        product, root = s.sem("product"), s.sem("root")
        scale1, stats_in = s.sem("scale1"), s.sem("stats_in")
        dve_s = Steps(s.sem("dve_s"), "gate res st0 st1 st2 st3 aggr inv norm g x1 hs h2")
        block = stack.enter_context(nc.Block())
        slot_of = lambda t: t % 2

        @block.sync
        def _(sp):
            def load_y(t, slot):
                sp.dma_start(yT[:, slot], d["YT"].rearrange("(k p) t -> p k t", p=P)[:, :, bass.ds(t * P, P)]).then_inc(y_in[slot], 16)

            def load_rows(c):
                for dst, seg in ((gt, 2), (sc, 4), (sh, 3)):
                    sp.dma_start(dst[:], d["MOD"][c, seg * D:(seg + 1) * D].partition_broadcast(P)).then_inc(row_in, 16)

            def load_x(t):
                sp.dma_start(x[:], d["X0"][bass.ds(t * P, P), :]).then_inc(x_in, 16)
            load_y(0, 0)
            for q in range(4):
                sp.dma_start(w[:, :, q * 512:(q + 1) * 512], d["w_out"].rearrange("(k p) n -> p k n", p=P)[:, :, q * 512:(q + 1) * 512]
                             ).then_inc(w_in[q], 16)
            load_rows(0)
            load_x(0)
            for dst, name in ((lg, "ln1_g"), (lb, "ln1_b")):
                sp.dma_start(dst[:], d[name].partition_broadcast(P)).then_inc(ln_in, 16)
            load_y(1, 1)

            def tile(t, slot, more_y, rows):
                if more_y:
                    sp.wait_ge(product, t + 1)
                    load_y(t + 2, slot)
                sp.wait_ge(dve_s.sem, dve_s.at("x1", t))
                sp.dma_start(d["X1"][bass.ds(t * P, P), :], a[:]).then_inc(x1_out, 16)
                sp.wait_ge(dve_s.sem, dve_s.at("h2", t))
                sp.dma_start(d["H2"][bass.ds(t * P, P), :], x[:]).then_inc(h2_out, 16)
                if rows:
                    load_rows(1)
                sp.wait_ge(h2_out, 16 * (t + 1))
            tile(0, 0, True, True)
            load_x(1)
            with sp.Fori(0, (NT - 3) // 2) as i:
                for b in range(2):
                    t = 2 * i + 1 + b
                    tile(t, (1 + b) % 2, True, False)
                    load_x(t + 1)
            for t in range(NT - 2, NT):
                tile(t, t % 2, False, False)
                if t + 1 < NT:
                    load_x(t + 1)
            sp.wait_ge(x1_out, 16 * NT)

        @block.gpsimd
        def _(pool):
            pool.memset(epsc[:], LN_EPS).then_inc(eps_set, 1)

        @block.tensor
        def _(pe):
            def one(wait_y, slot, bank_free, first):
                wait_y()
                bank_free()
                for q in range(4):
                    if first:
                        pe.wait_ge(w_in[q], 16)
                    for k in range(KT):
                        last = pe.matmul(acc[slot][:, q, :], yT[:, slot, k, :], w[:, k, q * 512:(q + 1) * 512],
                                         start=k == 0, stop=k == KT - 1)
                last.then_inc(product, 1)
            one(lambda: pe.wait_ge(y_in[0], 16), 0, lambda: None, True)
            one(lambda: pe.wait_ge(y_in[1], 16), 1, lambda: None, False)
            with pe.Fori(0, (NT - 3) // 2) as i:
                for b in range(2):
                    t = 2 * i + 2 + b
                    one(lambda: pe.wait_ge(y_in[b], 16 * (i + 2)), b, lambda: pe.wait_ge(dve_s.sem, dve_s.at("gate", t - 2)), False)
            one(lambda: pe.wait_ge(y_in[0], 16 * ((NT + 1) // 2)), 0, lambda: pe.wait_ge(dve_s.sem, dve_s.at("gate", NT - 3)), False)

        @block.scalar
        def _(act):
            act.wait_ge(eps_set, 1)
            with act.Fori(0, NT) as t:
                act.wait_ge(dve_s.sem, dve_s.at("aggr", t))
                act.activation(rstd[:], mv[:, 1:2], ACT.Sqrt, bias=epsc[:, 0:1]).then_inc(root, 1)

        @block.vector
        def _(dve):
            def tile(t, slot, rows):
                at = lambda n: dve.wait_ge(dve_s.sem, dve_s.at(n, t))
                done = dve_s.done
                if rows is not None:
                    dve.wait_ge(row_in, 48 * (rows + 1))
                    dve.tensor_scalar(sc[:], sc[:], 1.0, None, ALU.add).then_inc(scale1, 1)
                    dve.wait_ge(scale1, rows + 1)
                dve.wait_ge(product, t + 1)
                if not isinstance(t, int) or t:
                    dve.wait_ge(x1_out, 16 * t)
                done(dve.tensor_tensor(a[:].rearrange("p (q c) -> p q c", q=4), acc[slot][:], gt[:].rearrange("p (q c) -> p q c", q=4),
                                       ALU.mult), "gate")
                at("gate")
                dve.wait_ge(x_in, 16 * (t + 1))
                done(dve.scalar_tensor_tensor(a[:], x[:], ALPHA, a[:], ALU.mult, ALU.add), "res")
                at("res")
                for q in range(4):
                    done(dve.bn_stats(stats[:, q, :], a[:, q * 512:(q + 1) * 512]), f"st{q}")
                at("st3")
                dve.sem_inc(stats_in, 1)
                done(dve.bn_aggr(mv[:], stats[:].rearrange("p q s -> p (q s)")), "aggr")
                dve.wait_ge(root, t + 1)
                done(dve.reciprocal(rstd[:], rstd[:]), "inv")
                at("inv")
                done(dve.tensor_scalar(a[:], a[:], mv[:, 0:1], rstd[:, 0:1], ALU.subtract, ALU.mult), "norm")
                at("norm")
                dve.wait_ge(ln_in, 32)
                done(dve.tensor_tensor(a[:], a[:], lg[:], ALU.mult), "g")
                at("g")
                done(dve.tensor_tensor(a[:], a[:], lb[:], ALU.add), "x1")
                at("x1")
                done(dve.tensor_tensor(x[:], a[:], sc[:], ALU.mult), "hs")
                at("hs")
                done(dve.tensor_tensor(x[:], x[:], sh[:], ALU.add), "h2")
                at("h2")
            tile(0, 0, 0)
            tile(1, 1, 1)
            with dve.Fori(0, (NT - 3) // 2) as i:
                for b in range(2):
                    tile(2 * i + 2 + b, b, None)
            tile(NT - 1, 0, None)


def routing(nc, d, keep):
    idx_s, idx_c, gate_s, gate_c = keep
    with ExitStack() as stack:
        s = Scope(nc, stack, "rt")
        ident = s.sb("ident", [P, P])
        rw = s.sb("rw", [P, KT, E])
        h = s.sb("h", [P, D])
        hT = s.sb("hT", [P, KT, P])
        lg = s.sb("lg", [P, E])
        nmax = s.sb("nmax", [P, 1])
        ssum = s.sb("ssum", [P, 1])
        aff = s.sb("aff", [P, E])
        affT = s.sb("affT", [E, T])
        vals = s.sb("vals", [E, P + E])
        idx = s.sb("idx", [E, P + E], U32)
        idxf = s.sb("idxf", [E, P + E])
        zero = s.sb("zero", [P, D])
        tb = [s.ps(f"tb{i}") for i in range(4)]
        lp, ap = s.ps("lp"), s.ps("ap")
        const_in, h_in, zeroed, cleared = s.sem("const_in"), s.sem("h_in"), s.sem("zeroed"), s.sem("cleared")
        pe_s = Steps(s.sem("pe_s"), "t0 t1 t2 t3 logit affT")
        act_s = Steps(s.sem("act_s"), "c0 c2 exp")
        dve_s = Steps(s.sem("dve_s"), "c1 c3 max rec aff affT")
        picked, chosen, turned = s.sem("picked"), s.sem("chosen"), s.sem("turned")
        block = stack.enter_context(nc.Block())

        @block.sync
        def _(sp):
            sp.dma_start(h[:], d["H2"][0:P, :]).then_inc(h_in, 16)
            sp.dma_start(ident[:], d["ident"]).then_inc(const_in, 16)
            sp.dma_start(rw[:], d["router_w"].rearrange("(k p) e -> p k e", p=P)).then_inc(const_in, 16)
            with sp.Fori(1, NT) as t:
                sp.wait_ge(pe_s.sem, pe_s.at("t3", t - 1))
                sp.dma_start(h[:], d["H2"][bass.ds(t * P, P), :]).then_inc(h_in, 16)
            sp.wait_ge(zeroed, 1)
            for t in range(NT):
                sp.dma_start(d["ACC"][t * P:(t + 1) * P, :], zero[:]).then_inc(cleared, 16)
            sp.wait_ge(cleared, 16 * NT)

        @block.gpsimd
        def _(pool):
            pool.memset(zero[:], 0.0).then_inc(zeroed, 1)

        @block.tensor
        def _(pe):
            pe.wait_ge(const_in, 32)
            with pe.Fori(0, NT) as t:
                pe.wait_ge(h_in, 16 * (t + 1))
                for q in range(4):
                    for b in range(4):
                        k = 4 * q + b
                        last = pe.transpose(tb[q][:, b * P:(b + 1) * P], h[:, k * P:(k + 1) * P], ident[:])
                    pe_s.done(last, f"t{q}")
                pe.wait_ge(act_s.sem, act_s.at("c2", t))
                pe.wait_ge(dve_s.sem, dve_s.at("c3", t))
                for k in range(KT):
                    last = pe.matmul(lp[:, 0:E], hT[:, k, :], rw[:, k, :], start=k == 0, stop=k == KT - 1)
                pe_s.done(last, "logit")
                pe.wait_ge(dve_s.sem, dve_s.at("aff", t))
                pe_s.done(pe.transpose(ap[0:E, 0:P], aff[:], ident[:]), "affT")
            pe.wait_ge(chosen, 1)
            pe.transpose(tb[0][:, 0:E], idxf[:, 0:P], ident[0:E, 0:E])
            pe.transpose(tb[0][:, E:2 * E], vals[:, 0:P], ident[0:E, 0:E])
            pe.transpose(tb[0][0:E, 2 * E:3 * E], idxf[:, P:P + E], ident[0:E, 0:E])
            pe.transpose(tb[0][0:E, 3 * E:4 * E], vals[:, P:P + E], ident[0:E, 0:E]).then_inc(turned, 1)

        @block.scalar
        def _(act):
            with act.Fori(0, NT) as t:
                for q in (0, 2):
                    act.wait_ge(pe_s.sem, pe_s.at(f"t{q}", t))
                    act_s.done(act.activation(hT[:, 4 * q:4 * q + 4, :].rearrange("p k t -> p (k t)"), tb[q][:], ACT.Copy), f"c{q}")
                act.wait_ge(dve_s.sem, dve_s.at("max", t))
                act_s.done(act.activation(lg[:], lp[:, 0:E], ACT.Exp, bias=nmax[:, 0:1], accum_out=ssum[:, 0:1]), "exp")

        @block.vector
        def _(dve):
            with dve.Fori(0, NT) as t:
                at = lambda n: dve.wait_ge(dve_s.sem, dve_s.at(n, t))
                for q in (1, 3):
                    dve.wait_ge(pe_s.sem, pe_s.at(f"t{q}", t))
                    dve_s.done(dve.tensor_copy(hT[:, 4 * q:4 * q + 4, :].rearrange("p k t -> p (k t)"), tb[q][:]), f"c{q}")
                dve.wait_ge(pe_s.sem, pe_s.at("logit", t))
                dve_s.done(dve.tensor_reduce(nmax[:], lp[:, 0:E], AX.X, ALU.max, negate=True), "max")
                dve.wait_ge(act_s.sem, act_s.at("exp", t))
                dve_s.done(dve.reciprocal(ssum[:], ssum[:]), "rec")
                at("rec")
                dve_s.done(dve.tensor_scalar(aff[:], lg[:], ssum[:, 0:1], None, ALU.mult), "aff")
                dve.wait_ge(pe_s.sem, pe_s.at("affT", t))
                dve_s.done(dve.tensor_copy(affT[:, bass.ds(t * P, P)], ap[0:E, 0:P]), "affT")
            link = Chain(dve, picked)
            dve.wait_ge(dve_s.sem, dve_s.at("affT", NT - 1))
            for rounds, lo, n, at_col in ((CAP_S // 8, TC, TS, 0), (CAP_C // 8, 0, TC, P)):
                cur = affT[:, lo:lo + n]
                for r in range(rounds):
                    c8 = slice(at_col + 8 * r, at_col + 8 * r + 8)
                    link(dve.max(vals[:, c8], cur))
                    link(dve.max_index(idx[:, c8], vals[:, c8], cur))
                    link(dve.match_replace(cur, vals[:, c8], cur, -1.0))
            link(dve.tensor_copy(idxf[:], idx[:]))
            dve.tensor_scalar(idxf[:, 0:P], idxf[:, 0:P], float(TC), None, ALU.add).then_inc(chosen, 1)
            dve.wait_ge(turned, 1)
            dve.tensor_copy(idx_s[:, 0:E], tb[0][:, 0:E])
            dve.tensor_copy(gate_s[:, 0:E], tb[0][:, E:2 * E])
            dve.tensor_copy(idx_c[:, 0:E], tb[0][0:E, 2 * E:3 * E])
            dve.tensor_copy(gate_c[:, 0:E], tb[0][0:E, 3 * E:4 * E])
            dve.tensor_copy(idx_s[:, E:E + 1], tb[0][:, 0:1])
            dve.tensor_copy(idx_c[:, E:E + 1], tb[0][0:E, 2 * E:2 * E + 1]).then_inc(chosen, 1)


def experts(nc, d, keep):
    idx_s, idx_c, gate_s, gate_c = keep
    RING, NF = 12, FE // P
    GU, SLABS = KT, KT + NF
    ROUNDS = SLABS // RING
    C = CAP
    TPB = 3
    with ExitStack() as stack:
        s = Scope(nc, stack, "ex")
        ident = s.sb("ident", [P, P])
        ring = s.sb("ring", [P, RING, D])
        xs, xc = s.sb("xs", [P, D]), s.sb("xc", [E, D])
        xT = s.sb("xT", [P, KT, C])
        sg = s.sb("sg", [P, NF, C])
        at_ = s.sb("act", [P, NF, C])
        yT = s.sb("yT", [P, KT, C])
        ys, yc = s.sb("ys", [P, D]), s.sb("yc", [E, D])
        gi_s, gi_c = s.sb("gi_s", [P, 1], I32), s.sb("gi_c", [E, 1], I32)
        si_s, si_c = s.sb("si_s", [P, 1], I32), s.sb("si_c", [E, 1], I32)
        gt_s, gt_c = s.sb("gt_s", [P, 1]), s.sb("gt_c", [E, 1])
        bank = [s.ps(f"bank{i}") for i in range(8)]
        tb = bank[6:8]
        ident_in = s.sem("ident_in")
        slab_in = [s.sem(f"slab_in{i}") for i in range(RING)]
        slab_used = s.sem("slab_used")
        gathered, scattered, x_turned, y_turned = s.sem("gathered"), s.sem("scattered"), s.sem("x_turned"), s.sem("y_turned")
        gu_done, down_done = s.sem("gu_done"), s.sem("down_done")
        x_act, x_dve = s.sem("x_act"), s.sem("x_dve")
        silu, acted = s.sem("silu"), s.sem("acted")
        yT_act, yT_dve = s.sem("yT_act"), s.sem("yT_dve")
        y_act, y_dve = s.sem("y_act"), s.sem("y_dve")
        gidx, sidx, drained, begun = (s.sem(n) for n in ("gidx", "sidx", "drained", "begun"))
        block = stack.enter_context(nc.Block())
        XG = -(-KT // TPB)
        YG = 8
        tiles = lambda b, n: range(TPB * b, min(TPB * b + TPB, n))

        @block.sync
        def _(sp):
            sp.dma_start(ident[:], d["ident"]).then_inc(ident_in, 16)

            def load(e, k):
                slot = k % RING
                if k < GU:
                    for n, name in enumerate(("w_gate", "w_up")):
                        sp.dma_start(ring[:, slot, n * FE:(n + 1) * FE], d[name][bass.ds(e * D + k * P, P), :]).then_inc(slab_in[slot], 16)
                else:
                    for n in range(2):
                        sp.dma_start(ring[:, slot, n * FE:(n + 1) * FE],
                                     d["w_down"][bass.ds(e * FE + (k - GU) * P, P), n * FE:(n + 1) * FE]).then_inc(slab_in[slot], 16)
            for k in range(RING):
                load(0, k)

            def refill(e, k):
                if k == GU - 1:
                    sp.wait_ge(gu_done, e * 6 + 6)
                elif k == SLABS - 1:
                    sp.wait_ge(down_done, e * 6 + 6)
                else:
                    sp.wait_ge(slab_used, e * (SLABS - 2) + k - (k >= GU) + 1)
                if k + RING < SLABS:
                    load(e, k + RING)
                else:
                    load(e + 1, k + RING - SLABS)
            with sp.Fori(0, E - 1) as e:
                for k in range(SLABS):
                    refill(e, k)
            for k in range(SLABS - RING):
                refill(E - 1, k)

        @block.gpsimd
        def _(pool):
            def gather(e):
                pool.wait_ge(gidx, e + 1)
                pool.sem_inc(begun, 1)
                for dst, src in ((xs, gi_s), (xc, gi_c)):
                    pool.indirect_dma_start(out=dst[:], out_offset=None, in_=d["H2"],
                                            in_offset=bass.IndirectOffsetOnAxis(ap=src[:, 0:1], axis=0)).then_inc(gathered, 16)
            pool.sem_inc(drained, 1)
            gather(0)
            with pool.Fori(0, E) as e:
                gather(e + 1)
                pool.wait_ge(sidx, e + 1)
                pool.wait_ge(y_act, (e + 1) * YG // 2)
                pool.wait_ge(y_dve, (e + 1) * YG // 2)
                pool.sem_inc(begun, 1)
                for src, ix in ((ys, si_s), (yc, si_c)):
                    pool.indirect_dma_start(out=d["ACC"], out_offset=bass.IndirectOffsetOnAxis(ap=ix[:, 0:1], axis=0),
                                            in_=src[:], in_offset=None, compute_op=ALU.add).then_inc(scattered, 16)
                pool.wait_ge(scattered, 32 * (e + 1))
                pool.sem_inc(drained, 1)

        @block.tensor
        def _(pe):
            pe.wait_ge(ident_in, 16)

            def turn_x(e):
                pe.wait_ge(gathered, 32 * (e + 1))
                for i in range(XG):
                    if i >= 2:
                        pe.wait_ge(x_act if i % 2 == 0 else x_dve, e * XG // 2 + i // 2)
                    for n, k in enumerate(tiles(i, KT)):
                        pe.transpose(tb[i % 2][:, n * C:n * C + P], xs[:, k * P:(k + 1) * P], ident[:])
                        last = pe.transpose(tb[i % 2][:, n * C + P:(n + 1) * C], xc[:, k * P:(k + 1) * P], ident[0:E, 0:E])
                    last.then_inc(x_turned, 1)

            def slab(e, k):
                pe.wait_ge(slab_in[k % RING], (e * ROUNDS + k // RING + 1) * 32)
            turn_x(0)
            with pe.Fori(0, E) as e:
                pe.wait_ge(x_act, (e + 1) * XG // 2)
                pe.wait_ge(x_dve, (e + 1) * XG // 2)
                pe.wait_ge(yT_act, e * 3 + 3)
                pe.wait_ge(yT_dve, e * 3 + 3)
                for k in range(GU):
                    slab(e, k)
                    for h in range(2):
                        for f in range(NF):
                            b, n = 3 * h + f // TPB, f % TPB
                            last = pe.matmul(bank[b][:, n * C:(n + 1) * C], ring[:, k % RING, h * FE + f * P:h * FE + (f + 1) * P],
                                             xT[:, k, :], start=k == 0 and n == 0, stop=k == GU - 1, skip_group_check=True)
                            if k == GU - 1 and (n == TPB - 1 or f == NF - 1):
                                last.then_inc(gu_done, 1)
                    if k < GU - 1:
                        last.then_inc(slab_used, 1)
                turn_x(e + 1)
                pe.wait_ge(acted, (e + 1) * 3)
                for f in range(NF):
                    slab(e, GU + f)
                    for t in range(KT):
                        b, n = t // TPB, t % TPB
                        last = pe.matmul(bank[b][:, n * C:(n + 1) * C], ring[:, (GU + f) % RING, t * P:(t + 1) * P],
                                         at_[:, f, :], start=f == 0 and n == 0, stop=f == NF - 1, skip_group_check=True)
                        if f == NF - 1 and (n == TPB - 1 or t == KT - 1):
                            last.then_inc(down_done, 1)
                    if f < NF - 1:
                        last.then_inc(slab_used, 1)
                for i in range(YG):
                    if i < 2:
                        pe.wait_ge(x_act if i == 0 else x_dve, (e + 2) * XG // 2)
                    else:
                        pe.wait_ge(y_act if i % 2 == 0 else y_dve, e * YG // 2 + i // 2)
                    pe.wait_ge(yT_act, e * 3 + 6)
                    pe.wait_ge(yT_dve, e * 3 + 6)
                    g = i // 2
                    for n in range(4):
                        k = 4 * g + n
                        if i % 2 == 0:
                            last = pe.transpose(tb[0][:, n * P:(n + 1) * P], yT[:, k, 0:P], ident[:])
                        else:
                            last = pe.transpose(tb[1][0:E, n * P:(n + 1) * P], yT[:, k, P:C], ident[:])
                    last.then_inc(y_turned, 1)

        @block.scalar
        def _(act):
            act.sem_inc(yT_act, 3)

            def copy_x(e):
                for i in range(0, XG, 2):
                    act.wait_ge(x_turned, e * XG + i + 1)
                    k = tiles(i, KT)
                    act.activation(xT[:, k[0]:k[-1] + 1, :].rearrange("p k c -> p (k c)"), tb[0][:, 0:len(k) * C], ACT.Copy).then_inc(x_act, 1)
            copy_x(0)
            with act.Fori(0, E) as e:
                for b in range(3):
                    act.wait_ge(gu_done, e * 6 + b + 1)
                    f = tiles(b, NF)
                    act.activation(sg[:, f[0]:f[-1] + 1, :].rearrange("p f c -> p (f c)"), bank[b][:, 0:len(f) * C], ACT.Silu).then_inc(silu, 1)
                copy_x(e + 1)
                for b in range(0, 6, 2):
                    act.wait_ge(down_done, e * 6 + b + 1)
                    k = tiles(b, KT)
                    act.activation(yT[:, k[0]:k[-1] + 1, :].rearrange("p k c -> p (k c)"), bank[b][:, 0:len(k) * C], ACT.Copy).then_inc(yT_act, 1)
                act.wait_ge(sidx, e + 1)
                for g in range(YG // 2):
                    act.wait_ge(y_turned, e * YG + 2 * g + 1)
                    act.activation(ys[:, g * 512:(g + 1) * 512], tb[0][:], ACT.Copy, scale=gt_s[:, 0:1]).then_inc(y_act, 1)

        @block.vector
        def _(dve):
            dve.sem_inc(yT_dve, 3)

            def rows(dst, src, e, n=None):
                return dve.tensor_copy(dst[:], src[:, bass.ds(e, 1)])

            def copy_x(e):
                for i in range(1, XG, 2):
                    dve.wait_ge(x_turned, e * XG + i + 1)
                    k = tiles(i, KT)
                    dve.tensor_copy(xT[:, k[0]:k[-1] + 1, :].rearrange("p k c -> p (k c)"), tb[1][:, 0:len(k) * C]).then_inc(x_dve, 1)
            rows(gi_s, idx_s, 0)
            rows(gi_c, idx_c, 0).then_inc(gidx, 1)
            copy_x(0)
            with dve.Fori(0, E) as e:
                dve.wait_ge(gathered, 32 * (e + 1))
                dve.wait_ge(x_turned, (e + 1) * XG)
                rows(gi_s, idx_s, e + 1)
                rows(gi_c, idx_c, e + 1).then_inc(gidx, 1)
                for b in range(3):
                    dve.wait_ge(silu, e * 3 + b + 1)
                    dve.wait_ge(gu_done, e * 6 + 3 + b + 1)
                    f = tiles(b, NF)
                    flat = lambda x: x[:, f[0]:f[-1] + 1, :].rearrange("p f c -> p (f c)")
                    dve.tensor_tensor(flat(at_), bank[3 + b][:, 0:len(f) * C], flat(sg), ALU.mult).then_inc(acted, 1)
                copy_x(e + 1)
                for b in range(1, 6, 2):
                    dve.wait_ge(down_done, e * 6 + b + 1)
                    k = tiles(b, KT)
                    dve.tensor_copy(yT[:, k[0]:k[-1] + 1, :].rearrange("p k c -> p (k c)"), bank[b][:, 0:len(k) * C]).then_inc(yT_dve, 1)
                dve.wait_ge(drained, e + 1)
                rows(si_s, idx_s, e)
                rows(si_c, idx_c, e)
                rows(gt_s, gate_s, e)
                rows(gt_c, gate_c, e).then_inc(sidx, 1)
                dve.wait_ge(sidx, e + 1)
                for g in range(YG // 2):
                    dve.wait_ge(y_turned, e * YG + 2 * g + 2)
                    dve.tensor_scalar(yc[:, g * 512:(g + 1) * 512], tb[1][0:E, :], gt_c[:, 0:1], None, ALU.mult).then_inc(y_dve, 1)


def final_norm(nc, d):
    with ExitStack() as stack:
        s = Scope(nc, stack, "fn")
        gt, lg, lb = s.sb("gt", [P, 2, D]), s.sb("lg", [P, D]), s.sb("lb", [P, D])
        x, m = s.sb("x", [P, 3, D]), s.sb("m", [P, 3, D])
        stats, mv, rstd, epsc = s.sb("stats", [P, 4, 6]), s.sb("mv", [P, 2, 2]), s.sb("rstd", [P, 2]), s.sb("epsc", [P, 1])
        ln_in, eps_set = s.sem("ln_in"), s.sem("eps_set")
        x_in = [s.sem(f"x_in{i}") for i in range(3)]
        out = [s.sem(f"out{i}") for i in range(3)]
        root = s.sem("root")
        dve_s = Steps(s.sem("dve_s"), "res st0 st1 st2 st3 aggr inv norm b")
        pool_s = Steps(s.sem("pool_s"), "gate")
        block = stack.enter_context(nc.Block())

        @block.sync
        def _(sp):
            for t in range(NT):
                if t == 1:
                    for c in range(2):
                        sp.dma_start(gt[:, c], d["MOD"][c, 5 * D:6 * D].partition_broadcast(P)).then_inc(ln_in, 16)
                    for dst, name in ((lg, "ln2_g"), (lb, "ln2_b")):
                        sp.dma_start(dst[:], d[name].partition_broadcast(P)).then_inc(ln_in, 16)
                if t >= 3:
                    sp.wait_ge(out[t % 3], 16 * (t // 3))
                for dst, src in ((x, "X1"), (m, "ACC")):
                    sp.dma_start(dst[:, t % 3], d[src][t * P:(t + 1) * P, :]).then_inc(x_in[t % 3], 16)

        @block.gpsimd
        def _(pool):
            pool.memset(epsc[:], LN_EPS).then_inc(eps_set, 1)
            pool.wait_ge(ln_in, 64)
            for t in range(NT):
                pool.wait_ge(x_in[t % 3], 32 * (t // 3 + 1))
                pool_s.done(pool.tensor_tensor(m[:, t % 3], m[:, t % 3], gt[:, min(t, 1)], ALU.mult), "gate")

        @block.scalar
        def _(act):
            act.wait_ge(eps_set, 1)
            for t in range(NT):
                act.wait_ge(dve_s.sem, dve_s.at("aggr", t))
                act.activation(rstd[:, t % 2:t % 2 + 1], mv[:, t % 2, 1:2], ACT.Sqrt, bias=epsc[:, 0:1]).then_inc(root, 1)
                act.wait_ge(dve_s.sem, dve_s.at("b", t))
                dst = d["y_prompt"] if t == 0 else d["y_sample"][(t - 1) * P:t * P, :]
                act.dma_start(dst, x[:, t % 3]).then_inc(out[t % 3], 16)
            for i in range(3):
                act.wait_ge(out[i], 16 * (NT // 3))

        @block.vector
        def _(dve):
            for t in range(NT):
                at = lambda n: dve.wait_ge(dve_s.sem, dve_s.at(n, t))
                done = dve_s.done
                a = x[:, t % 3]
                dve.wait_ge(pool_s.sem, pool_s.at("gate", t))
                done(dve.scalar_tensor_tensor(a, a, ALPHA, m[:, t % 3], ALU.mult, ALU.add), "res")
                at("res")
                for q in range(4):
                    done(dve.bn_stats(stats[:, q, :], a[:, q * 512:(q + 1) * 512]), f"st{q}")
                at("st3")
                done(dve.bn_aggr(mv[:, t % 2], stats[:].rearrange("p q s -> p (q s)")), "aggr")
                dve.wait_ge(root, t + 1)
                r = rstd[:, t % 2:t % 2 + 1]
                done(dve.reciprocal(r, r), "inv")
                at("inv")
                done(dve.scalar_tensor_tensor(a, a, mv[:, t % 2, 0:1], lg[:], ALU.subtract, ALU.mult), "norm")
                at("norm")
                done(dve.scalar_tensor_tensor(a, a, r, lb[:], ALU.mult, ALU.add), "b")


def moe(nc, d):
    with ExitStack() as stack:
        s = Scope(nc, stack, "moe")
        keep = (s.sb("idx_s", [P, E + 1], I32), s.sb("idx_c", [E, E + 1], I32), s.sb("gate_s", [P, E]), s.sb("gate_c", [E, E]))
        routing(nc, d, keep)
        experts(nc, d, keep)


def rwkv_masks():
    t, u = np.arange(64)[:, None], np.arange(64)[None, :]
    level = lambda m: (t // (2 * m) == u // (2 * m)) & (t % (2 * m) >= m) & (u % (2 * m) < m)
    forward = [level(m) | (t == u) for m in (2, 4, 8, 16, 32)] + [t < u, t <= u, level(1), level(1).T]
    both = [forward, [m.T for m in forward]]
    out = np.stack([np.stack([np.kron(np.eye(2), m) for m in ms]) for ms in both]).astype(np.float32)
    for r, ms in enumerate(both):
        out[r, 6, :, 0:64] = np.concatenate([ms[6], ms[6]], 0)
    return out.transpose(2, 0, 1, 3)


def layout(**a):
    col = lambda v: np.ascontiguousarray(v.reshape(-1, P).T)
    quarter = D // 4
    omega = 1.0 / (10000.0 ** (np.arange(quarter, dtype=np.float32) / quarter)).astype(np.float32)
    ids = np.arange(TS)
    ang = [(ids // 64).astype(np.float32)[:, None] * omega[None], (ids % 64).astype(np.float32)[:, None] * omega[None]]
    out = {
        "x": np.concatenate([a["x_prompt"][0], a["x_sample"][0]], 0),
        "pos": np.concatenate([f(v) for v in ang for f in (np.sin, np.cos)], -1).astype(np.float32),
        "cond": np.stack([col(a["c_ctx"]), col(a["c"][0])], -1),
        "b_mod": np.stack([a["b_mod"][0]] * 2),
        "w_mod": a["w_mod"][0],
        "w_in": a["w_in"][0],
        "lru_par": np.stack([col(v) for v in [*a["lru_conv_w"][0], a["lru_conv_b"][0], *a["lru_lambda"][0]]], 1),
        "lru_bias": np.stack([col(v) for v in [*a["lru_b_a"][0], *a["lru_b_x"][0]]], 1),
        "lru_h0": np.stack([col(v) for v in a["state_rglru"][0, 0]], 1),
        "lru_gates": np.concatenate([a["lru_w_a"][0], a["lru_w_x"][0]], 0),
        "ssd_par": np.stack([col(v) for v in [*a["ssd_conv_w"][0], a["ssd_conv_b"][0]]], 1),
        "ssd_dt": np.stack([a["ssd_dt_bias"][0].reshape(-1), a["ssd_a_log"][0].reshape(-1)], 1),
        "ssd_d": np.broadcast_to(a["ssd_d"][0], (P, 12)),
        "ssd_norm_g": col(a["ssd_norm_g"][0]),
        "ssd_s0": a["state_ssd"][0, 0].reshape(-1, P),
        "ones": np.ones((P, P), np.float32),
        "upper": np.triu(np.ones((P, P), np.float32)),
        "lower": np.tril(np.ones((P, P), np.float32)),
        "rw_mu": col(a["rwkv_mu"][0]),
        "rw_par": np.stack([col(v) for v in [*a["rwkv_w0"][0], *a["rwkv_a0"][0], a["rwkv_k_k"][0], a["rwkv_k_a"][0],
                                             a["rwkv_r_k"][0]]], 1),
        "rw_up": np.stack([a["rwkv_w_up"][0].reshape(P, -1), a["rwkv_a_up"][0].reshape(P, -1), a["rwkv_g_up"][0]], 1),
        "rw_gn": np.stack([col(a["rwkv_gn_g"][0]), col(a["rwkv_gn_b"][0])], 1),
        "rw_s0": a["state_rwkv"][0, 0],
        "rw_masks": rwkv_masks(),
        "bd_ones": np.kron(np.eye(2, dtype=np.float32), np.ones((64, 64), np.float32)),
        "bd_mean": np.kron(np.eye(2, dtype=np.float32), np.full((64, 64), 1 / 64, np.float32)),
        "w_out": a["w_out"][0],
        "ln1_g": a["ln1_g"][0], "ln1_b": a["ln1_b"][0], "ln2_g": a["ln2_g"][0], "ln2_b": a["ln2_b"][0],
        "router_w": a["router_w"][0],
        "w_gate": a["exp_w_gate"].reshape(E * D, FE),
        "w_up": a["exp_w_up"].reshape(E * D, FE),
        "w_down": a["exp_w_down"].reshape(E * FE, D),
        "ident": np.eye(P, dtype=np.float32),
    }
    return {n: np.ascontiguousarray(v) for n, v in out.items()}


SCRATCH = {
    "MOD": [2, 6 * D],
    "X0": [T, D],
    "FEAT": [FT * P, T],
    "YT": [D, T],
    "RW": [4, 2, 512, T],
    "RT": [2, 512, T],
    "PC": [P, 2 * 4 * (T // 64)],
    "GATE": [512, T],
    "BONUS": [512, T],
    "YD": [2, 512, T],
    "X1": [T, D],
    "H2": [T, D],
    "ACC": [T, D],
    "XBC": [SSD_CH, T],
    "ROWS": [48, T],
}
OUTS = {"y_prompt": [TC, D], "y_sample": [TS, D], "new_rwkv": [2, 8, 64, 64], "new_ssd": [2 * 12 * 64, 128], "new_rglru": [2 * (D_B // P), P]}


STAGES = (modulation, projection, rwkv_features, rwkv_recurrence, rwkv_output, rglru, ssd, output_projection, moe, final_norm)


def program(nc, d):
    for stage in STAGES:
        stage(nc, d)


def kernel(**inputs):
    import concourse.bacc as bacc
    from concourse.bass_utils import run_bass_kernel_spmd

    nc = bacc.Bacc("TRN2", target_bir_lowering=False, num_devices=1)
    arrays, d = {}, {}
    for name, a in layout(**{n: np.asarray(v) for n, v in inputs.items()}).items():
        arrays[f"in_{name}"] = a
        d[name] = nc.dram_tensor(f"in_{name}", a.shape, mybir.dt.from_np(a.dtype), kind="ExternalInput").ap()
    for name, shape in SCRATCH.items():
        d[name] = nc.dram_tensor(f"scratch_{name}", shape, F32, kind="Internal").ap()
    for name, shape in OUTS.items():
        d[name] = nc.dram_tensor(f"out_{name}", shape, F32, kind="ExternalOutput").ap()
    program(nc, d)
    got = run_bass_kernel_spmd(nc, [arrays], core_ids=[0]).results[0]
    out = lambda name, shape: got[f"out_{name}"].reshape(shape)
    return (out("y_prompt", (1, TC, D)), out("y_sample", (1, TS, D)), out("new_rwkv", (1, 1, 2, 8, 64, 64)),
            out("new_rglru", (1, 1, 2, D_B)), out("new_ssd", (1, 1, 2, 12, 64, 128)))
```
